# Optimizing a Trainium2 kernel written in Bass

```python
import math
import jax
import jax.numpy as jnp
from jax import lax
import numpy as np
import jax, jax.numpy as jnp

D_MODEL = 1024
BATCH = 1
SEQ = 512
DEPTH = 1

GRID_W = 64
CTX_LEN = 256
N_MIX_GROUPS = 4
D_GROUP = D_MODEL // N_MIX_GROUPS
D_MIX = N_MIX_GROUPS * D_GROUP
A_HEADS = 4
A_QK = 32
A_V = D_GROUP // A_HEADS
Q_BLOCK = 128
ROPE_BASE = 10000.0
B_HEADS = 4
B_DIM = D_GROUP // B_HEADS
WIN_R = 8
WIN_C = 16
POOL_SIZES = (2, 4, 8, 16)
POOL_CH = D_GROUP // len(POOL_SIZES)
HY_CH = D_GROUP
HY_ORDER = 2
HY_SHORT = 3
HY_BANDS = 16
HY_EMB = 1 + 2 * HY_BANDS
HY_HIDDEN = 64
HY_SIN_FREQ = 1.0
HY_MIN_DECAY = math.log(1e-2) / 1.5
HY_MAX_DECAY = math.log(1e-2) / 0.3
D_IN = 2 * A_HEADS * 2 * A_QK + A_HEADS * A_V + 3 * B_HEADS * B_DIM + D_GROUP + (HY_ORDER + 1) * HY_CH
N_EXPERTS = 16
N_EXPERT_GROUPS = 4
TOPK_GROUPS = 1
TOP_K = 2
D_EXPERT = 512
EPS = 1e-6


F32 = jnp.float32

def rmsnorm(x, g):
    xf = x.astype(F32)
    return (xf * lax.rsqrt(jnp.mean(xf * xf, axis=-1, keepdims=True) + EPS)).astype(x.dtype) * g

def split_cols(u):
    sizes = (A_HEADS * 2 * A_QK, A_HEADS * 2 * A_QK, A_HEADS * A_V,
             B_HEADS * B_DIM, B_HEADS * B_DIM, B_HEADS * B_DIM,
             D_GROUP, (HY_ORDER + 1) * HY_CH)
    offs, acc = [], 0
    for s in sizes[:-1]:
        acc += s
        offs.append(acc)
    return jnp.split(u, offs, axis=-1)

def axial_rope(x):
    L, dim = x.shape[1], x.shape[-1]
    n_freq = dim // 4
    inv = ROPE_BASE ** (-jnp.arange(n_freq, dtype=F32) / n_freq)
    t = jnp.arange(L)
    row = (t // GRID_W).astype(F32)
    col = (t % GRID_W).astype(F32)
    ang = jnp.concatenate([row[:, None] * inv, col[:, None] * inv], axis=-1)
    shape = (1, L) + (1,) * (x.ndim - 3) + (dim // 2,)
    cos, sin = jnp.cos(ang).reshape(shape), jnp.sin(ang).reshape(shape)
    x1, x2 = x[..., : dim // 2].astype(F32), x[..., dim // 2:].astype(F32)
    return jnp.concatenate([x1 * cos - x2 * sin, x2 * cos + x1 * sin], axis=-1).astype(x.dtype)

def diff_attention(uq_c, uk_c, uv_c, uq_l, uk_l, uv_l, lam_vecs, subln_g, li, need_ctx):
    B, S = uq_l.shape[:2]
    C = uq_c.shape[1]
    lam_init = 0.8 - 0.6 * math.exp(-0.3 * li)
    lv = lam_vecs.astype(F32)
    lam = jnp.exp(jnp.sum(lv[0] * lv[1])) - jnp.exp(jnp.sum(lv[2] * lv[3])) + lam_init
    qc = uq_c.reshape(B, C, A_HEADS, 2, A_QK)
    kc = uk_c.reshape(B, C, A_HEADS, 2, A_QK)
    vc = uv_c.reshape(B, C, A_HEADS, A_V)
    ql = axial_rope(uq_l.reshape(B, S, A_HEADS, 2, A_QK))
    kl = axial_rope(uk_l.reshape(B, S, A_HEADS, 2, A_QK))
    vl = uv_l.reshape(B, S, A_HEADS, A_V)
    k_all = jnp.concatenate([kc, kl], axis=1)
    v_all = jnp.concatenate([vc, vl], axis=1)

    def attend(q, k, v):
        s = jnp.einsum('bqhcd,bkhcd->bhcqk', q, k, preferred_element_type=F32) * (A_QK ** -0.5)
        p = jax.nn.softmax(s, axis=-1)
        a = p[:, :, 0] - lam * p[:, :, 1]
        return jnp.einsum('bhqk,bkhd->bqhd', a.astype(v.dtype), v)

    def post(o):
        o = rmsnorm(o, subln_g) * (1.0 - lam_init)
        return o.reshape(o.shape[0], o.shape[1], A_HEADS * A_V)

    nb = S // Q_BLOCK
    qb = jnp.moveaxis(ql.reshape(B, nb, Q_BLOCK, A_HEADS, 2, A_QK), 1, 0)
    ol = lax.map(lambda qblk: attend(qblk, k_all, v_all), qb)
    ol = jnp.moveaxis(ol, 0, 1).reshape(B, S, A_HEADS, A_V)
    out_c = post(attend(qc, kc, vc)) if need_ctx else None
    return out_c, post(ol)

def neighbourhood_attention(uq_c, uk_c, uv_c, uq_l, uk_l, uv_l, rpb, need_ctx):
    B, S = uq_l.shape[:2]
    C = uq_c.shape[1]
    R = S // GRID_W
    wr = min(WIN_R, R)
    scale = B_DIM ** -0.5
    qc = uq_c.reshape(B, C, B_HEADS, B_DIM)
    kc = uk_c.reshape(B, C, B_HEADS, B_DIM)
    vc = uv_c.reshape(B, C, B_HEADS, B_DIM)
    qg = uq_l.reshape(B, R, GRID_W, B_HEADS, B_DIM)
    kg = uk_l.reshape(B, R, GRID_W, B_HEADS, B_DIM)
    vg = uv_l.reshape(B, R, GRID_W, B_HEADS, B_DIM)
    rows = jnp.arange(R)
    r0 = jnp.clip(rows - wr // 2, 0, R - wr)
    row_idx = r0[:, None] + jnp.arange(wr)[None, :]
    k_rows = kg[:, row_idx]
    v_rows = vg[:, row_idx]
    cols = jnp.arange(GRID_W)
    c0 = jnp.clip(cols - WIN_C // 2, 0, GRID_W - WIN_C)
    in_win = (cols[None, :] >= c0[:, None]) & (cols[None, :] < c0[:, None] + WIN_C)
    dr = row_idx - rows[:, None]
    dc = jnp.clip(cols[None, :] - cols[:, None], -(WIN_C - 1), WIN_C - 1)
    bias = rpb.astype(F32)[:, dr[:, None, :, None] + (WIN_R - 1), dc[None, :, None, :] + (WIN_C - 1)]
    bias = jnp.where(in_win[:, None, :], bias, -jnp.inf)
    bias = jnp.transpose(bias, (1, 0, 2, 3, 4))[None]
    s_win = jnp.einsum('brqhd,brikhd->brhqik', qg, k_rows, preferred_element_type=F32) * scale + bias
    s_win = s_win.reshape(B, R, B_HEADS, GRID_W, wr * GRID_W)
    s_ctx = jnp.einsum('brqhd,bkhd->brhqk', qg, kc, preferred_element_type=F32) * scale
    p = jax.nn.softmax(jnp.concatenate([s_win, s_ctx], axis=-1), axis=-1)
    p_win = p[..., : wr * GRID_W].reshape(B, R, B_HEADS, GRID_W, wr, GRID_W).astype(vg.dtype)
    p_ctx = p[..., wr * GRID_W:].astype(vg.dtype)
    ol = jnp.einsum('brhqik,brikhd->brqhd', p_win, v_rows) + jnp.einsum('brhqk,bkhd->brqhd', p_ctx, vc)
    ol = ol.reshape(B, S, B_HEADS * B_DIM)
    out_c = None
    if need_ctx:
        pc = jax.nn.softmax(jnp.einsum('bqhd,bkhd->bhqk', qc, kc, preferred_element_type=F32) * scale, axis=-1)
        out_c = jnp.einsum('bhqk,bkhd->bqhd', pc.astype(vc.dtype), vc).reshape(B, C, B_HEADS * B_DIM)
    return out_c, ol

def pool_mix(u, w_pool, pool_scale):
    B, L, _ = u.shape
    uf = u.astype(F32)
    cs = jnp.concatenate([jnp.zeros((B, 1, D_GROUP), F32), lax.cumsum(uf, axis=1)], axis=1)
    t = jnp.arange(L)
    outs = []
    for g, w in enumerate(POOL_SIZES):
        lo = jnp.clip(t - w // 2, 0, L)
        hi = jnp.clip(t + w // 2, 0, L)
        sl = slice(g * POOL_CH, (g + 1) * POOL_CH)
        mean = (cs[:, hi, sl] - cs[:, lo, sl]) / (hi - lo).astype(F32)[None, :, None]
        outs.append((mean - uf[..., sl]).astype(u.dtype) @ w_pool[g])
    return jnp.concatenate(outs, axis=-1) * pool_scale

def hyena_filters(L, w1, b1, w2, b2, w3, b3):
    t = jnp.arange(L, dtype=F32)
    t_norm = t / max(L - 1, 1)
    bands = jnp.linspace(1e-4, HY_BANDS - 1, HY_BANDS, dtype=F32)
    ang = (2.0 * math.pi / L) * t[:, None] * bands[None, :]
    z = jnp.concatenate([t_norm[:, None], jnp.cos(ang), jnp.sin(ang)], axis=-1)
    h = jnp.sin(HY_SIN_FREQ * (z @ w1.astype(F32) + b1.astype(F32)))
    h = jnp.sin(HY_SIN_FREQ * (h @ w2.astype(F32) + b2.astype(F32)))
    h = (h @ w3.astype(F32) + b3.astype(F32)).reshape(L, HY_ORDER, 2, HY_CH)
    deltas = jnp.abs(jnp.linspace(HY_MIN_DECAY, HY_MAX_DECAY, HY_CH, dtype=F32))
    h = h * jnp.exp(-t_norm[:, None, None, None] * deltas)
    return h * lax.rsqrt(jnp.sum(h * h, axis=(0, 2), keepdims=True) + EPS)

def bidir_long_conv(u, h_fwd, h_bwd, d_skip):
    L = u.shape[1]
    k = jnp.concatenate([h_fwd, jnp.zeros_like(h_fwd[:1]), h_bwd[:0:-1]], axis=0)
    uf = u.astype(F32)
    y = jnp.fft.irfft(jnp.fft.rfft(uf, n=2 * L, axis=1) * jnp.fft.rfft(k, axis=0)[None], n=2 * L, axis=1)[:, :L]
    return (y + uf * d_skip.astype(F32)).astype(u.dtype)

def hyena_mix(u, w_short, b_short, filt, d_skip):
    up = jnp.pad(u, ((0, 0), (1, 1), (0, 0)))
    u = up[:, :-2] * w_short[0] + up[:, 1:-1] * w_short[1] + up[:, 2:] * w_short[2] + b_short
    x1, x2, v = jnp.split(u, 3, axis=-1)
    z = x1 * bidir_long_conv(v, filt[:, 0, 0], filt[:, 0, 1], d_skip[0])
    return x2 * bidir_long_conv(z, filt[:, 1, 0], filt[:, 1, 1], d_skip[1])

def moe(x, router_w, router_b, w1, w3, w2):
    N = x.shape[0]
    per_group = N_EXPERTS // N_EXPERT_GROUPS
    scores = jax.nn.softmax((x @ router_w).astype(F32), axis=-1)
    sel = scores + router_b.astype(F32)
    grp_score = jnp.sum(lax.top_k(sel.reshape(N, N_EXPERT_GROUPS, per_group), TOP_K)[0], axis=-1)
    _, gidx = lax.top_k(grp_score, TOPK_GROUPS)
    gmask = jnp.sum(jax.nn.one_hot(gidx, N_EXPERT_GROUPS, dtype=F32), axis=1)
    emask = jnp.repeat(gmask, per_group, axis=1) > 0
    _, eidx = lax.top_k(jnp.where(emask, sel, -jnp.inf), TOP_K)
    w = jnp.take_along_axis(scores, eidx, axis=1)
    w = w / jnp.sum(w, axis=-1, keepdims=True)
    gates = jnp.sum(jax.nn.one_hot(eidx, N_EXPERTS, dtype=F32) * w[..., None], axis=1).astype(x.dtype)
    out = jnp.zeros_like(x)
    for e in range(N_EXPERTS):
        h = jax.nn.silu(x @ w1[e]) * (x @ w3[e])
        out = out + gates[:, e:e + 1] * (h @ w2[e])
    return out

def trunk_layer(xc, xl, c, c_ctx, lp, router_w, router_b, li, need_ctx):
    B, S, D = xl.shape
    C = xc.shape[1]
    mod_l = jnp.split(jax.nn.silu(c) @ lp['ada_w'] + lp['ada_b'], 6, axis=-1)
    mod_c = jnp.split(jax.nn.silu(c_ctx) @ lp['ada_w'] + lp['ada_b'], 6, axis=-1)
    sh1_l, sc1_l, g1_l, sh2_l, sc2_l, g2_l = [m[:, None, :] for m in mod_l]
    sh1_c, sc1_c, g1_c, sh2_c, sc2_c, g2_c = mod_c
    hl = rmsnorm(xl, lp['norm1_g']) * (1.0 + sc1_l) + sh1_l
    hc = rmsnorm(xc, lp['norm1_g']) * (1.0 + sc1_c) + sh1_c
    aq_l, ak_l, av_l, bq_l, bk_l, bv_l, pool_l, hy_l = split_cols(hl @ lp['w_in'])
    aq_c, ak_c, av_c, bq_c, bk_c, bv_c, pool_c, hy_c = split_cols(hc @ lp['w_in'])
    a_c, a_l = diff_attention(aq_c, ak_c, av_c, aq_l, ak_l, av_l, lp['a_lambda'], lp['a_subln_g'], li, need_ctx)
    b_c, b_l = neighbourhood_attention(bq_c, bk_c, bv_c, bq_l, bk_l, bv_l, lp['b_rpb'], need_ctx)
    p_l = pool_mix(pool_l, lp['pool_w'], lp['pool_scale'])
    filt_l = hyena_filters(S, lp['hy_f_w1'], lp['hy_f_b1'], lp['hy_f_w2'], lp['hy_f_b2'], lp['hy_f_w3'], lp['hy_f_b3'])
    h_l = hyena_mix(hy_l, lp['hy_short_w'], lp['hy_short_b'], filt_l, lp['hy_skip'])
    xl = xl + g1_l * (jnp.concatenate([a_l, b_l, p_l, h_l], axis=-1) @ lp['w_out'])
    if need_ctx:
        p_c = pool_mix(pool_c, lp['pool_w'], lp['pool_scale'])
        filt_c = hyena_filters(C, lp['hy_f_w1'], lp['hy_f_b1'], lp['hy_f_w2'], lp['hy_f_b2'], lp['hy_f_w3'], lp['hy_f_b3'])
        h_c = hyena_mix(hy_c, lp['hy_short_w'], lp['hy_short_b'], filt_c, lp['hy_skip'])
        xc = xc + g1_c * (jnp.concatenate([a_c, b_c, p_c, h_c], axis=-1) @ lp['w_out'])
    hl2 = rmsnorm(xl, lp['norm2_g']) * (1.0 + sc2_l) + sh2_l
    if need_ctx:
        hc2 = rmsnorm(xc, lp['norm2_g']) * (1.0 + sc2_c) + sh2_c
        tok = jnp.concatenate([hc2, hl2], axis=1).reshape(B * (C + S), D)
        y = moe(tok, router_w, router_b, lp['moe_w1'], lp['moe_w3'], lp['moe_w2']).reshape(B, C + S, D)
        xc = xc + g2_c * y[:, :C]
        xl = xl + g2_l * y[:, C:]
    else:
        y = moe(hl2.reshape(B * S, D), router_w, router_b, lp['moe_w1'], lp['moe_w3'], lp['moe_w2'])
        xl = xl + g2_l * y.reshape(B, S, D)
    return xc, xl

def first_inputs(seed: int = 0) -> dict:
    key = jax.random.key(seed)
    ks = iter(jax.random.split(key, 40))

    def nrm(shape, s):
        return s * jax.random.normal(next(ks), shape, F32)

    return {
        'x': nrm((BATCH, SEQ, D_MODEL), 1.0),
        'c': nrm((BATCH, D_MODEL), 1.0),
        'ctx': nrm((BATCH, CTX_LEN, D_MODEL), 1.0),
        'c_ctx': nrm((D_MODEL,), 1.0),
        'norm1_g': 1.0 + nrm((DEPTH, D_MODEL), 0.1),
        'norm2_g': 1.0 + nrm((DEPTH, D_MODEL), 0.1),
        'ada_w': nrm((DEPTH, D_MODEL, 6 * D_MODEL), 0.5 * D_MODEL ** -0.5),
        'ada_b': nrm((DEPTH, 6 * D_MODEL), 0.02),
        'w_in': nrm((DEPTH, D_MODEL, D_IN), D_MODEL ** -0.5),
        'w_out': nrm((DEPTH, D_MIX, D_MODEL), D_MIX ** -0.5),
        'a_lambda': nrm((DEPTH, 4, A_QK), 0.1),
        'a_subln_g': 1.0 + nrm((DEPTH, A_V), 0.1),
        'b_rpb': nrm((DEPTH, B_HEADS, 2 * WIN_R - 1, 2 * WIN_C - 1), 0.1),
        'pool_w': nrm((DEPTH, len(POOL_SIZES), POOL_CH, POOL_CH), POOL_CH ** -0.5),
        'pool_scale': 1.0 + nrm((DEPTH, D_GROUP), 0.1),
        'hy_short_w': nrm((DEPTH, HY_SHORT, (HY_ORDER + 1) * HY_CH), 0.5),
        'hy_short_b': nrm((DEPTH, (HY_ORDER + 1) * HY_CH), 0.02),
        'hy_f_w1': nrm((DEPTH, HY_EMB, HY_HIDDEN), HY_EMB ** -0.5),
        'hy_f_b1': nrm((DEPTH, HY_HIDDEN), 0.1),
        'hy_f_w2': nrm((DEPTH, HY_HIDDEN, HY_HIDDEN), HY_HIDDEN ** -0.5),
        'hy_f_b2': nrm((DEPTH, HY_HIDDEN), 0.1),
        'hy_f_w3': nrm((DEPTH, HY_HIDDEN, HY_ORDER * 2 * HY_CH), HY_HIDDEN ** -0.5),
        'hy_f_b3': nrm((DEPTH, HY_ORDER * 2 * HY_CH), 0.1),
        'hy_skip': nrm((DEPTH, HY_ORDER, HY_CH), 0.5),
        'router_w': nrm((D_MODEL, N_EXPERTS), D_MODEL ** -0.5),
        'router_b': nrm((N_EXPERTS,), 0.01),
        'moe_w1': nrm((DEPTH, N_EXPERTS, D_MODEL, D_EXPERT), D_MODEL ** -0.5),
        'moe_w3': nrm((DEPTH, N_EXPERTS, D_MODEL, D_EXPERT), D_MODEL ** -0.5),
        'moe_w2': nrm((DEPTH, N_EXPERTS, D_EXPERT, D_MODEL), D_EXPERT ** -0.5),
        'final_g': 1.0 + nrm((D_MODEL,), 0.1),
    }

def first_block(x, c, ctx, c_ctx, norm1_g, norm2_g, ada_w, ada_b, w_in, w_out, a_lambda, a_subln_g,
              b_rpb, pool_w, pool_scale, hy_short_w, hy_short_b, hy_f_w1, hy_f_b1, hy_f_w2, hy_f_b2,
              hy_f_w3, hy_f_b3, hy_skip, router_w, router_b, moe_w1, moe_w3, moe_w2, final_g):
    xl, xc = x, ctx
    for li in range(DEPTH):
        lp = {
            'norm1_g': norm1_g[li], 'norm2_g': norm2_g[li], 'ada_w': ada_w[li], 'ada_b': ada_b[li],
            'w_in': w_in[li], 'w_out': w_out[li], 'a_lambda': a_lambda[li], 'a_subln_g': a_subln_g[li],
            'b_rpb': b_rpb[li], 'pool_w': pool_w[li], 'pool_scale': pool_scale[li],
            'hy_short_w': hy_short_w[li], 'hy_short_b': hy_short_b[li],
            'hy_f_w1': hy_f_w1[li], 'hy_f_b1': hy_f_b1[li], 'hy_f_w2': hy_f_w2[li], 'hy_f_b2': hy_f_b2[li],
            'hy_f_w3': hy_f_w3[li], 'hy_f_b3': hy_f_b3[li], 'hy_skip': hy_skip[li],
            'moe_w1': moe_w1[li], 'moe_w3': moe_w3[li], 'moe_w2': moe_w2[li],
        }
        xc, xl = trunk_layer(xc, xl, c, c_ctx, lp, router_w, router_b, li, need_ctx=(li < DEPTH - 1))
    return rmsnorm(xl, final_g)


DEPTH_2 = 2

N_META = 16
BLOCK = 128
META_PAD = BLOCK - N_META
RMS_EPS = 1e-6
NEG_INF = -1e30

LRU_WIDTH = D_MODEL // 2
LRU_HEADS = 8
LRU_BLOCK_W = LRU_WIDTH // LRU_HEADS
CONV_W = 4
LRU_C = 8.0

ATT_HEADS = 8
ATT_KV_HEADS = 2
ATT_HEAD_DIM = 64
WINDOW = 128
ROPE_THETA = 500000.0
ROT_DIM = ATT_HEAD_DIM // 4
Q_WIDTH = ATT_HEADS * ATT_HEAD_DIM
KV_WIDTH = ATT_KV_HEADS * ATT_HEAD_DIM
AB_IN_WIDTH = 2 * LRU_WIDTH + Q_WIDTH + 2 * KV_WIDTH
AB_OUT_WIDTH = LRU_WIDTH + Q_WIDTH
SPLIT_AB = (LRU_WIDTH, 2 * LRU_WIDTH, 2 * LRU_WIDTH + Q_WIDTH, 2 * LRU_WIDTH + Q_WIDTH + KV_WIDTH)

RET_HEADS = 4
RET_QK_DIM = D_MODEL // RET_HEADS
RET_V_DIM = 2 * D_MODEL // RET_HEADS
RET_THETA = 10000.0
RET_IN_WIDTH = 6 * D_MODEL
SPLIT_RET = (D_MODEL, 2 * D_MODEL, 4 * D_MODEL)

D_FF = -(-8 * D_MODEL // (3 * 256)) * 256


F32_2 = jnp.float32

def _rmsnorm(x, gain):
    xf = x.astype(F32_2)
    y = xf * lax.rsqrt(jnp.mean(xf * xf, axis=-1, keepdims=True) + RMS_EPS)
    return (y * gain.astype(F32_2)).astype(x.dtype)

def _rms_noaffine(x):
    xf = x.astype(F32_2)
    return xf * lax.rsqrt(jnp.mean(xf * xf, axis=-1, keepdims=True) + RMS_EPS)

def _rope_tables(n_pos, rot_dim, theta):
    half = rot_dim // 2
    inv_freq = jnp.power(jnp.asarray(theta, F32_2), -jnp.arange(half, dtype=F32_2) / half)
    ang = jnp.arange(n_pos, dtype=F32_2)[:, None] * inv_freq[None, :]
    return jnp.cos(ang), jnp.sin(ang)

def _rotary(x, cos, sin):
    half = cos.shape[-1]
    c = cos[None, :, None, :]
    s = sin[None, :, None, :]
    x1 = x[..., :half].astype(F32_2)
    x2 = x[..., half:2 * half].astype(F32_2)
    rot = jnp.concatenate([x1 * c - x2 * s, x2 * c + x1 * s], axis=-1).astype(x.dtype)
    return jnp.concatenate([rot, x[..., 2 * half:]], axis=-1)

def _rg_lru(xr, conv_w, conv_b, w_a, b_a, w_i, b_i, lam):
    B, T, W = xr.shape
    xp = jnp.pad(xr, ((0, 0), (CONV_W - 1, 0), (0, 0)))
    xc = sum((xp[:, j:j + T, :] * conv_w[j] for j in range(CONV_W)), conv_b)
    xh = xc.reshape(B, T, LRU_HEADS, LRU_BLOCK_W)
    r = jax.nn.sigmoid((jnp.einsum('bthi,hij->bthj', xh, w_a) + b_a).astype(F32_2)).reshape(B, T, W)
    i = jax.nn.sigmoid((jnp.einsum('bthi,hij->bthj', xh, w_i) + b_i).astype(F32_2)).reshape(B, T, W)
    log_a = -LRU_C * r * jax.nn.softplus(-lam.astype(F32_2))
    a = jnp.exp(log_a)
    mult = jnp.sqrt(-jnp.expm1(2.0 * log_a))
    mult = jnp.where(jnp.arange(T)[None, :, None] == 0, 1.0, mult)
    b = mult * i * xc.astype(F32_2)

    def combine(left, right):
        a_l, b_l = left
        a_r, b_r = right
        return a_l * a_r, a_r * b_l + b_r

    _, h = lax.associative_scan(combine, (a, b), axis=1)
    return h.astype(xr.dtype)

def _swa_with_sinks(q, k, v, sinks):
    B, T, Hq, Dh = q.shape
    G = ATT_HEADS // ATT_KV_HEADS
    Tp = T + META_PAD
    NB = Tp // BLOCK
    qb = jnp.pad(q, ((0, 0), (META_PAD, 0), (0, 0), (0, 0))).reshape(B, NB, BLOCK, ATT_KV_HEADS, G, Dh)
    kpad = ((0, 0), (META_PAD + BLOCK, 0), (0, 0), (0, 0))
    kb = jnp.pad(k, kpad).reshape(B, NB + 1, BLOCK, ATT_KV_HEADS, Dh)
    vb = jnp.pad(v, kpad).reshape(B, NB + 1, BLOCK, ATT_KV_HEADS, Dh)
    k_win = jnp.concatenate([kb[:, :-1], kb[:, 1:]], axis=2)
    v_win = jnp.concatenate([vb[:, :-1], vb[:, 1:]], axis=2)
    k_meta = k[:, :N_META]
    v_meta = v[:, :N_META]
    scale = Dh ** -0.5
    s_meta = jnp.einsum('bnqhgd,bkhd->bnhgqk', qb, k_meta)
    s_win = jnp.einsum('bnqhgd,bnkhd->bnhgqk', qb, k_win)
    s = jnp.concatenate([s_meta, s_win], axis=-1).astype(F32_2) * scale
    nb = jnp.arange(NB)[:, None]
    qpos = nb * BLOCK + jnp.arange(BLOCK)[None, :] - META_PAD
    kpos = (nb - 1) * BLOCK + jnp.arange(2 * BLOCK)[None, :] - META_PAD
    qp = qpos[:, :, None]
    kp = kpos[:, None, :]
    win_mask = (kp >= N_META) & (kp <= qp) & (qp - kp < WINDOW)
    meta_mask = jnp.arange(N_META)[None, None, :] <= qp
    mask = jnp.concatenate([meta_mask, win_mask], axis=-1)
    s = jnp.where(mask[None, :, None, None], s, NEG_INF)
    sink = jnp.broadcast_to(sinks.astype(F32_2).reshape(1, 1, ATT_KV_HEADS, G, 1, 1), s.shape[:-1] + (1,))
    p = jax.nn.softmax(jnp.concatenate([s, sink], axis=-1), axis=-1)[..., :-1].astype(v.dtype)
    o = (jnp.einsum('bnhgqk,bkhd->bnqhgd', p[..., :N_META], v_meta)
         + jnp.einsum('bnhgqk,bnkhd->bnqhgd', p[..., N_META:], v_win))
    return o.reshape(B, Tp, Hq * Dh)[:, META_PAD:]

def _mixer_rglru_swa(h, cos, sin, w_in, conv_w, conv_b, w_a, b_a, w_i, b_i, lam,
                     q_gain, k_gain, sinks, w_out):
    B, T, _ = h.shape
    x_rnn, gate, q, k, v = jnp.split(h @ w_in, SPLIT_AB, axis=-1)
    y_rnn = jax.nn.gelu(gate) * _rg_lru(x_rnn, conv_w, conv_b, w_a, b_a, w_i, b_i, lam)
    q = _rotary(_rmsnorm(q.reshape(B, T, ATT_HEADS, ATT_HEAD_DIM), q_gain), cos, sin)
    k = _rotary(_rmsnorm(k.reshape(B, T, ATT_KV_HEADS, ATT_HEAD_DIM), k_gain), cos, sin)
    v = v.reshape(B, T, ATT_KV_HEADS, ATT_HEAD_DIM)
    y_att = _swa_with_sinks(q, k, v, sinks)
    return jnp.concatenate([y_rnn, y_att], axis=-1) @ w_out

def _mixer_retention(h, cos, sin, w_in, w_out):
    B, T, _ = h.shape
    q, k, v, g = jnp.split(h @ w_in, SPLIT_RET, axis=-1)
    q = _rotary(q.reshape(B, T, RET_HEADS, RET_QK_DIM), cos, sin)
    k = _rotary(k.reshape(B, T, RET_HEADS, RET_QK_DIM), cos, sin) * (RET_QK_DIM ** -0.5)
    v = v.reshape(B, T, RET_HEADS, RET_V_DIM)
    Tp = T + META_PAD
    NC = Tp // BLOCK

    def to_chunks(t):
        d = t.shape[-1]
        t = jnp.pad(t, ((0, 0), (META_PAD, 0), (0, 0), (0, 0)))
        return t.reshape(B, NC, BLOCK, RET_HEADS, d).transpose(1, 0, 3, 2, 4)

    qc, kc, vc = to_chunks(q), to_chunks(k), to_chunks(v)
    log_g = jnp.log1p(-jnp.exp2(-5.0 - jnp.arange(RET_HEADS, dtype=F32_2)))
    idx = jnp.arange(BLOCK, dtype=F32_2)
    diff = idx[:, None] - idx[None, :]
    decay_intra = jnp.where(diff >= 0, jnp.exp(jnp.maximum(diff, 0.0)[None] * log_g[:, None, None]), 0.0)
    decay_q = jnp.exp((idx + 1.0)[None] * log_g[:, None])
    decay_k = jnp.exp((BLOCK - 1.0 - idx)[None] * log_g[:, None])
    decay_chunk = jnp.exp(BLOCK * log_g)

    def step(state, chunk):
        qn, kn, vn = chunk
        vf = vn.astype(F32_2)
        qk = jnp.einsum('bhid,bhjd->bhij', qn, kn).astype(F32_2) * decay_intra
        o = (jnp.einsum('bhij,bhjv->bhiv', qk, vf)
             + jnp.einsum('bhid,bhdv->bhiv', qn.astype(F32_2) * decay_q[..., None], state))
        state = (decay_chunk[:, None, None] * state
                 + jnp.einsum('bhjd,bhjv->bhdv', kn.astype(F32_2) * decay_k[..., None], vf))
        return state, o

    state0 = jnp.zeros((B, RET_HEADS, RET_QK_DIM, RET_V_DIM), F32_2)
    _, o = lax.scan(step, state0, (qc, kc, vc))
    o = o.transpose(1, 0, 3, 2, 4).reshape(B, Tp, RET_HEADS, RET_V_DIM)[:, META_PAD:]
    o = _rms_noaffine(o).reshape(B, T, 2 * D_MODEL).astype(h.dtype)
    return (jax.nn.silu(g) * o) @ w_out

def _swiglu(h, w_gu, w_down):
    gate, up = jnp.split(h @ w_gu, 2, axis=-1)
    return (jax.nn.silu(gate) * up) @ w_down

def second_inputs(seed: int = 0) -> dict:
    key = jax.random.key(seed)
    keys = jax.random.split(key, 24)
    n_even = (DEPTH_2 + 1) // 2
    n_odd = DEPTH_2 // 2

    def normal(k, shape, scale):
        return jax.random.normal(k, shape, F32_2) * scale

    def gain(k, shape):
        return 1.0 + 0.02 * jax.random.normal(k, shape, F32_2)

    u = jax.random.uniform(keys[10], (n_even, LRU_WIDTH), F32_2, minval=0.9, maxval=0.999)
    a = u ** (1.0 / LRU_C)
    lam = jnp.log(a) - jnp.log1p(-a)
    return {
        'x': normal(keys[0], (BATCH, SEQ, D_MODEL), 1.0),
        'meta_tokens': normal(keys[1], (N_META, D_MODEL), 1.0),
        'mix_norm_ab': gain(keys[2], (n_even, D_MODEL)),
        'ab_w_in': normal(keys[3], (n_even, D_MODEL, AB_IN_WIDTH), D_MODEL ** -0.5),
        'lru_conv_w': normal(keys[4], (n_even, CONV_W, LRU_WIDTH), CONV_W ** -0.5),
        'lru_conv_b': normal(keys[5], (n_even, LRU_WIDTH), 0.01),
        'lru_w_a': normal(keys[6], (n_even, LRU_HEADS, LRU_BLOCK_W, LRU_BLOCK_W), LRU_BLOCK_W ** -0.5),
        'lru_b_a': normal(keys[7], (n_even, LRU_HEADS, LRU_BLOCK_W), 0.01),
        'lru_w_i': normal(keys[8], (n_even, LRU_HEADS, LRU_BLOCK_W, LRU_BLOCK_W), LRU_BLOCK_W ** -0.5),
        'lru_b_i': normal(keys[9], (n_even, LRU_HEADS, LRU_BLOCK_W), 0.01),
        'lru_lambda': lam,
        'q_norm': gain(keys[11], (n_even, ATT_HEAD_DIM)),
        'k_norm': gain(keys[12], (n_even, ATT_HEAD_DIM)),
        'attn_sinks': normal(keys[13], (n_even, ATT_HEADS), 0.5),
        'ab_w_out': normal(keys[14], (n_even, AB_OUT_WIDTH, D_MODEL), AB_OUT_WIDTH ** -0.5),
        'mix_norm_ret': gain(keys[15], (n_odd, D_MODEL)),
        'ret_w_in': normal(keys[16], (n_odd, D_MODEL, RET_IN_WIDTH), D_MODEL ** -0.5),
        'ret_w_out': normal(keys[17], (n_odd, 2 * D_MODEL, D_MODEL), (2 * D_MODEL) ** -0.5),
        'ffn_norm': gain(keys[18], (DEPTH_2, D_MODEL)),
        'ffn_w_gu': normal(keys[19], (DEPTH_2, D_MODEL, 2 * D_FF), D_MODEL ** -0.5),
        'ffn_w_down': normal(keys[20], (DEPTH_2, D_FF, D_MODEL), D_FF ** -0.5),
    }

def second_block(x, meta_tokens, mix_norm_ab, ab_w_in, lru_conv_w, lru_conv_b, lru_w_a, lru_b_a,
              lru_w_i, lru_b_i, lru_lambda, q_norm, k_norm, attn_sinks, ab_w_out,
              mix_norm_ret, ret_w_in, ret_w_out, ffn_norm, ffn_w_gu, ffn_w_down):
    B = x.shape[0]
    meta = jnp.broadcast_to(meta_tokens[None].astype(x.dtype), (B, N_META, D_MODEL))
    h = jnp.concatenate([meta, x], axis=1)
    T = h.shape[1]
    att_cos, att_sin = _rope_tables(T, ROT_DIM, ROPE_THETA)
    ret_cos, ret_sin = _rope_tables(T, RET_QK_DIM, RET_THETA)
    for layer in range(DEPTH_2):
        j = layer // 2
        if layer % 2 == 0:
            h = h + _mixer_rglru_swa(_rmsnorm(h, mix_norm_ab[j]), att_cos, att_sin, ab_w_in[j],
                                     lru_conv_w[j], lru_conv_b[j], lru_w_a[j], lru_b_a[j],
                                     lru_w_i[j], lru_b_i[j], lru_lambda[j], q_norm[j], k_norm[j],
                                     attn_sinks[j], ab_w_out[j])
        else:
            h = h + _mixer_retention(_rmsnorm(h, mix_norm_ret[j]), ret_cos, ret_sin,
                                     ret_w_in[j], ret_w_out[j])
        h = h + _swiglu(_rmsnorm(h, ffn_norm[layer]), ffn_w_gu[layer], ffn_w_down[layer])
    return h[:, N_META:]


def setup_inputs(seed=0):
    out = dict(first_inputs(seed))
    for name, value in second_inputs(seed + 1).items():
        if name != "x":
            out[name + "_2"] = value
    return out


def reference(
    x, c, ctx, c_ctx, norm1_g, norm2_g, ada_w, ada_b, w_in, w_out, a_lambda, a_subln_g, b_rpb,
    pool_w, pool_scale, hy_short_w, hy_short_b, hy_f_w1, hy_f_b1, hy_f_w2, hy_f_b2, hy_f_w3,
    hy_f_b3, hy_skip, router_w, router_b, moe_w1, moe_w3, moe_w2, final_g, meta_tokens_2,
    mix_norm_ab_2, ab_w_in_2, lru_conv_w_2, lru_conv_b_2, lru_w_a_2, lru_b_a_2, lru_w_i_2,
    lru_b_i_2, lru_lambda_2, q_norm_2, k_norm_2, attn_sinks_2, ab_w_out_2, mix_norm_ret_2,
    ret_w_in_2, ret_w_out_2, ffn_norm_2, ffn_w_gu_2, ffn_w_down_2,
):
    x = first_block(
        x, c, ctx, c_ctx, norm1_g, norm2_g, ada_w, ada_b, w_in, w_out, a_lambda, a_subln_g,
        b_rpb, pool_w, pool_scale, hy_short_w, hy_short_b, hy_f_w1, hy_f_b1, hy_f_w2, hy_f_b2,
        hy_f_w3, hy_f_b3, hy_skip, router_w, router_b, moe_w1, moe_w3, moe_w2, final_g,
    )
    return second_block(
        x, meta_tokens_2, mix_norm_ab_2, ab_w_in_2, lru_conv_w_2, lru_conv_b_2, lru_w_a_2,
        lru_b_a_2, lru_w_i_2, lru_b_i_2, lru_lambda_2, q_norm_2, k_norm_2, attn_sinks_2,
        ab_w_out_2, mix_norm_ret_2, ret_w_in_2, ret_w_out_2, ffn_norm_2, ffn_w_gu_2,
        ffn_w_down_2,
    )


_drawn_inputs = setup_inputs


def setup_inputs(seed=0):
    import zlib

    import numpy as np

    out = dict(_drawn_inputs(seed))
    spreads = {}
    factors = {'a_lambda': 8.0,
     'b_rpb': 8.0,
     'mix_norm_ab_2': 3.708,
     'lru_b_a_2': 44.077,
     'lru_b_i_2': 32.54,
     'q_norm_2': 8.0,
     'k_norm_2': 8.0,
     'attn_sinks_2': 200.0,
     'mix_norm_ret_2': 75.863,
     'lru_conv_b_2': 4.927,
     'ffn_norm_2': 8.0}
    for name, (base, spread) in spreads.items():
        noise = np.random.default_rng([zlib.crc32(name.encode()), seed]).standard_normal(out[name].shape)
        drawn = base * np.exp(spread * noise) if base else spread * noise
        out[name] = jnp.asarray(drawn.astype(out[name].dtype))
    for name, factor in factors.items():
        out[name] = (out[name] * factor).astype(out[name].dtype)
    return out
```

```python
import math
from contextlib import ExitStack

import concourse.bass as bass
from concourse import mybir

ALU = mybir.AluOpType
ACT = mybir.ActivationFunctionType
AX_X = mybir.AxisListType.X
F32 = mybir.dt.float32
U32 = mybir.dt.uint32
I32 = mybir.dt.int32

P = 128
D = 1024
KT = D // P
S = 512
C = 256
META = 16
T2 = META + S
HALF2 = T2 // 2
NKEY = C + S
ST = S // P
NKT = NKEY // P
GRID = 64
WIN_R, WIN_C = 8, 16
HEADS = 4
DH = 64
EXPERTS = 16
FF = 2816
FFT = FF // P
SWA_HEADS = 8
RET_HEADS = 4
LAM_INIT = 0.8 - 0.6 * math.exp(0.0)
EPS = 1e-6
NEG = -1e30
TWO_PI_HI = 6.28125
TWO_PI_LO = 2 * math.pi - TWO_PI_HI
ROUND = 1.5 * 2.0 ** 23
PI_BELOW = 3.1415925

RING = 12
TILE = 1024
STREAM = [
    ("dft", 4),
    ("mod1", 16),
    ("hyena", 6), ("mixers", 10), ("values", 4),
    ("mod2", 32),
    ("w_out", 8),
    ("ab", 13), ("ab_values", 1), ("lru_gates", 1), ("ab_out", 8),
    ("ffn0", 2 * FFT + 24),
    ("ret", 12 * RET_HEADS), ("ret_out", 16),
    ("ffn1", 2 * FFT + 24),
]
EXPERT_TILES = 12
JOBS = 24
MIN_JOBS = 2 * S // P
START, N_TILES = {}, 0
for _name, _n in STREAM:
    START[_name] = N_TILES
    N_TILES += _n

SMALL = [
    ("c", 16), ("norm1_g", 8), ("norm2_g", 8), ("final_g", 8), ("norm_ab", 8), ("norm_ret", 8),
    ("norm_ffn", 16), ("ada_b", 48), ("a_lambda", 128), ("subln_g", 1), ("pool_scale", 2),
    ("short_w", 18), ("short_b", 6), ("f_b1", 1), ("f_b2", 1), ("skip", 4), ("router_w", 128),
    ("router_b", 16), ("conv_w", 16), ("conv_b", 4), ("b_a", 4), ("b_i", 4), ("lam", 4),
    ("q_norm", 1), ("k_norm", 1), ("sinks", 8),
]
CONST = [("ident", 128), ("ones", 128), ("head_ones", 128), ("swap_a", 128), ("swap_q", 128),
         ("win_mask", 64), ("falling", 16), ("earlier", 128), ("job", JOBS)]
FILTER = [("w1", 64), ("w2", 64), ("w3", 1024), ("z", 512), ("decay", 1024)]


def offsets(parts):
    at, out = 0, {}
    for name, n in parts:
        out[name] = (at, n)
        at += n
    return out, at


class Product:

    def __init__(self, banks, order, after, released, order_step=0, free_step=0):
        self.bank, self.banks, self.order, self.after, self.released = banks[0], banks, order, after, released
        self.order_step, self.free_step = order_step, free_step


class Banks:

    def __init__(self):
        self.order = 0
        self.releases = [0] * 8
        self.last = [None] * 8
        self.turn = 0

    def take(self, *banks):
        after = sorted({self.last[b] for b in banks if self.last[b] is not None})
        first = banks[0]
        self.releases[first] += 1
        p = Product(banks, self.order, after, self.releases[first])
        for b in banks:
            self.last[b] = (first, self.releases[first])
        self.order += 1
        return p

    def many(self, n, banks=tuple(range(8))):
        out = []
        for _ in range(n):
            out.append(self.take(banks[self.turn % len(banks)]))
            self.turn += 1
        return out

    def settle(self):
        waits = sorted({x for x in self.last if x is not None})
        self.last = [(b, self.releases[b]) if self.releases[b] else None for b in range(8)]
        self.turn = 0
        return waits

    def loop(self, n, turns, banks):
        assert n % len(banks) == 0
        out = [self.take(banks[i % len(banks)]) for i in range(n)]
        for p in out:
            p.order_step, p.free_step = n, n // len(banks)
        self.order += n * (turns - 1)
        for b in banks:
            self.releases[b] += (turns - 1) * (n // len(banks))
            self.last[b] = (b, self.releases[b])
        self.turn = 0
        return out


def plan():
    b = Banks()
    r = {}
    r["f_h1"], r["f_h2"] = b.many(2)
    r["f_h3"] = b.many(8)
    r["f_norm"], = b.many(1)
    r["f_spec"] = b.many(8)

    r["mod1"], r["ms_x"], r["ms_c"] = b.many(3)

    r["hy"] = b.many(6)
    for o in range(2):
        r["hy_t", o] = b.many(4)
        r["hy_f", o] = b.many(4)
        r["hy_i", o] = b.many(2)

    for name, n in (("aq", 2), ("ak", 4), ("rope", 4), ("bq", 2), ("bk", 4), ("pool", 2), ("v", NKT),
                    ("pool_w", 2)):
        r[name] = b.many(n)

    r["mod2"] = b.take(7)
    b.order -= 1
    pair = 0
    for i in range(-1, len(UNITS)):
        if i + 1 < len(UNITS):
            r["scores", i + 1] = []
            for _ in range(2 if UNITS[i + 1][0] == "A" else 1):
                r["scores", i + 1].append(b.take(2 * pair, 2 * pair + 1))
                pair = 1 - pair
        if i == len(UNITS) - 1:
            r["mod2"].order = b.order
            b.order += 1
        if i >= 0:
            r["T", i] = [b.take(4), b.take(5)]
            r["PV", i] = b.take(6)
    r["subln"] = [b.take(4), b.take(5)]

    r["before_w_out"] = b.settle()
    r["w_out"] = b.many(8)

    r["ms_2"], r["router"] = b.many(2)
    r["rows"] = b.many(8)
    r["rank"], = b.many(1)
    r["before_jobs"] = b.settle()
    r["moe_out"] = b.many(8)
    r["ms_f"], = b.many(1)
    r["ms_ab"] = b.many(2)
    r["ab"] = b.many(26)
    r["ab_v"] = b.many(5)
    r["lru"] = b.many(16)
    r["qk_ms"] = b.many(10)
    r["qk_sw"] = b.many(10)
    r["before_swa"] = b.settle()
    for i in range(-1, len(GROUPS)):
        if i + 1 < len(GROUPS):
            r["swa_s", i + 1] = b.take(0, 1, 2, 3)
        if i >= 0:
            r["swa_t", i] = [b.take(4 + h % 2) for h in range(4)]
            r["swa_o", i] = b.take(6 + i % 2)
    r["before_ab_out"] = b.settle()
    r["ab_out"] = b.many(16)

    for n, halves in ((0, 2), (1, 1)):
        r["ffn_ms", n] = b.many(halves)
        r["before_ffn", n] = b.settle()
        r["ffn_loop", n] = b.loop(12 * halves, 3, range(6))
        r["ffn_rest", n] = b.many(8 * halves, tuple(range(6)))
        r["before_down", n] = b.settle()
        r["ffn_down", n] = b.loop(4 * halves, 2, range(4 * halves))
        if n == 0:
            r["ms_ret"] = b.many(2)
            r["before_ret"] = b.settle()
            body = b.loop(25, RET_HEADS, range(5))
            for name, k in (("q", 2), ("k", 4), ("v", 5), ("g", 4), ("s", 5), ("o", 4), ("ms", 1)):
                r["ret", name], body = body[:k], body[k:]
            r["ret_out"] = b.many(8)
    return r


UNITS = [(a, h, t) for a in "AB" for h in range(HEADS) for t in range(ST)]
GROUPS = [(t, a) for t in range(5) for a in range(2)]
HALVES2 = [(0, HALF2), (HALF2, HALF2)]


def swa_keys(t):
    if t == 0:
        return [(0, 0, META)]
    if t == 1:
        return [(0, 0, META + P)]
    return [(0, 0, META), (META, META + P * (t - 2), 2 * P)]


def swa_queries(t):
    return (0, META) if t == 0 else (META + P * (t - 1), P)


def swa_chunks(t):
    chunks = [(0, META, 0)]
    if t >= 1:
        chunks += [(META, P, max(t - 1, 1))]
    if t >= 2:
        chunks += [(META + P, P, t)]
    return chunks


SWA_MASKS = {0: (2 * META + 3 * P, META), 1: (META + 2 * P, META + P)}


MIXED_1 = 4
MIXED_2 = MIXED_1 + 4


def two_blocks(nc, d):
    r = plan()
    s_off, s_n = offsets(SMALL)
    c_off, c_n = offsets(CONST)
    f_off, f_n = offsets(FILTER)
    with ExitStack() as ctx:
        def sb(name, *shape):
            return ctx.enter_context(nc.sbuf_tensor(name, [P, *shape], F32))

        def sem(name):
            return ctx.enter_context(nc.semaphore(name))

        ring = sb("ring", RING, TILE)
        x = sb("residual", KT, T2)
        h_flat = sb("normed", KT * NKEY)
        mix = sb("mixed", KT, T2)
        small = sb("small", s_n)
        const = sb("const_sb", c_n)
        rstd = sb("rstd", T2 + C)
        tiny = sb("tiny", 640)
        arena = sb("arena", 23552)
        ps = ctx.enter_context(nc.psum_tensor("products", [P, 8, 512], F32))
        h1 = h_flat[:, :].rearrange("p (k t) -> p k t", k=KT)
        h2 = h_flat[:, 0:KT * T2].rearrange("p (k t) -> p k t", k=KT)

        def par(name):
            o, n = s_off[name]
            return small[:, o:o + n]

        def con(name):
            o, n = c_off[name]
            return const[:, o:o + n]

        def piece(of, at, *shape):
            n = math.prod(shape)
            v = of[:, at:at + n]
            if len(shape) == 2:
                v = v.rearrange("p (a b) -> p a b", a=shape[0])
            if len(shape) == 3:
                v = v.rearrange("p (a b c) -> p a b c", a=shape[0], b=shape[1])
            if len(shape) == 4:
                v = v.rearrange("p (a b c e) -> p a b c e", a=shape[0], b=shape[1], c=shape[2])
            return v

        ident, ones, head_ones = con("ident"), con("ones"), con("head_ones")
        eps = tiny[:, 0:1]
        silu_c = piece(tiny, 2, KT, 2)
        mod1 = piece(tiny, 18, 16, 2)
        gain1 = piece(tiny, 50, KT, 2)
        mod2 = tiny[:, 66:98]
        gain2 = tiny[:, 98:106]
        conv_rs = tiny[:, 106:110]
        lam_t = tiny[:, 110:180]
        neg_lam = tiny[:, 180:181]
        sub_g = tiny[:, 181:182]
        neg_max = piece(tiny, 182, 2, 4)
        row_sum = piece(tiny, 190, 2, 4)
        row_inv = piece(tiny, 198, 2, 4)
        qk_gain = tiny[:, 206:208]
        lru_t = tiny[:, 208:244]
        lru_c = tiny[:, 244:248]
        neg_sink = tiny[:, 248:256]
        sink_d = piece(tiny, 256, 2, 4)
        sink_e = piece(tiny, 264, 2, 4)

        kc = piece(arena, 0, ST, 2, 256)
        ks = piece(arena, 2048, ST, 2, 256)
        dft = piece(arena, 4096, 2, ST, S)
        filt = piece(arena, 8192, ST, 2, 2, 256)
        diff = piece(arena, 12288, ST, 2, 256)
        arg = piece(arena, 14336, 3, S)
        sin1, sin2 = h_flat[:, 4736:5248], h_flat[:, 5248:5760]
        ctx_raw = piece(h_flat, 0, KT, C)
        f_in = h_flat[:, 2048:2048 + f_n]

        def fil(name):
            o, n = f_off[name]
            return f_in[:, o:o + n]

        f_sq = mix[:, :, :].rearrange("p k t -> p (k t)")[:, 0:4096].rearrange(
            "p (a b c e) -> p a b c e", a=ST, b=2, c=2)
        hy_raw = piece(arena, 8192, 6, S + 2)
        hy = piece(arena, 11276, 6, S)
        sig_t = piece(arena, 8192, ST, 256)
        spec = piece(arena, 9216, 2, ST, 256)
        prod_t = piece(arena, 14348, 2, 2, 256)
        z1 = piece(arena, 15372, 2, S)
        y_t = piece(arena, 16396, S)
        bias = piece(arena, 17656, HEADS, 15, GRID)
        rope_a = piece(arena, 21496, 2, S)
        pool_inv = piece(arena, 22520, 2, S)
        pool_w = piece(arena, 17400, 2, P)
        aq = piece(arena, 0, 2, S)
        ak = piece(arena, 1024, 2, NKEY)
        bq = piece(arena, 2560, 2, S)
        bk = piece(arena, 3584, 2, NKEY)
        vals = piece(arena, 5120, NKT, 2, 256)
        o_a = piece(arena, 8192, 2, S)
        prob = piece(arena, 9216, 2, 2, NKEY)
        prob_t = piece(arena, 12288, 2, NKT, P)
        raw_a = piece(arena, 13824, 4, S)
        prob_sq = piece(arena, 13824, 2, S)
        sub_rs_t = arena[:, 14848:15872]
        pool_u = piece(arena, 9216, 2, S + 16)
        pool_s = [piece(arena, 10272 + 1056 * i, 2, S + 16) for i in range(4)]
        pool_y = piece(arena, 9216 + 1056 * 5, 2, S)
        rows = piece(arena, 0, ST, D)
        job_in = arena[:, 4096:5120]
        job_t = piece(arena, 5120, KT, P)
        silu_t = arena[:, 6144:6656]
        hid = piece(arena, 6656, 4, P)
        job_out = piece(arena, 7168, 2, S)
        got = piece(arena, 8192, 2, ST, D)
        both = piece(arena, 0, ST, D)
        rt = [piece(arena, 16384 + 64 * i, ST, EXPERTS) for i in range(18)]
        place = piece(arena, 17536, 2, ST)
        place_i = arena[:, 17544:17552].bitcast(U32)
        gate_c = piece(arena, 17552, 2, ST)
        job_e = arena[:, 17568:17568 + JOBS]
        job_i = arena[:, 17600:17600 + JOBS].bitcast(I32)
        n_jobs_i = arena[:, 17632:17633].bitcast(I32)
        job_x = nc.dram_tensor("job_rows", (JOBS * P, D), F32, kind="Internal").ap()
        xr = piece(arena, 0, 4, 3 + T2)
        gate = piece(arena, 2124, 4, T2)
        qk = piece(arena, 4236, 5, T2)
        val2 = piece(arena, 6876, 5, P)
        xc = piece(arena, 7516, 4, T2)
        g_r = piece(arena, 9628, 4, T2)
        g_i = piece(arena, 11740, 4, T2)
        g_a = piece(arena, 13852, 4, T2)
        g_m = piece(arena, 15964, 4, T2)
        rope_q = piece(arena, 18076, 2, T2)
        swa_mask = arena[:, 19132:19564]
        qk_sq = piece(arena, 7516, 5, T2)
        qk_rs = piece(arena, 10156, 5, T2)
        rope_t = piece(arena, 12796, 2, T2)
        prob2 = piece(arena, 7516, 2, 4, 272)
        prob2_t = piece(arena, 9692, 2, 4, 384)
        act_w = piece(arena, 0, FFT, T2)
        silu_w = piece(arena, 11616, 6, T2)
        ret_y = piece(arena, 0, 16, S)
        ret_q = piece(arena, 8192, 2, S)
        ret_k = piece(arena, 9216, 2, T2)
        ret_v = piece(arena, 10272, 5, S)
        ret_g = piece(arena, 12832, 4, S)
        ret_o = piece(arena, 14880, 4, S)
        ret_sq = piece(arena, 16928, 4, S)
        decay_r = piece(arena, 18976, RET_HEADS, T2)
        rope_r = piece(arena, 21088, 2, T2)
        rot_t = piece(arena, 22144, 2, T2)
        ret_s = mix[:, 0:5, 0:S]

        landed = [sem(f"weights_in_{i}") for i in range(RING)]
        begun = sem("tile_begun")
        done = sem("products_done")
        bank_free = [sem(f"bank_free_{i}") for i in range(8)]
        dve_step = sem("dve_step")
        act_step = sem("act_step")
        small_in, const_in, filter_in, x_in, ctx_in = (sem(n + "_in") for n in ("small", "const", "filter", "x", "ctx"))
        dft_in, att_in, swa_in, ret_in = (sem(n + "_in") for n in ("dft", "att", "swa", "ret"))
        eps_set = sem("eps_set")
        sin_arg, sin_ready, filter_sq, filter_rs, spec_in = (sem(n) for n in (
            "sin_arg", "sin_ready", "filter_squares", "filter_norms", "spectra_inputs"))
        silu_ready = sem("silu_c_ready")
        squares = sem("squares_ready")
        rstd_ready = sem("rstd_ready")
        scaled = sem("h_scaled")
        h_ready = sem("h_ready")
        mod1_ready, mod2_ready = sem("mod1_ready"), sem("mod2_ready")
        conv_ready, spec_ready, z_ready = sem("conv_ready"), sem("spectrum_ready"), sem("z_ready")
        roped, pooled = sem("roped"), sem("pooled")
        max_ready, exp_ready, prob_ready = sem("max_ready"), sem("exp_ready"), sem("prob_ready")
        bias_set, lam_arg, lam_exp = sem("bias_set"), sem("lam_arg"), sem("lam_exp")
        sub_sq, sub_rs = sem("o_a_squares"), sem("o_a_rstd")
        mixed = sem("mixed_ready")
        route_exp, chosen, jobs_ready = (sem(n) for n in ("router_exp", "experts_chosen", "jobs_ready"))
        zero_set, zeros_in, scattered = sem("zero_set"), sem("zeros_in"), sem("rows_scattered")
        e_landed = [sem(f"expert_tile_in_{i}") for i in range(RING)]
        e_begun = sem("expert_tile_begun")
        e_done = sem("job_products_done")
        job_read, job_turned = sem("job_rows_in"), sem("job_rows_turned")
        silu_out, hid_ready = sem("silu_ready"), sem("hidden_ready")
        y_ready, y_stored = sem("job_results_ready"), sem("job_results_stored")
        gathered, combined = [sem(f"results_in_{i}") for i in range(ST)], sem("results_combined")
        x_normed = sem("x_normed")
        xc_ready, lru_y, lru_e, lru_cr, lru_m, lru_s = (sem(n) for n in (
            "xc_ready", "lru_abs", "lru_exp", "lru_c_ready", "lru_mult_arg", "lru_mult"))
        lru_act = sem("lru_activated")
        qk_sqr, qk_rsr, qk_n, qk_rot = (sem(n) for n in ("qk_squares", "qk_rstd", "qk_normed", "qk_roped"))
        swa_max, swa_exp, swa_prob = sem("swa_max"), sem("swa_exp"), sem("swa_prob")
        wide_silu = sem("wide_silu")
        ret_qk, ret_sc, ret_or, ret_sqr, ret_rs, ret_yr = (sem(n) for n in (
            "ret_qk_ready", "ret_scores", "ret_o_ready", "ret_squares", "ret_rstd", "ret_y_ready"))
        stored = sem("stored")
        block = ctx.enter_context(nc.Block())

        def bank(p, n=512):
            return ps[:, p.bank, 0:n]

        def wide(p, n):
            return ps[:, p.bank:p.bank + len(p.banks), :].rearrange("p b n -> p (b n)")[:, 0:n]

        def plus(value, step, it):
            return value + it * step if it is not None and step else value

        def ready(eng, p, it=None):
            eng.wait_ge(done, plus(p.order + 1, p.order_step, it))

        def read(eng, p, it=None):
            eng.wait_ge(bank_free[p.bank], plus(p.released, p.free_step, it))

        def read_last(eng, p, turns):
            eng.wait_ge(bank_free[p.bank], p.released + p.free_step * (turns - 1))

        def bcast(ap, axis, n):
            a = ap.unsqueeze(axis)
            shape = list(a.shape)
            shape[axis] = n
            return a.to_broadcast(shape)

        def store(sp):
            read_last(sp, r["ffn_down", 1][-1], 2)
            sp.dma_start(d["out"], x[:, :, META:T2]).then_inc(stored, 16)
            sp.wait_ge(stored, 16)

        class Steps:

            def __init__(self, eng, step):
                self.eng, self.step, self.n, self.it, self.per = eng, step, 0, None, 0

            def link(self, ins):
                ins.then_inc(self.step, 1)
                self.n += 1
                self.eng.wait_ge(self.step, plus(self.n, self.per, self.it))

            def loop(self, it, per):
                self.it, self.per, self.first = it, per, self.n

            def end(self, turns):
                assert self.n - self.first == self.per, (self.n - self.first, self.per)
                self.n += self.per * (turns - 1)
                self.it, self.per = None, 0

        @block.sync
        def _(sp):
            def load(n):
                if n >= RING:
                    sp.wait_ge(begun, n - RING + 2)
                sp.dma_start(ring[:, n % RING, :], d["weights"][n]).then_inc(landed[n % RING], 16)

            def stream(first, last):
                turns = (last - first) // RING
                with sp.Fori(0, turns) as it:
                    for s in range(RING):
                        n = first + s
                        sp.wait_ge(begun, it * RING + (n - RING + 2))
                        sp.dma_start(ring[:, n % RING, :], d["weights"][it * RING + n]).then_inc(landed[n % RING], 16)
                for n in range(first + turns * RING, last):
                    load(n)

            before = START["ab"]
            for n in range(RING):
                load(n)
            stream(RING, before)
            slots = [(before + i) % RING for i in range(EXPERT_TILES)]
            sp.wait_ge(jobs_ready, 1)
            n_jobs = sp.value_load(n_jobs_i[0:1, 0:1], min_val=MIN_JOBS, max_val=JOBS - 1)
            e = sp.value_load(job_i[0:1, 0:1], min_val=0, max_val=EXPERTS - 1)
            for i, s in enumerate(slots):
                sp.dma_start(ring[:, s, :], d["experts"][e, i]).then_inc(e_landed[s], 16)
            with sp.Fori(1, n_jobs) as it:
                e = sp.value_load(job_i[0:1, bass.ds(it, 1)], min_val=0, max_val=EXPERTS - 1)
                for i, s in enumerate(slots):
                    sp.wait_ge(e_begun, it * EXPERT_TILES + (i - EXPERT_TILES + 2))
                    sp.dma_start(ring[:, s, :], d["experts"][e, i]).then_inc(e_landed[s], 16)
            sp.wait_ge(e_done, n_jobs * 5 + 2)
            for n in range(before, before + RING):
                sp.dma_start(ring[:, n % RING, :], d["weights"][n]).then_inc(landed[n % RING], 16)
            stream(before + RING, N_TILES)
            store(sp)

        @block.gpsimd
        def _(pool):
            pool.dma_start(small[:, :], d["small"]).then_inc(small_in, 16)
            pool.dma_start(const[:, :], d["const"]).then_inc(const_in, 16)
            pool.dma_start(f_in, d["filter"]).then_inc(filter_in, 16)
            pool.dma_start(x[:, :, META:T2], d["x"]).then_inc(x_in, 16)
            pool.dma_start(ctx_raw, d["ctx"]).then_inc(ctx_in, 16)
            pool.dma_start(x[:, :, 0:META], d["meta"]).then_inc(x_in, 16)
            pool.dma_start(dft, d["dft_half"]).then_inc(dft_in, 16)
            for to, name in ((bias, "bias"), (rope_a, "rope_a"), (pool_inv, "pool_inv"), (pool_w, "pool_w")):
                pool.dma_start(to, d[name]).then_inc(att_in, 16)
            pool.wait_ge(zero_set, 1)
            for j in range(JOBS):
                pool.dma_start(job_x[j * P:(j + 1) * P, :], h_flat[:, 0:D]).then_inc(zeros_in, 16)
            pool.wait_ge(zeros_in, 16 * JOBS)
            pool.wait_ge(jobs_ready, 1)
            for t in range(ST):
                read(pool, r["rows"][2 * t])
                read(pool, r["rows"][2 * t + 1])
                for c in range(2):
                    k = c * ST + t
                    pool.indirect_dma_start(
                        out=job_x, out_offset=bass.IndirectOffsetOnAxis(ap=place_i[:, k:k + 1], axis=0),
                        in_=rows[:, t, :], in_offset=None).then_inc(scattered, 16)
            pool.wait_ge(scattered, 16 * 2 * ST)
            pool.dma_start(job_in, job_x[0:P, :]).then_inc(job_read, 16)
            n_jobs = pool.value_load(n_jobs_i[0:1, 0:1], min_val=MIN_JOBS, max_val=JOBS - 1)
            with pool.Fori(0, n_jobs) as it:
                pool.wait_ge(e_done, it * 5 + 2)
                pool.dma_start(job_in, job_x[bass.ds(it * P + P, P), :]).then_inc(job_read, 16)
                pool.wait_ge(y_ready, it * 2 + 2)
                pool.dma_start(job_x[bass.ds(it * P, P), :], job_out.rearrange("p a b -> p (a b)")).then_inc(y_stored, 16)
                pool.wait_ge(y_stored, it * 16 + 16)
            for t in range(ST):
                for c in range(2):
                    k = c * ST + t
                    pool.indirect_dma_start(
                        out=got[:, c, t, :], out_offset=None,
                        in_=job_x, in_offset=bass.IndirectOffsetOnAxis(ap=place_i[:, k:k + 1], axis=0)).then_inc(gathered[t], 16)
            read(pool, r["moe_out"][-1])
            pool.dma_start(rope_q, d["rope_q"]).then_inc(swa_in, 16)
            pool.dma_start(swa_mask, d["swa_mask"]).then_inc(swa_in, 16)
            read_last(pool, r["ffn_down", 0][-1], 2)
            pool.dma_start(rope_r, d["rope_r"]).then_inc(ret_in, 16)
            pool.dma_start(decay_r, d["decay_r"]).then_inc(ret_in, 16)

        @block.tensor
        def _(pe):
            made = [0]
            tile_no = [0]

            def fill(p, it=None):
                for b, v in p.after:
                    pe.wait_ge(bank_free[b], plus(v, p.free_step, it))

            def finish(p, ins):
                assert p.order == made[0], (p.order, made[0])
                made[0] += 1
                ins.then_inc(done, 1)

            def weights(name, i, it=None):
                n = START[name] + i
                assert n == tile_no[0], (name, i, n, tile_no[0])
                tile_no[0] += 1
                pe.wait_ge(landed[n % RING], plus(16 * (n // RING + 1), 16, it))
                return ring[:, n % RING, :]

            def begin(ins):
                ins.then_inc(begun, 1)

            def linear(w, acts, products, pieces, before=None, it=None, tile_first=True):
                kt = w.shape[1]
                for j, (p, (at, n)) in enumerate(zip(products, pieces)):
                    fill(p, it)
                    for k in range(kt):
                        if before is not None and j == 0:
                            before(k)
                        m = pe.matmul(bank(p, n), w[:, k, :], acts[:, k, at:at + n], start=(k == 0), stop=(k == kt - 1))
                        if tile_first and j == 0 and k == 0:
                            begin(m)
                    finish(p, m)

            def k8(w):
                return w.rearrange("p (k m) -> p k m", k=KT)

            def mean_square(sq, products, pieces, base, it=None):
                for j, (p, (at, n)) in enumerate(zip(products, pieces)):
                    fill(p, it)
                    for k in range(KT):
                        if j == 0:
                            pe.wait_ge(squares, base + k + 1)
                        m = pe.matmul(bank(p, n), ones, sq[:, k, at:at + n], start=(k == 0), stop=(k == KT - 1))
                    finish(p, m)

            def filters():
                pe.wait_ge(filter_in, 16)
                p = r["f_h1"]
                fill(p)
                finish(p, pe.matmul(bank(p)[0:64], fil("w1")[0:33], fil("z")[0:33], start=True, stop=True))
                p = r["f_h2"]
                fill(p)
                pe.wait_ge(sin_ready, 1)
                finish(p, pe.matmul(bank(p)[0:64], fil("w2")[0:64], sin1[0:64], start=True, stop=True))
                pe.wait_ge(sin_ready, 2)
                pe.wait_ge(eps_set, 1)
                for i, p in enumerate(r["f_h3"]):
                    tt, half = i // 2, i % 2
                    fill(p)
                    finish(p, pe.matmul(bank(p), sin2[0:65, tt * P:(tt + 1) * P],
                                        fil("w3")[0:65, half * 512:(half + 1) * 512], start=True, stop=True))
                p = r["f_norm"]
                fill(p)
                pe.wait_ge(filter_sq, ST)
                pe.wait_ge(const_in, 16)
                for o in range(2):
                    for c in range(2):
                        for i in range(2 * ST):
                            m = pe.matmul(ps[:, p.bank, 2 * o + c:2 * o + c + 1], f_sq[:, i // 2, o, i % 2, c * P:(c + 1) * P],
                                          ones[:, 0:1], start=(i == 0), stop=(i == 2 * ST - 1))
                finish(p, m)
                pe.wait_ge(spec_in, 1)
                for kt in range(ST):
                    w = weights("dft", kt).rearrange("p (c t k) -> p c t k", c=2, t=ST)
                    for c in range(2):
                        p = r["f_spec"][2 * kt + c]
                        fill(p)
                        for tt in range(ST):
                            m = pe.matmul(bank(p), w[:, c, tt, :], filt[:, tt, :, 0, :] if c == 0 else diff[:, tt],
                                          start=(tt == 0), stop=(tt == ST - 1))
                            if c == 0 and tt == 0:
                                begin(m)
                        finish(p, m)

            def modulation():
                p = r["mod1"]
                fill(p)
                pe.wait_ge(silu_ready, 1)
                for i in range(16):
                    w = k8(weights("mod1", i))
                    for k in range(KT):
                        m = pe.matmul(ps[:, p.bank, 2 * i:2 * i + 2], w[:, k, :], silu_c[:, k, :], start=(k == 0), stop=(k == KT - 1))
                        if k == 0:
                            begin(m)
                finish(p, m)
                sq = mix[:, :, :]
                mean_square(sq, [r["ms_x"]], [(0, S)], 0)
                mean_square(sq, [r["ms_c"]], [(0, C)], KT)

            def hyena():
                for i in range(6):
                    w = k8(weights("hyena", i))
                    linear(w, h1, [r["hy"][i]], [(C, S)], before=(lambda k: pe.wait_ge(h_ready, KT + k + 1)) if i == 0 else None)
                pe.wait_ge(dft_in, 16)
                for o in range(2):
                    for tt in range(ST):
                        p = r["hy_t", o][tt]
                        fill(p)
                        for c in range(2):
                            if o == 0:
                                pe.wait_ge(conv_ready, c + 1)
                            else:
                                pe.wait_ge(z_ready, c + 1)
                            sig = hy[:, c] if o == 0 else z1[:, c]
                            m = pe.transpose(ps[:, p.bank, c * P:(c + 1) * P], sig[:, tt * P:(tt + 1) * P], ident)
                        finish(p, m)
                    for kt in range(ST):
                        p = r["hy_f", o][kt]
                        fill(p)
                        for c in range(2):
                            for tt in range(ST):
                                if kt == 0 and c == 0:
                                    read(pe, r["hy_t", o][tt])
                                m = pe.matmul(ps[:, p.bank, c * 256:(c + 1) * 256], dft[:, c, tt, kt * P:(kt + 1) * P],
                                              sig_t[:, tt], start=(tt == 0), stop=(tt == ST - 1))
                        finish(p, m)
                    for c in range(2):
                        p = r["hy_i", o][c]
                        fill(p)
                        for kt in range(ST):
                            if c == 0:
                                pe.wait_ge(spec_ready, ST * o + kt + 1)
                            for part in range(2):
                                m = pe.matmul(bank(p), spec[:, part, kt, c * P:(c + 1) * P], dft[:, part, kt, :],
                                              start=(kt == 0 and part == 0), stop=(kt == ST - 1 and part == 1))
                        finish(p, m)

            def projections():
                for i in range(2):
                    linear(k8(weights("mixers", i)), h1, [r["aq"][i]], [(C, S)])
                for i in range(2):
                    linear(k8(weights("mixers", 2 + i)), h1, r["ak"][2 * i:2 * i + 2], [(C, S), (0, C)])
                for i in range(4):
                    p = r["rope"][i]
                    fill(p)
                    read(pe, r["aq"][i] if i < 2 else r["ak"][2 * (i - 2)])
                    finish(p, pe.matmul(bank(p), con("swap_a"), raw_a[:, i], start=True, stop=True))
                for i in range(2):
                    linear(k8(weights("mixers", 4 + i)), h1, [r["bq"][i]], [(C, S)])
                for i in range(2):
                    linear(k8(weights("mixers", 6 + i)), h1, r["bk"][2 * i:2 * i + 2], [(C, S), (0, C)])
                for i in range(2):
                    linear(k8(weights("mixers", 8 + i)), h1, [r["pool"][i]], [(C, S)])
                w = [weights("values", j).rearrange("p (k n) -> p k n", k=2) for j in range(4)]
                for t in range(NKT):
                    token_major(r["v"][t], lambda k, t=t: h1[:, k, t * P:(t + 1) * P], w, P, t == NKT - 1)
                for i in range(2):
                    p = r["pool_w"][i]
                    fill(p)
                    pe.wait_ge(att_in, 64)
                    pe.wait_ge(pooled, i + 1)
                    finish(p, pe.matmul(bank(p), pool_w[:, i, :], pool_y[:, i], start=True, stop=True))

            def token_major(p, acts, w, n_tok, last, it=None):
                fill(p, it)
                for k in range(KT):
                    m = pe.matmul(ps[0:n_tok, p.bank, :], acts(k), w[k // 2][:, k % 2, :], start=(k == 0), stop=(k == KT - 1))
                    if last and k % 2 == 0:
                        begin(m)
                finish(p, m)

            def attentions():
                def scores(i):
                    kind, h, t = UNITS[i]
                    for c, p in enumerate(r["scores", i]):
                        fill(p)
                        if kind == "A":
                            o, n, q, k = 64 * (h % 2) + 32 * c, 32, aq, ak
                            if i == 0 and c == 0:
                                pe.wait_ge(roped, 4)
                                read(pe, r["ak"][3])
                                read(pe, r["ak"][1])
                        else:
                            o, n, q, k = 64 * (h % 2), 64, bq, bk
                        for at, width in ((0, 512), (512, 256)):
                            m = pe.matmul(wide(p, NKEY)[:, at:at + width], q[o:o + n, h // 2, t * P:(t + 1) * P],
                                          k[o:o + n, h // 2, at:at + width], start=True, stop=True)
                        finish(p, m)

                read(pe, r["bq"][1])
                for j in range(4):
                    read(pe, r["bk"][j])
                for j in range(NKT):
                    read(pe, r["v"][j])
                fill(r["mod2"])
                scores(0)
                for i, (kind, h, t) in enumerate(UNITS):
                    if i + 1 < len(UNITS):
                        scores(i + 1)
                    w = k8(weights("mod2", i))
                    b = r["mod2"].bank
                    for k in range(KT):
                        mod_m = pe.matmul(ps[:, b, i:i + 1], w[:, k, :], silu_c[:, k, 0:1], start=(k == 0), stop=(k == KT - 1))
                        if k == 0:
                            begin(mod_m)
                    if i == len(UNITS) - 1:
                        finish(r["mod2"], mod_m)
                    pe.wait_ge(prob_ready, i + 1)
                    for j, p in enumerate(r["T", i]):
                        fill(p)
                        for kt in range(4 * j, min(4 * j + 4, NKT)):
                            m = pe.transpose(ps[:, p.bank, (kt % 4) * P:(kt % 4 + 1) * P], prob[:, i % 2, 0, kt * P:(kt + 1) * P], ident)
                        finish(p, m)
                    p = r["PV", i]
                    fill(p)
                    o = DH * (h % 2)
                    for kt in range(NKT):
                        if kt % 4 == 0:
                            read(pe, r["T", i][kt // 4])
                        m = pe.matmul(ps[o:o + DH, p.bank, 0:P], vals[:, kt, 0 if kind == "A" else 1, h * DH:(h + 1) * DH],
                                      prob_t[:, i % 2, kt, :], start=(kt == 0), stop=(kt == NKT - 1))
                    finish(p, m)
                for c, p in enumerate(r["subln"]):
                    fill(p)
                    pe.wait_ge(sub_sq, 1)
                    finish(p, pe.matmul(bank(p), head_ones, prob_sq[:, c], start=True, stop=True))

            def first_out():
                for b, v in r["before_w_out"]:
                    pe.wait_ge(bank_free[b], v)
                pe.wait_ge(mixed, MIXED_1)
                for i in range(8):
                    linear(k8(weights("w_out", i)), mix[:, :, 0:S], [r["w_out"][i]], [(0, S)])

            def router():
                mean_square(mix[:, :, :], [r["ms_2"]], [(0, S)], 2 * KT)
                p = r["router"]
                fill(p)
                rw = par("router_w").rearrange("p (k e) -> p k e", k=KT)
                for tt in range(ST):
                    for k in range(KT):
                        if tt == 0:
                            pe.wait_ge(h_ready, 2 * KT + k + 1)
                        m = pe.matmul(ps[:, p.bank, tt * EXPERTS:(tt + 1) * EXPERTS], h2[:, k, tt * P:(tt + 1) * P], rw[:, k, :],
                                      start=(k == 0), stop=(k == KT - 1))
                finish(p, m)
                for i, p in enumerate(r["rows"]):
                    fill(p)
                    for k in range(4):
                        f, t = 4 * (i % 2) + k, i // 2
                        m = pe.transpose(ps[:, p.bank, k * P:(k + 1) * P], h2[:, f, t * P:(t + 1) * P], ident)
                    finish(p, m)
                ranks()

            def ranks():
                p = r["rank"]
                fill(p)
                pe.wait_ge(chosen, 1)
                for t in range(ST):
                    for u in range(t + 1):
                        pe.matmul(ps[:, p.bank, t * EXPERTS:(t + 1) * EXPERTS], con("earlier") if u == t else ones, rt[11][:, u, :],
                                  start=(u == 0), stop=(u == t))
                for u in range(ST):
                    m = pe.matmul(ps[:, p.bank, 64:64 + EXPERTS], ones, rt[11][:, u, :], start=(u == 0), stop=(u == ST - 1))
                finish(p, m)

            def experts():
                for b, v in r["before_jobs"]:
                    pe.wait_ge(bank_free[b], v)
                pe.wait_ge(jobs_ready, 1)
                n_jobs = pe.value_load(n_jobs_i[0:1, 0:1], min_val=MIN_JOBS, max_val=JOBS - 1)
                slots = [(START["ab"] + i) % RING for i in range(EXPERT_TILES)]

                def turn():
                    for k in range(KT):
                        m = pe.transpose(ps[:, 2 + k // 4, (k % 4) * P:(k % 4 + 1) * P], job_in[:, k * P:(k + 1) * P], ident)
                        if k % 4 == 3:
                            m.then_inc(e_done, 1)

                pe.wait_ge(job_read, 16)
                turn()
                with pe.Fori(0, n_jobs) as it:
                    pe.wait_ge(job_turned, it * 2 + 2)
                    for side in range(2):
                        for m_ in range(4):
                            s = slots[4 * side + m_]
                            pe.wait_ge(e_landed[s], it * 16 + 16)
                            w = k8(ring[:, s, :])
                            for k in range(KT):
                                m = pe.matmul(ps[:, side, m_ * P:(m_ + 1) * P], w[:, k, :], job_t[:, k, :],
                                              start=(k == 0), stop=(k == KT - 1))
                                if k == 0:
                                    m.then_inc(e_begun, 1)
                        m.then_inc(e_done, 1)
                    pe.wait_ge(job_read, it * 16 + 32)
                    turn()
                    pe.wait_ge(hid_ready, it + 1)
                    for k in range(4):
                        s = slots[8 + k]
                        pe.wait_ge(e_landed[s], it * 16 + 16)
                        for half in range(2):
                            m = pe.matmul(ps[:, 4 + half, :], hid[:, k, :], ring[:, s, half * 512:(half + 1) * 512],
                                          start=(k == 0), stop=(k == 3))
                            if half == 0:
                                m.then_inc(e_begun, 1)
                    m.then_inc(e_done, 1)
                for k in range(KT):
                    p = r["moe_out"][k]
                    if k == 0:
                        pe.wait_ge(combined, ST)
                    for t in range(ST):
                        m = pe.transpose(ps[:, p.bank, t * P:(t + 1) * P], both[:, t, k * P:(k + 1) * P], ident)
                    finish(p, m)

            def ab_in():
                mean_square(mix[:, :, :], [r["ms_f"]], [(0, S)], 3 * KT)
                mean_square(mix[:, :, :], r["ms_ab"], HALVES2, 4 * KT)
                for i in range(13):
                    linear(k8(weights("ab", i)), h2, r["ab"][2 * i:2 * i + 2], HALVES2,
                           before=(lambda k: pe.wait_ge(h_ready, 3 * KT + k + 1)) if i == 0 else None)
                w = k8(weights("ab_values", 0))
                for t, p in enumerate(r["ab_v"]):
                    at, n = swa_queries(t)
                    fill(p)
                    for k in range(KT):
                        m = pe.matmul(ps[0:n, p.bank, 0:P], h2[:, k, at:at + n], w[:, k, :], start=(k == 0), stop=(k == KT - 1))
                        if t == 0 and k == 0:
                            begin(m)
                    finish(p, m)

            def lru():
                w = weights("lru_gates", 0).rearrange("p (i g m) -> p i g m", i=4, g=2)
                for i in range(4):
                    pe.wait_ge(xc_ready, i + 1)
                    for g in range(2):
                        for j, (at, n) in enumerate(HALVES2):
                            p = r["lru"][4 * i + 2 * g + j]
                            fill(p)
                            m = pe.matmul(bank(p, n), w[:, i, g, :], xc[:, i, at:at + n], start=True, stop=True)
                            finish(p, m)

            def swa():
                for i in range(5):
                    pe.wait_ge(qk_sqr, i + 1)
                    for j, (at, n) in enumerate(HALVES2):
                        p = r["qk_ms"][2 * i + j]
                        fill(p)
                        finish(p, pe.matmul(bank(p, n), head_ones, qk_sq[:, i, at:at + n], start=True, stop=True))
                for i in range(5):
                    pe.wait_ge(qk_n, i + 1)
                    for j, (at, n) in enumerate(HALVES2):
                        p = r["qk_sw"][2 * i + j]
                        fill(p)
                        finish(p, pe.matmul(bank(p, n), con("swap_q"), qk[:, i, at:at + n], start=True, stop=True))
                for b, v in r["before_swa"]:
                    pe.wait_ge(bank_free[b], v)
                pe.wait_ge(qk_rot, 5)

                def scores(i):
                    t, a = GROUPS[i]
                    q0, nq = swa_queries(t)
                    p = r["swa_s", i]
                    fill(p)
                    for hh in range(4):
                        j, kv = 2 * a + hh // 2, hh % 2
                        o = DH * kv
                        for col, key, n in swa_keys(t):
                            m = pe.matmul(ps[0:nq, hh, col:col + n], qk[o:o + DH, j, q0:q0 + nq], qk[o:o + DH, 4, key:key + n],
                                          start=True, stop=True)
                    finish(p, m)

                scores(0)
                for i, (t, a) in enumerate(GROUPS):
                    if i + 1 < len(GROUPS):
                        scores(i + 1)
                    q0, nq = swa_queries(t)
                    pe.wait_ge(swa_prob, i + 1)
                    for hh, p in enumerate(r["swa_t", i]):
                        fill(p)
                        for c, (col, n, _) in enumerate(swa_chunks(t)):
                            m = pe.transpose(ps[0:n, p.bank, c * P:c * P + nq], prob2[0:nq, i % 2, hh, col:col + n], ident[0:nq, 0:nq])
                        finish(p, m)
                    p = r["swa_o", i]
                    fill(p)
                    chunks = swa_chunks(t)
                    for hh in range(4):
                        if hh < 2:
                            read(pe, r["swa_t", i][2 + hh])
                        o = DH * (hh % 2)
                        for c, (col, n, vt) in enumerate(chunks):
                            m = pe.matmul(ps[o:o + DH, p.bank, (hh // 2) * P:(hh // 2) * P + nq], val2[0:n, vt, o:o + DH],
                                          prob2_t[0:n, i % 2, hh, c * P:c * P + nq], start=(c == 0), stop=(c == len(chunks) - 1))
                    finish(p, m)

            def ab_out():
                for b, v in r["before_ab_out"]:
                    pe.wait_ge(bank_free[b], v)
                pe.wait_ge(mixed, MIXED_2)
                for i in range(8):
                    w = k8(weights("ab_out", i))
                    linear(w, mix[:, :, :], r["ab_out"][2 * i:2 * i + 2], HALVES2, tile_first=True)

            def ffn(n):
                pieces = HALVES2 if n == 0 else [(0, S)]
                np_ = len(pieces)
                name = f"ffn{n}"
                base = (5 if n == 0 else 7) * KT
                mean_square(mix[:, :, :], r["ffn_ms", n], pieces, base)
                for b, v in r["before_ffn", n]:
                    pe.wait_ge(bank_free[b], v)
                for k in range(KT):
                    pe.wait_ge(h_ready, (4 if n == 0 else 6) * KT + k + 1)
                with pe.Fori(0, 3) as it:
                    for i in range(12):
                        linear(k8(weights(name, i, it)), h2, r["ffn_loop", n][np_ * i:np_ * (i + 1)], pieces, it=it)
                made[0] += 12 * np_ * 2
                tile_no[0] += 24
                for i in range(8):
                    linear(k8(weights(name, 36 + i)), h2, r["ffn_rest", n][np_ * i:np_ * (i + 1)], pieces)
                for b, v in r["before_down", n]:
                    pe.wait_ge(bank_free[b], v)
                with pe.Fori(0, 2) as it:
                    for m_ in range(4):
                        w = [k8(weights(name, 44 + 3 * m_ + s, it)) for s in range(3)]
                        for j, (at, n_) in enumerate(pieces):
                            p = r["ffn_down", n][np_ * m_ + j]
                            fill(p, it)
                            for k in range(FFT):
                                m = pe.matmul(bank(p, n_), w[k // 8][:, k % 8, :], act_w[:, k, at:at + n_],
                                              start=(k == 0), stop=(k == FFT - 1))
                                if j == np_ - 1 and k % 8 == 0:
                                    begin(m)
                            finish(p, m)
                made[0] += 4 * np_
                tile_no[0] += 12

            def retention():
                mean_square(mix[:, :, :], r["ms_ret"], HALVES2, 6 * KT)
                for b, v in r["before_ret"]:
                    pe.wait_ge(bank_free[b], v)
                for k in range(KT):
                    pe.wait_ge(h_ready, 5 * KT + k + 1)
                with pe.Fori(0, RET_HEADS) as it:
                    for i in range(2):
                        linear(k8(weights("ret", i, it)), h2, [r["ret", "q"][i]], [(META, S)], it=it)
                    for i in range(2):
                        linear(k8(weights("ret", 2 + i, it)), h2, r["ret", "k"][2 * i:2 * i + 2], HALVES2, it=it)
                    w = [weights("ret", 4 + j, it).rearrange("p (k n) -> p k n", k=2) for j in range(4)]
                    for t, p in enumerate(r["ret", "v"]):
                        n = P if t < 4 else META
                        token_major(p, lambda k, t=t, n=n: h2[:, k, t * P:t * P + n], w, n, t == 4, it)
                    for i in range(4):
                        linear(k8(weights("ret", 8 + i, it)), h2, [r["ret", "g"][i]], [(META, S)], it=it)
                    pe.wait_ge(ret_qk, it + 1)
                    for t, p in enumerate(r["ret", "s"]):
                        n = P if t < 4 else META
                        at = max(P * t - META, 0)
                        fill(p, it)
                        for c in range(2):
                            m = pe.matmul(ps[0:n, p.bank, at:S], ret_k[:, c, t * P:t * P + n], ret_q[:, c, at:S],
                                          start=(c == 0), stop=(c == 1))
                        finish(p, m)
                    assert r["ret", "o"][0].bank == r["ret", "s"][0].bank == r["ret", "v"][4].bank
                    for i, p in enumerate(r["ret", "o"]):
                        fill(p, it)
                        for t in range(5):
                            n = P if t < 4 else META
                            at = max(P * t - META, 0)
                            if i == 0 and t > 0:
                                read(pe, r["ret", "s"][t], it)
                            m = pe.matmul(ps[:, p.bank, at:S], ret_v[0:n, t, i * P:(i + 1) * P], ret_s[0:n, t, at:S],
                                          start=(t == 0), stop=(t == 4), skip_group_check=True)
                        finish(p, m)
                    p, = r["ret", "ms"]
                    fill(p, it)
                    for i in range(4):
                        pe.wait_ge(ret_sqr, it * 4 + i + 1)
                        m = pe.matmul(bank(p), ones, ret_sq[:, i], start=(i == 0), stop=(i == 3))
                    finish(p, m)
                made[0] += 25 * (RET_HEADS - 1)
                tile_no[0] += 12 * (RET_HEADS - 1)

            def ret_out():
                pe.wait_ge(ret_yr, RET_HEADS)
                for i in range(8):
                    w = [k8(weights("ret_out", 2 * i + s)) for s in range(2)]
                    p = r["ret_out"][i]
                    fill(p)
                    for k in range(16):
                        m = pe.matmul(bank(p), w[k // 8][:, k % 8, :], ret_y[:, k], start=(k == 0), stop=(k == 15))
                        if k % 8 == 0:
                            begin(m)
                    finish(p, m)

            filters()
            modulation()
            hyena()
            projections()
            attentions()
            first_out()
            router()
            experts()
            ab_in()
            lru()
            swa()
            ab_out()
            ffn(0)
            retention()
            ret_out()
            ffn(1)

        @block.scalar
        def _(act):
            me = Steps(act, act_step)

            def squares_of(src, dst, n, wait_first=None):
                for k in range(KT):
                    act.activation(dst[:, k, 0:n], src[:, k], ACT.Square).then_inc(squares, 1)

            def root(p_list, pieces, scale, out, sem_, it=None):
                for p, (at, n) in zip(p_list, pieces):
                    ready(act, p, it)
                    act.activation(out[:, at:at + n], bank(p, n), ACT.Ln, bias=eps, scale=scale).then_inc(bank_free[p.bank], 1)
                for p, (at, n) in zip(p_list, pieces):
                    read(act, p, it)
                    act.activation(out[:, at:at + n], out[:, at:at + n], ACT.Exp, scale=-0.5).then_inc(sem_, 1)

            def copy(p, out, src, scale=1.0, it=None):
                ready(act, p, it)
                act.activation(out, src, ACT.Copy, scale=scale).then_inc(bank_free[p.bank], 1)

            def filters():
                act.wait_ge(small_in, 16)
                act.activation(silu_c, par("c").rearrange("p (k v) -> p k v", k=KT), ACT.Silu).then_inc(silu_ready, 1)
                for i, out in enumerate((sin1, sin2)):
                    act.wait_ge(sin_arg, i + 1)
                    act.activation(out[0:64], arg[0:64, 0], ACT.Sin).then_inc(sin_ready, 1)
                for tt in range(ST):
                    read(act, r["f_h3"][2 * tt])
                    read(act, r["f_h3"][2 * tt + 1])
                    act.activation(f_sq[:, tt], filt[:, tt], ACT.Square).then_inc(filter_sq, 1)
                p = r["f_norm"]
                ready(act, p)
                act.wait_ge(eps_set, 1)
                act.activation(conv_rs, ps[:, p.bank, 0:4], ACT.Ln, bias=eps).then_inc(bank_free[p.bank], 1)
                read(act, p)
                act.activation(conv_rs, conv_rs, ACT.Exp, scale=-0.5).then_inc(filter_rs, 1)
                for i, p in enumerate(r["f_spec"]):
                    copy(p, (kc, ks)[i % 2][:, i // 2], bank(p).rearrange("p (o c) -> p o c", o=2), scale=1.0 / S)

            def modulation():
                act.wait_ge(x_in, 32)
                squares_of(x[:, :, META:T2], mix, S)
                act.wait_ge(ctx_in, 16)
                ready(act, r["ms_x"])
                squares_of(ctx_raw, mix, C)
                root([r["ms_x"]], [(0, S)], 1.0 / D, rstd, rstd_ready)
                root([r["ms_c"]], [(0, C)], 1.0 / D, rstd[:, T2:T2 + C], rstd_ready)
                act.wait_ge(mod1_ready, 1)
                for j, k in enumerate([7, 6, 5, 4, 3, 2, 1, 0]):
                    act.wait_ge(scaled, KT)
                    act.activation(h1[:, k, 0:C], h1[:, k, 0:C], ACT.Identity, bias=mod1[:, k, 1:2]).then_inc(h_ready, 1)
                for k in range(KT):
                    act.wait_ge(scaled, KT + k + 1)
                    act.activation(h1[:, k, C:], h1[:, k, C:], ACT.Identity, bias=mod1[:, k, 0:1]).then_inc(h_ready, 1)

            def hyena():
                for i in range(6):
                    copy(r["hy"][i], hy_raw[:, i, 1:S + 1], bank(r["hy"][i]))
                for o in range(2):
                    for tt, p in enumerate(r["hy_t", o]):
                        if o == 0 and tt == 0:
                            act.wait_ge(conv_ready, 6)
                        copy(p, sig_t[:, tt], bank(p, 256))

            def projections():
                scale = 32 ** -0.5
                act.wait_ge(mixed, 2)
                for i in range(2):
                    copy(r["aq"][i], raw_a[:, i], bank(r["aq"][i]), scale)
                for i in range(2):
                    copy(r["ak"][2 * i], raw_a[:, 2 + i], bank(r["ak"][2 * i]))
                    copy(r["ak"][2 * i + 1], ak[:, i, 0:C], bank(r["ak"][2 * i + 1], C))
                for i in range(2):
                    copy(r["bq"][i], bq[:, i], bank(r["bq"][i]), DH ** -0.5)
                for i in range(2):
                    copy(r["bk"][2 * i], bk[:, i, C:], bank(r["bk"][2 * i]))
                    copy(r["bk"][2 * i + 1], bk[:, i, 0:C], bank(r["bk"][2 * i + 1], C))
                for i in range(2):
                    copy(r["pool"][i], pool_u[:, i, 8:8 + S], bank(r["pool"][i]))
                for t in range(NKT):
                    copy(r["v"][t], vals[:, t], bank(r["v"][t]).rearrange("p (a c) -> p a c", a=2))

            def attentions():
                act.wait_ge(lam_arg, 1)
                act.activation(lam_t[:, 66:68], lam_t[:, 64:66], ACT.Exp).then_inc(lam_exp, 1)
                unit = [0]

                def exps(i):
                    for c, p in enumerate(r["scores", i]):
                        unit[0] += 1
                        act.wait_ge(max_ready, unit[0])
                        act.activation(prob[:, i % 2, c], wide(p, NKEY), ACT.Exp, bias=neg_max[:, i % 2, c:c + 1],
                                       accum_out=row_sum[:, i % 2, c:c + 1]).then_inc(bank_free[p.bank], 1)

                exps(0)
                for i in range(len(UNITS)):
                    if i + 1 < len(UNITS):
                        exps(i + 1)
                    for j, p in enumerate(r["T", i]):
                        n = 4 if j == 0 else 2
                        copy(p, prob_t[:, i % 2, 4 * j:4 * j + n], bank(p, n * P).rearrange("p (k q) -> p k q", k=n))
                read(act, r["PV", HEADS * ST - 1])
                act.activation(prob_sq, o_a, ACT.Square).then_inc(sub_sq, 1)
                root(r["subln"], [(0, S), (S, S)], 1.0 / DH, sub_rs_t, sub_rs)

            def router():
                read(act, r["w_out"][-1])
                squares_of(x[:, :, META:T2], mix, S)
                root([r["ms_2"]], [(0, S)], 1.0 / D, rstd, rstd_ready)
                act.wait_ge(mod2_ready, 1)
                for k in range(KT):
                    act.wait_ge(scaled, 2 * KT + k + 1)
                    act.activation(h2[:, k, 0:S], h2[:, k, 0:S], ACT.Identity, bias=mod2[:, 8 + k:9 + k]).then_inc(h_ready, 1)
                read(act, r["router"])
                act.activation(rt[1], rt[0], ACT.Exp).then_inc(route_exp, 1)
                for i, p in enumerate(r["rows"]):
                    copy(p, rows[:, i // 2, (i % 2) * 512:(i % 2 + 1) * 512], bank(p))

            def experts():
                act.wait_ge(jobs_ready, 1)
                n_jobs = act.value_load(n_jobs_i[0:1, 0:1], min_val=MIN_JOBS, max_val=JOBS - 1)

                def turned(at, it):
                    for h in range(2):
                        act.wait_ge(e_done, plus(at + h, 5, it))
                        act.activation(job_t[:, 4 * h:4 * h + 4], ps[:, 2 + h, :].rearrange("p (k t) -> p k t", k=4), ACT.Copy)\
                           .then_inc(job_turned, 1)

                turned(1, None)
                with act.Fori(0, n_jobs) as it:
                    act.wait_ge(e_done, it * 5 + 3)
                    act.activation(silu_t, ps[:, 0, :], ACT.Silu).then_inc(silu_out, 1)
                    turned(5, it)
                    act.wait_ge(e_done, it * 5 + 7)
                    for h in range(2):
                        act.activation(job_out[:, h], ps[:, 4 + h, :], ACT.Copy).then_inc(y_ready, 1)

            def ab_in():
                read(act, r["moe_out"][-1])
                squares_of(x[:, :, META:T2], mix, S)
                root([r["ms_f"]], [(0, S)], 1.0 / D, rstd, rstd_ready)
                act.wait_ge(x_normed, KT)
                squares_of(x[:, :, :], mix, T2)
                root(r["ms_ab"], HALVES2, 1.0 / D, rstd, rstd_ready)
                for i in range(13):
                    for j, (at, n) in enumerate(HALVES2):
                        p = r["ab"][2 * i + j]
                        if i < 4:
                            copy(p, xr[:, i, 3 + at:3 + at + n], bank(p, n))
                        elif i < 8:
                            ready(act, p)
                            act.activation(gate[:, i - 4, at:at + n], bank(p, n), ACT.Gelu_apprx_tanh).then_inc(bank_free[p.bank], 1)
                        else:
                            copy(p, qk[:, i - 8, at:at + n], bank(p, n))
                for t, p in enumerate(r["ab_v"]):
                    n = swa_queries(t)[1]
                    copy(p, val2[0:n, t], ps[0:n, p.bank, 0:P])

            def lru():
                act.wait_ge(lru_y, 1)
                act.activation(lru_t[:, 4:8], lru_t[:, 0:4], ACT.Exp, scale=-1.0).then_inc(lru_e, 1)
                for i in range(4):
                    for g, (out, b) in enumerate(((g_r, "b_a"), (g_i, "b_i"))):
                        for j, (at, n) in enumerate(HALVES2):
                            p = r["lru"][4 * i + 2 * g + j]
                            ready(act, p)
                            act.activation(out[:, i, at:at + n], bank(p, n), ACT.Sigmoid, bias=par(b)[:, i:i + 1])\
                               .then_inc(bank_free[p.bank], 1)
                for p in r["lru"][-8:]:
                    read(act, p)
                act.wait_ge(lru_cr, 1)
                for i in range(4):
                    act.activation(g_a[:, i], g_r[:, i], ACT.Exp, scale=lru_c[:, i:i + 1]).then_inc(lru_act, 1)
                for i in range(4):
                    act.activation(g_r[:, i], g_r[:, i], ACT.Tanh, scale=lru_c[:, i:i + 1]).then_inc(lru_act, 1)
                for i in range(4):
                    act.wait_ge(lru_m, i + 1)
                    act.activation(g_m[:, i], g_m[:, i], ACT.Sqrt, scale=-1.0).then_inc(lru_s, 1)

            def swa():
                act.wait_ge(mixed, MIXED_2)
                for i in range(5):
                    act.activation(qk_sq[:, i], qk[:, i], ACT.Square).then_inc(qk_sqr, 1)
                for i in range(5):
                    root(r["qk_ms"][2 * i:2 * i + 2], HALVES2, 1.0 / DH, qk_rs[:, i], qk_rsr)
                for i, (t, a) in enumerate(GROUPS):
                    if i == 0:
                        swa_exps(0)
                    if i + 1 < len(GROUPS):
                        swa_exps(i + 1)
                    nq = swa_queries(t)[1]
                    n = len(swa_chunks(t))
                    for hh, p in enumerate(r["swa_t", i]):
                        ready(act, p)
                        to = prob2_t[:, i % 2, hh, :].rearrange("p (c q) -> p c q", c=3)
                        of = ps[:, p.bank, 0:384].rearrange("p (c q) -> p c q", c=3)
                        last = act.activation(to[0:META, 0, 0:nq], of[0:META, 0, 0:nq], ACT.Copy)
                        if n > 1:
                            last = act.activation(to[:, 1:n, 0:nq], of[:, 1:n, 0:nq], ACT.Copy)
                        last.then_inc(bank_free[p.bank], 1)

            def swa_exps(i):
                t, a = GROUPS[i]
                nq, (col, _, n) = swa_queries(t)[1], swa_keys(t)[-1]
                p = r["swa_s", i]
                act.wait_ge(swa_max, i + 1)
                act.activation(sink_e[0:nq, i % 2], sink_d[0:nq, i % 2], ACT.Exp).then_inc(swa_exp, 1)
                for hh in range(4):
                    ins = act.activation(prob2[0:nq, i % 2, hh, 0:col + n], ps[0:nq, hh, 0:col + n], ACT.Exp,
                                         bias=neg_max[0:nq, i % 2, hh:hh + 1], accum_out=row_sum[0:nq, i % 2, hh:hh + 1])
                ins.then_inc(bank_free[p.bank], 1)

            def ffn(n):
                t0, pieces = (0, HALVES2) if n == 0 else (META, [(0, S)])
                np_ = len(pieces)
                last = r["ab_out"][-1] if n == 0 else r["ret_out"][-1]
                read(act, last)
                width = T2 if n == 0 else S
                squares_of(x[:, :, t0:T2], mix, width)
                root(r["ffn_ms", n], pieces, 1.0 / D, rstd, rstd_ready)
                with act.Fori(0, 3) as it:
                    for i in range(6):
                        for j, (at, w) in enumerate(pieces):
                            p = r["ffn_loop", n][np_ * 2 * i + j]
                            ready(act, p, it)
                            act.activation(silu_w[:, i, at:at + w], bank(p, w), ACT.Silu).then_inc(bank_free[p.bank], 1)
                for i in range(4):
                    for j, (at, w) in enumerate(pieces):
                        p = r["ffn_rest", n][np_ * 2 * i + j]
                        ready(act, p)
                        act.activation(silu_w[:, i, at:at + w], bank(p, w), ACT.Silu).then_inc(bank_free[p.bank], 1)

            def retention():
                read_last(act, r["ffn_down", 0][-1], 2)
                squares_of(x[:, :, :], mix, T2)
                root(r["ms_ret"], HALVES2, 1.0 / D, rstd, rstd_ready)
                with act.Fori(0, RET_HEADS) as it:
                    for t, p in enumerate(r["ret", "v"]):
                        n = P if t < 4 else META
                        copy(p, ret_v[0:n, t], ps[0:n, p.bank, :], it=it)
                    for i, p in enumerate(r["ret", "g"]):
                        ready(act, p, it)
                        act.activation(ret_g[:, i], bank(p), ACT.Silu).then_inc(bank_free[p.bank], 1)
                    for i, p in enumerate(r["ret", "o"]):
                        copy(p, ret_o[:, i], bank(p), it=it)
                        read(act, p, it)
                        act.activation(ret_sq[:, i], ret_o[:, i], ACT.Square).then_inc(ret_sqr, 1)
                    p, = r["ret", "ms"]
                    ready(act, p, it)
                    act.activation(rstd[:, 0:S], bank(p), ACT.Ln, bias=eps, scale=1.0 / 512).then_inc(bank_free[p.bank], 1)
                    read(act, p, it)
                    act.activation(rstd[:, 0:S], rstd[:, 0:S], ACT.Exp, scale=-0.5).then_inc(ret_rs, 1)

            filters()
            modulation()
            hyena()
            projections()
            attentions()
            router()
            experts()
            ab_in()
            lru()
            swa()
            ffn(0)
            retention()
            ffn(1)

        @block.vector
        def _(dve):
            me = Steps(dve, dve_step)
            link = me.link
            tt_ = dve.tensor_tensor
            ts = dve.tensor_scalar
            stt = dve.scalar_tensor_tensor

            def norm(gain, src, dst, n, rs, sem_, count):
                dve.wait_ge(rstd_ready, count)
                for k in range(KT):
                    stt(dst[:, k, 0:n], src[:, k, 0:n], gain[:, k:k + 1], rs, ALU.mult, ALU.mult).then_inc(sem_, 1)

            def filters():
                dve.memset(eps, EPS)
                dve.memset(sin2[64:65], 1.0).then_inc(eps_set, 1)
                dve.wait_ge(small_in, 16)
                for i, p in enumerate((r["f_h1"], r["f_h2"])):
                    b = par(("f_b1", "f_b2")[i])
                    a, n, t = (arg[0:64, j] for j in range(3))
                    ready(dve, p)
                    if i == 1:
                        dve.wait_ge(sin_ready, 1)
                    ts(a, bank(p)[0:64], b[0:64], None, ALU.add).then_inc(bank_free[p.bank], 1)
                    read(dve, p)
                    link(ts(n, a, 1.0 / (2 * math.pi), ROUND, ALU.mult, ALU.add))
                    link(ts(n, n, ROUND, None, ALU.subtract))
                    link(stt(t, n, -TWO_PI_HI, a, ALU.mult, ALU.add))
                    link(stt(t, n, -TWO_PI_LO, t, ALU.mult, ALU.add))
                    ts(a, t, PI_BELOW, -PI_BELOW, ALU.min, ALU.max).then_inc(sin_arg, 1)
                decay = fil("decay").rearrange("p (t c) -> p t c", t=ST)
                for i, p in enumerate(r["f_h3"]):
                    tt, o = i // 2, i % 2
                    ready(dve, p)
                    tt_(filt[:, tt, o], bank(p).rearrange("p (d c) -> p d c", d=2), bcast(decay[:, tt], 1, 2), ALU.mult)\
                        .then_inc(bank_free[p.bank], 1)
                dve.wait_ge(filter_sq, ST)
                link(dve.memset(filt[0:1, 0, :, 1, :], 0.0))
                for tt in range(ST):
                    ins = tt_(diff[:, tt], filt[:, tt, :, 0, :], filt[:, tt, :, 1, :], ALU.subtract)
                link(ins)
                for tt in range(ST):
                    ins = tt_(filt[:, tt, :, 0, :], filt[:, tt, :, 0, :], filt[:, tt, :, 1, :], ALU.add)
                ins.then_inc(spec_in, 1)

            def modulation():
                p = r["mod1"]
                ready(dve, p)
                tt_(mod1, ps[:, p.bank, 0:32].rearrange("p (m v) -> p m v", m=16), bcast(par("ada_b")[:, 0:16], 2, 2), ALU.add)\
                    .then_inc(bank_free[p.bank], 1)
                read(dve, p)
                stt(gain1, mod1[:, 8:16], 1.0, bcast(par("norm1_g"), 2, 2), ALU.add, ALU.mult).then_inc(mod1_ready, 1)
                dve.wait_ge(mod1_ready, 1)
                dve.wait_ge(rstd_ready, 2)
                for j, k in enumerate(range(KT - 1, -1, -1)):
                    stt(h1[:, k, 0:C], ctx_raw[:, k], gain1[:, k, 1:2], rstd[:, T2:T2 + C], ALU.mult, ALU.mult).then_inc(scaled, 1)
                    dve.wait_ge(scaled, j + 1)
                norm(gain1[:, :, 0], x[:, :, META:T2], h1[:, :, C:], S, rstd[:, 0:S], scaled, 2)

            def hyena():
                sw = par("short_w").rearrange("p (i j) -> p i j", i=6)
                sbias = par("short_b")
                ready(dve, r["hy"][0])
                for i in range(6):
                    dve.memset(hy_raw[:, i, 0:1], 0.0)
                    ins = dve.memset(hy_raw[:, i, S + 1:S + 2], 0.0)
                link(ins)
                for i in range(6):
                    c = (i + 4) % 6
                    read(dve, r["hy"][i])
                    out = hy[:, i]
                    link(ts(out, hy_raw[:, i, 1:S + 1], sw[:, c, 1:2], sbias[:, c:c + 1], ALU.mult, ALU.add))
                    link(stt(out, hy_raw[:, i, 0:S], sw[:, c, 0:1], out, ALU.mult, ALU.add))
                    stt(out, hy_raw[:, i, 2:S + 2], sw[:, c, 2:3], out, ALU.mult, ALU.add).then_inc(conv_ready, 1)
                dve.wait_ge(conv_ready, 6)
                dve.wait_ge(filter_rs, 1)
                skip = par("skip").rearrange("p (o c) -> p o c", o=2)
                for q in r["f_spec"]:
                    read(dve, q)
                for o in range(2):
                    for kt, p in enumerate(r["hy_f", o]):
                        ready(dve, p)
                        u = ps[:, p.bank, :].rearrange("p (s c) -> p s c", s=2)
                        tt_(prod_t[:, 0], u, bcast(kc[:, kt, o], 1, 2), ALU.mult)
                        tt_(prod_t[:, 1], u, bcast(ks[:, kt, o], 1, 2), ALU.mult).then_inc(bank_free[p.bank], 1)
                        read(dve, p)
                        tt_(spec[:, 0, kt], prod_t[:, 0, 0], prod_t[:, 1, 1], ALU.subtract)
                        tt_(spec[:, 1, kt], prod_t[:, 0, 1], prod_t[:, 1, 0], ALU.add).then_inc(spec_ready, 1)
                        dve.wait_ge(spec_ready, ST * o + kt + 1)
                    for c, p in enumerate(r["hy_i", o]):
                        sig = hy[:, c] if o == 0 else z1[:, c]
                        ready(dve, p)
                        ts(y_t, bank(p), conv_rs[:, 2 * o + c:2 * o + c + 1], None, ALU.mult).then_inc(bank_free[p.bank], 1)
                        read(dve, p)
                        link(stt(y_t, sig, skip[:, o, c:c + 1], y_t, ALU.mult, ALU.add))
                        out = z1[:, c] if o == 0 else mix[:, 6 + c, 0:S]
                        tt_(out, y_t, hy[:, 2 + 2 * o + c], ALU.mult).then_inc(z_ready if o == 0 else mixed, 1)
                        dve.wait_ge(z_ready if o == 0 else mixed, c + 1)

            def projections():
                dve.wait_ge(mixed, 2)
                dve.wait_ge(att_in, 64)
                dve.memset(pool_u[:, :, 0:8], 0.0)
                link(dve.memset(pool_u[:, :, S + 8:S + 16], 0.0))
                for i in range(4):
                    p = r["rope"][i]
                    to = aq[:, i] if i < 2 else ak[:, i - 2, C:]
                    read(dve, r["aq"][i] if i < 2 else r["ak"][2 * (i - 2)])
                    ready(dve, p)
                    tt_(y_t, bank(p), rope_a[:, 1], ALU.mult).then_inc(bank_free[p.bank], 1)
                    link(tt_(to, raw_a[:, i], rope_a[:, 0], ALU.mult))
                    tt_(to, to, y_t, ALU.add).then_inc(roped, 1)
                    dve.wait_ge(roped, i + 1)
                for i in range(2):
                    read(dve, r["pool"][i])
                src = pool_u
                for j, w in enumerate((2, 4, 8, 16)):
                    n = S + 16 - w + 1
                    link(tt_(pool_s[j][:, :, 0:n], src[:, :, 0:n], src[:, :, w // 2:w // 2 + n], ALU.add))
                    src = pool_s[j]
                for i in range(2):
                    for g in range(2):
                        w = 2 << (2 * i + g)
                        o = DH * g
                        mean = pool_s[2 * i + g][o:o + DH, i, 8 - w // 2:8 - w // 2 + S]
                        link(tt_(mean, mean, pool_inv[o:o + DH, i], ALU.mult))
                        ins = tt_(pool_y[o:o + DH, i], mean, pool_u[o:o + DH, i, 8:8 + S], ALU.subtract)
                    ins.then_inc(pooled, 1)
                for i, p in enumerate(r["pool_w"]):
                    ready(dve, p)
                    ts(mix[:, 4 + i, 0:S], bank(p), par("pool_scale")[:, i:i + 1], None, ALU.mult).then_inc(bank_free[p.bank], 1)

            def attentions():
                ready(dve, r["v"][-1])
                dve.memset(h_flat[:, 0:D], 0.0).then_inc(zero_set, 1)
                for h in range(HEADS):
                    ins = tt_(bias[:, h], bias[:, h], bcast(con("win_mask"), 1, 15), ALU.add)
                link(ins)
                al = par("a_lambda").rearrange("p (v c) -> p v c", v=4)
                link(tt_(lam_t[:, 0:64].rearrange("p (a c) -> p a c", a=2), al[:, 0:4:2], al[:, 1:4:2], ALU.mult))
                dve.tensor_reduce(lam_t[:, 64:66], lam_t[:, 0:64].rearrange("p (a c) -> p a c", a=2), AX_X, ALU.add)\
                    .then_inc(lam_arg, 1)
                dve.wait_ge(lam_exp, 1)
                link(tt_(neg_lam, lam_t[:, 67:68], lam_t[:, 66:67], ALU.subtract))
                link(ts(neg_lam, neg_lam, -LAM_INIT, None, ALU.add))
                link(ts(sub_g, par("subln_g"), 1.0 - LAM_INIT, None, ALU.mult))

                def maxima(i):
                    kind, h, t = UNITS[i]
                    for c, p in enumerate(r["scores", i]):
                        ready(dve, p)
                        s = wide(p, NKEY)
                        if kind == "B":
                            b = bias[:, h, 7 - 2 * t:15 - 2 * t, :].rearrange("p a b -> p (a b)")
                            link(tt_(s[:, C:NKEY], s[:, C:NKEY], b, ALU.add))
                        dve.tensor_reduce(neg_max[:, i % 2, c:c + 1], s, AX_X, ALU.max, negate=True).then_inc(max_ready, 1)

                def take_o(i):
                    kind, h, t = UNITS[i]
                    p = r["PV", i]
                    o = DH * (h % 2)
                    ready(dve, p)
                    to = o_a[o:o + DH, h // 2] if kind == "A" else mix[o:o + DH, 2 + h // 2]
                    dve.tensor_copy(to[:, t * P:(t + 1) * P], ps[o:o + DH, p.bank, 0:P]).then_inc(bank_free[p.bank], 1)

                maxima(0)
                for i, (kind, h, t) in enumerate(UNITS):
                    if i + 1 < len(UNITS):
                        maxima(i + 1)
                    n = 2 if kind == "A" else 1
                    for p in r["scores", i]:
                        read(dve, p)
                    inv = row_inv[:, i % 2]
                    link(dve.reciprocal(inv[:, 0:n], row_sum[:, i % 2, 0:n]))
                    p0, p1 = prob[:, i % 2, 0], prob[:, i % 2, 1]
                    if kind == "A":
                        link(tt_(inv[:, 1:2], inv[:, 1:2], neg_lam, ALU.mult))
                        link(ts(p1, p1, inv[:, 1:2], None, ALU.mult))
                        stt(p0, p0, inv[:, 0:1], p1, ALU.mult, ALU.add).then_inc(prob_ready, 1)
                    else:
                        ts(p0, p0, inv[:, 0:1], None, ALU.mult).then_inc(prob_ready, 1)
                    if i >= 1:
                        take_o(i - 1)
                take_o(len(UNITS) - 1)
                dve.wait_ge(sub_rs, 2)
                for c in range(2):
                    stt(mix[:, c, 0:S], o_a[:, c], sub_g, sub_rs_t[:, c * S:(c + 1) * S], ALU.mult, ALU.mult).then_inc(mixed, 1)

            def first_out():
                p = r["mod2"]
                ready(dve, p)
                tt_(mod2, ps[:, p.bank, 0:32], par("ada_b")[:, 16:48], ALU.add).then_inc(bank_free[p.bank], 1)
                read(dve, p)
                stt(gain2, mod2[:, 16:24], 1.0, par("norm2_g"), ALU.add, ALU.mult).then_inc(mod2_ready, 1)
                dve.wait_ge(mod2_ready, 1)
                for i, p in enumerate(r["w_out"]):
                    ready(dve, p)
                    xi = x[:, i, META:T2]
                    stt(xi, bank(p), mod2[:, i:i + 1], xi, ALU.mult, ALU.add).then_inc(bank_free[p.bank], 1)

            def router():
                dve.wait_ge(zeros_in, 16 * JOBS)
                norm(gain2, x[:, :, META:T2], h2, S, rstd[:, 0:S], scaled, 3)
                p = r["router"]
                ready(dve, p)
                shifted, e_, score, sel, gs, oh, tmp, selm, o1, o2 = (rt[j] for j in range(10))
                lg = ps[:, p.bank, 0:64].rearrange("p (t e) -> p t e", t=ST)
                col = [rt[13 + j // 4][:, j % 4, 0:4] for j in range(12)]
                falling = con("falling")
                fall = bcast(falling, 1, ST)
                link(dve.tensor_reduce(col[0], lg, AX_X, ALU.max))
                tt_(shifted, lg, bcast(col[0], 2, EXPERTS), ALU.subtract).then_inc(bank_free[p.bank], 1)
                read(dve, p)
                dve.wait_ge(route_exp, 1)
                link(dve.tensor_reduce(col[1], e_, AX_X, ALU.add))
                link(dve.reciprocal(col[2], col[1]))
                link(tt_(score, e_, bcast(col[2], 2, EXPERTS), ALU.mult))
                link(tt_(sel, score, bcast(par("router_b"), 1, ST), ALU.add))
                s4 = sel.rearrange("p t (g e) -> p t g e", g=4)
                g1, g2 = gs[:, :, 0:4], gs[:, :, 4:8]
                first = True
                for a in range(4):
                    for b in range(a + 1, 4):
                        link(tt_(g1 if first else g2, s4[:, :, :, a], s4[:, :, :, b], ALU.add))
                        if not first:
                            link(tt_(g1, g1, g2, ALU.max))
                        first = False
                link(dve.tensor_reduce(col[3], g1, AX_X, ALU.max))
                link(tt_(g2, g1, bcast(col[3], 2, 4), ALU.is_equal))
                link(tt_(g2, g2, bcast(falling[:, EXPERTS - 4:EXPERTS], 1, ST), ALU.mult))
                link(dve.tensor_reduce(col[4], g2, AX_X, ALU.max))
                link(tt_(g2, g2, bcast(col[4], 2, 4), ALU.is_equal))
                link(dve.tensor_copy(oh.rearrange("p t (g e) -> p t g e", g=4), bcast(g2, 3, 4)))
                link(tt_(selm, sel, oh, ALU.mult))
                link(ts(tmp, oh, 1.0, -NEG, ALU.subtract, ALU.mult))
                link(tt_(selm, selm, tmp, ALU.add))
                for o, c in ((o1, 5), (o2, 7)):
                    link(dve.tensor_reduce(col[c], selm, AX_X, ALU.max))
                    link(tt_(o, selm, bcast(col[c], 2, EXPERTS), ALU.is_equal))
                    link(tt_(o, o, fall, ALU.mult))
                    link(dve.tensor_reduce(col[c + 1], o, AX_X, ALU.max))
                    link(tt_(o, o, bcast(col[c + 1], 2, EXPERTS), ALU.is_equal))
                    if c == 5:
                        link(stt(selm.rearrange("p t e -> p (t e)"), o.rearrange("p t e -> p (t e)"), 2 * NEG,
                                 selm.rearrange("p t e -> p (t e)"), ALU.mult, ALU.add))
                oh2, rank = rt[11], rt[12]
                tt_(oh2, o1, o2, ALU.add).then_inc(chosen, 1)
                for o, c in ((o1, 8), (o2, 9)):
                    link(tt_(tmp, o, score, ALU.mult))
                    link(dve.tensor_reduce(col[c], tmp, AX_X, ALU.add))
                link(tt_(col[10], col[8], col[9], ALU.add))
                link(dve.reciprocal(col[11], col[10]))
                for c in range(2):
                    link(tt_(gate_c[:, c], col[8 + c], col[11], ALU.mult))
                p = r["rank"]
                ready(dve, p)
                count, n_job, end, first = (rt[16][:, j] for j in range(4))
                dve.tensor_copy(count, ps[:, p.bank, 64:64 + EXPERTS])
                dve.tensor_copy(rank, ps[:, p.bank, 0:64].rearrange("p (t e) -> p t e", t=ST)).then_inc(bank_free[p.bank], 1)
                read(dve, p)
                link(ts(n_job, count, 1.0, None, ALU.is_ge))
                for k in range(1, S // P):
                    link(stt(n_job, count, float(k * P + 1), n_job, ALU.is_ge, ALU.add))
                link(dve.tensor_tensor_scan(end, ones[:, 0:EXPERTS], n_job, 0.0, ALU.mult, ALU.add))
                link(tt_(first, end, n_job, ALU.subtract))
                link(ts(first, first, float(P), None, ALU.mult))
                link(tt_(rank, rank, bcast(first, 1, ST), ALU.add))
                for c, o in enumerate((o1, o2)):
                    link(tt_(tmp, o, rank, ALU.mult))
                    link(dve.tensor_reduce(place[:, c], tmp, AX_X, ALU.add))
                link(dve.tensor_copy(place_i, place.rearrange("p c t -> p (c t)")))
                over = piece(arena, 17700, JOBS, EXPERTS)
                link(tt_(over, bcast(end, 1, JOBS), bcast(con("job"), 2, EXPERTS), ALU.is_le))
                link(dve.tensor_reduce(job_e, over, AX_X, ALU.add))
                link(ts(job_e, job_e, float(EXPERTS - 1), None, ALU.min))
                link(dve.tensor_copy(job_i, job_e))
                dve.tensor_copy(n_jobs_i, end[:, EXPERTS - 1:EXPERTS]).then_inc(jobs_ready, 1)

            def experts():
                dve.wait_ge(jobs_ready, 1)
                n_jobs = dve.value_load(n_jobs_i[0:1, 0:1], min_val=MIN_JOBS, max_val=JOBS - 1)
                hid_flat = hid.rearrange("p k t -> p (k t)")
                with dve.Fori(0, n_jobs) as it:
                    dve.wait_ge(e_done, it * 5 + 4)
                    dve.wait_ge(silu_out, it + 1)
                    tt_(hid_flat, ps[:, 1, :], silu_t, ALU.mult).then_inc(hid_ready, 1)
                for t in range(ST):
                    dve.wait_ge(gathered[t], 32)
                    link(ts(both[:, t], got[:, 0, t], gate_c[:, 0, t:t + 1], None, ALU.mult))
                    stt(both[:, t], got[:, 1, t], gate_c[:, 1, t:t + 1], both[:, t], ALU.mult, ALU.add).then_inc(combined, 1)
                for k, p in enumerate(r["moe_out"]):
                    ready(dve, p)
                    xk = x[:, k, META:T2]
                    stt(xk, bank(p), mod2[:, 24 + k:25 + k], xk, ALU.mult, ALU.add).then_inc(bank_free[p.bank], 1)

            def ab_in():
                norm(par("final_g"), x[:, :, META:T2], x[:, :, META:T2], S, rstd[:, 0:S], x_normed, 4)
                norm(par("norm_ab"), x, h2, T2, rstd[:, 0:T2], h_ready, 6)

            def lru():
                lam = par("lam")
                L = [lru_t[:, 4 * j:4 * j + 4] for j in range(9)]
                stt(L[0], lam, -1.0, lam, ALU.mult, ALU.max).then_inc(lru_y, 1)
                dve.wait_ge(lru_e, 1)
                link(ts(L[2], L[1], 2.0, None, ALU.add))
                link(dve.reciprocal(L[3], L[2]))
                link(tt_(L[2], L[1], L[3], ALU.mult))
                link(tt_(L[3], L[2], L[2], ALU.mult))
                link(ts(L[4], L[3], 1.0 / 17, None, ALU.mult))
                for n in (15, 13, 11, 9, 7, 5, 3):
                    link(stt(L[4], L[4], 1.0 / n, L[3], ALU.add, ALU.mult))
                link(stt(L[4], L[4], 1.0, L[2], ALU.add, ALU.mult))
                link(ts(L[5], lam, -1.0, 0.0, ALU.mult, ALU.max))
                link(stt(L[4], L[4], 2.0, L[5], ALU.mult, ALU.add))
                ts(lru_c, L[4], -8.0, None, ALU.mult).then_inc(lru_cr, 1)
                cw = par("conv_w").rearrange("p (i j) -> p i j", i=4)
                ready(dve, r["ab"][0])
                link(dve.memset(xr[:, :, 0:3], 0.0))
                for i in range(4):
                    read(dve, r["ab"][2 * i])
                    read(dve, r["ab"][2 * i + 1])
                    link(ts(xc[:, i], xr[:, i, 0:T2], cw[:, i, 0:1], par("conv_b")[:, i:i + 1], ALU.mult, ALU.add))
                    for j in (1, 2):
                        link(stt(xc[:, i], xr[:, i, j:j + T2], cw[:, i, j:j + 1], xc[:, i], ALU.mult, ALU.add))
                    stt(xc[:, i], xr[:, i, 3:3 + T2], cw[:, i, 3:4], xc[:, i], ALU.mult, ALU.add).then_inc(xc_ready, 1)
                for i in range(4):
                    dve.wait_ge(lru_act, 4 + i + 1)
                    link(tt_(g_m[:, i], g_a[:, i], g_a[:, i], ALU.mult))
                    stt(g_m[:, i], g_m[:, i], 1.0, g_r[:, i], ALU.add, ALU.mult).then_inc(lru_m, 1)
                for i in range(4):
                    dve.wait_ge(lru_s, i + 1)
                    link(dve.memset(g_m[:, i, 0:1], 1.0))
                    link(tt_(g_m[:, i], g_m[:, i], g_i[:, i], ALU.mult))
                    link(tt_(g_m[:, i], g_m[:, i], xc[:, i], ALU.mult))
                    link(dve.tensor_tensor_scan(g_r[:, i], g_a[:, i], g_m[:, i], 0.0, ALU.mult, ALU.add))
                    tt_(mix[:, i], g_r[:, i], gate[:, i], ALU.mult).then_inc(mixed, 1)

            def swa():
                link(ts(qk_gain[:, 0:1], par("q_norm"), DH ** -0.5, None, ALU.mult))
                link(dve.tensor_copy(qk_gain[:, 1:2], par("k_norm")))
                link(ts(neg_sink, par("sinks"), -1.0, None, ALU.mult))
                dve.wait_ge(swa_in, 32)
                for i in range(5):
                    g = qk_gain[:, 0:1] if i < 4 else qk_gain[:, 1:2]
                    dve.wait_ge(qk_rsr, 2 * i + 2)
                    stt(qk[:, i], qk[:, i], g, qk_rs[:, i], ALU.mult, ALU.mult).then_inc(qk_n, 1)
                for i in range(5):
                    dve.wait_ge(qk_n, i + 1)
                    for j, (at, n) in enumerate(HALVES2):
                        p = r["qk_sw"][2 * i + j]
                        ready(dve, p)
                        tt_(rope_t[:, i % 2, at:at + n], bank(p, n), rope_q[:, 1, at:at + n], ALU.mult).then_inc(bank_free[p.bank], 1)
                    read(dve, p)
                    link(tt_(qk[:, i], qk[:, i], rope_q[:, 0], ALU.mult))
                    tt_(qk[:, i], qk[:, i], rope_t[:, i % 2], ALU.add).then_inc(qk_rot, 1)

                def maxima(i):
                    t, a = GROUPS[i]
                    nq, (col, _, n) = swa_queries(t)[1], swa_keys(t)[-1]
                    mc, mw = SWA_MASKS.get(t, (0, col + n))
                    p = r["swa_s", i]
                    ready(dve, p)
                    s = ps[0:nq, 0:4, 0:col + n]
                    link(tt_(s, s, bcast(swa_mask[0:nq, mc:mc + mw], 1, 4), ALU.add))
                    nm = neg_max[0:nq, i % 2]
                    link(dve.tensor_reduce(nm, s, AX_X, ALU.max, negate=True))
                    link(tt_(nm, nm, neg_sink[0:nq, 4 * a:4 * a + 4], ALU.min))
                    tt_(sink_d[0:nq, i % 2], nm, neg_sink[0:nq, 4 * a:4 * a + 4], ALU.subtract).then_inc(swa_max, 1)

                def take_o(i):
                    t, a = GROUPS[i]
                    q0, nq = swa_queries(t)
                    p = r["swa_o", i]
                    ready(dve, p)
                    dve.tensor_copy(mix[:, 4 + 2 * a:6 + 2 * a, q0:q0 + nq],
                                    ps[:, p.bank, 0:2 * P].rearrange("p (j q) -> p j q", j=2)[:, :, 0:nq]).then_inc(bank_free[p.bank], 1)

                maxima(0)
                for i, (t, a) in enumerate(GROUPS):
                    if i + 1 < len(GROUPS):
                        maxima(i + 1)
                    nq, (col, _, n) = swa_queries(t)[1], swa_keys(t)[-1]
                    read(dve, r["swa_s", i])
                    inv = row_inv[0:nq, i % 2]
                    link(tt_(inv, row_sum[0:nq, i % 2], sink_e[0:nq, i % 2], ALU.add))
                    link(dve.reciprocal(inv, inv))
                    pr = prob2[0:nq, i % 2, :, 0:col + n]
                    tt_(pr, pr, bcast(inv, 2, col + n), ALU.mult).then_inc(swa_prob, 1)
                    if i >= 1:
                        take_o(i - 1)
                take_o(len(GROUPS) - 1)

            def residual(products, pieces, t0, m, it=None):
                for p, (at, n) in zip(products, pieces):
                    ready(dve, p, it)
                    xm = x[:, m, t0 + at:t0 + at + n]
                    tt_(xm, bank(p, n), xm, ALU.add).then_inc(bank_free[p.bank], 1)

            def ab_out():
                for i in range(8):
                    residual(r["ab_out"][2 * i:2 * i + 2], HALVES2, 0, i)

            def ffn(n):
                t0, pieces = (0, HALVES2) if n == 0 else (META, [(0, S)])
                np_ = len(pieces)
                width = T2 if n == 0 else S
                norm(par("norm_ffn")[:, 8 * n:8 * n + 8], x[:, :, t0:T2], h2, width, rstd[:, 0:width], h_ready,
                     8 if n == 0 else 12 - 1)

                def products(g, u, tile, i, it=None):
                    for j, (at, w) in enumerate(pieces):
                        ready(dve, u[j], it)
                        read(dve, g[j], it)
                        tt_(act_w[:, tile, at:at + w], bank(u[j], w), silu_w[:, i, at:at + w], ALU.mult)\
                            .then_inc(bank_free[u[j].bank], 1)

                with dve.Fori(0, 3) as it:
                    for i in range(6):
                        a = np_ * 2 * i
                        body = r["ffn_loop", n]
                        products(body[a:a + np_], body[a + np_:a + 2 * np_], it * 6 + i, i, it)
                for i in range(4):
                    a = np_ * 2 * i
                    rest = r["ffn_rest", n]
                    products(rest[a:a + np_], rest[a + np_:a + 2 * np_], 18 + i, i)
                with dve.Fori(0, 2) as it:
                    for m in range(4):
                        residual(r["ffn_down", n][np_ * m:np_ * (m + 1)], pieces, t0, it * 4 + m, it)

            def retention():
                norm(par("norm_ret"), x, h2, T2, rstd[:, 0:T2], h_ready, 10)
                dve.wait_ge(ret_in, 32)
                cos, sin = rope_r[:, 0], rope_r[:, 1]
                with dve.Fori(0, RET_HEADS) as it:
                    me.loop(it, 12)
                    for name, to, pieces, off in (("q", ret_q, [(0, S)], META), ("k", ret_k, HALVES2, 0)):
                        np_ = len(pieces)
                        for j, (at, n) in enumerate(pieces):
                            p1, p2 = r["ret", name][j], r["ret", name][np_ + j]
                            c, s = cos[:, off + at:off + at + n], sin[:, off + at:off + at + n]
                            a, b = rot_t[:, 0, 0:n], rot_t[:, 1, 0:n]
                            lo, hi = to[:, 0, at:at + n], to[:, 1, at:at + n]
                            ready(dve, p2, it)
                            tt_(lo, bank(p1, n), c, ALU.mult)
                            link(tt_(a, bank(p2, n), s, ALU.mult))
                            link(tt_(lo, lo, a, ALU.subtract))
                            tt_(hi, bank(p2, n), c, ALU.mult).then_inc(bank_free[p2.bank], 1)
                            tt_(b, bank(p1, n), s, ALU.mult).then_inc(bank_free[p1.bank], 1)
                            read(dve, p1, it)
                            ins = tt_(hi, hi, b, ALU.add)
                            if name == "k" and j == np_ - 1:
                                ins.then_inc(ret_qk, 1)
                            else:
                                link(ins)
                    for t, p in enumerate(r["ret", "s"]):
                        n = P if t < 4 else META
                        at = max(P * t - META, 0)
                        first = META + at - P * t
                        ready(dve, p, it)
                        tt_(ret_s[0:n, t, at:S], ps[0:n, p.bank, at:S],
                            decay_r[0:n, it, first:first + S - at], ALU.mult).then_inc(bank_free[p.bank], 1)
                    dve.wait_ge(ret_rs, it + 1)
                    for i in range(4):
                        ins = tt_(ret_o[:, i], ret_o[:, i], rstd[:, 0:S], ALU.mult)
                        link(ins)
                    for i in range(4):
                        ins = tt_(ret_y[:, it * 4 + i], ret_o[:, i], ret_g[:, i], ALU.mult)
                    ins.then_inc(ret_yr, 1)
                    me.end(RET_HEADS)

            def ret_out():
                for i in range(8):
                    residual([r["ret_out"][i]], [(0, S)], META, i)

            filters()
            modulation()
            hyena()
            projections()
            attentions()
            first_out()
            router()
            experts()
            ab_in()
            lru()
            swa()
            ab_out()
            ffn(0)
            retention()
            ret_out()
            ffn(1)



def shape_constants():
    import numpy as np
    f = np.float64
    out = {}
    ones = np.ones((P, P))
    head_ones = np.kron(np.eye(2), np.ones((DH, DH)))
    i = np.arange(P)
    swap_a = np.zeros((P, P)); swap_a[i ^ 16, i] = 1
    swap_q = np.zeros((P, P)); rot = i[i % DH < 16]; swap_q[rot ^ 8, rot] = 1
    qc, kc = i[:, None] % GRID, np.arange(GRID)[None, :]
    c0 = np.clip(qc - WIN_C // 2, 0, GRID - WIN_C)
    win = np.where((kc >= c0) & (kc < c0 + WIN_C), 0.0, NEG)
    falling = np.tile(EXPERTS - np.arange(EXPERTS), (P, 1))
    earlier = (i[:, None] < i[None, :]).astype(f)
    job = np.tile(np.arange(JOBS), (P, 1))
    out["const"] = np.concatenate([np.eye(P), ones, head_ones, swap_a, swap_q, win, falling, earlier, job], 1)

    inv = 10000.0 ** (-np.arange(8, dtype=f) / 8)
    t = np.arange(S)
    ang = np.concatenate([(t // GRID)[:, None] * inv, (t % GRID)[:, None] * inv], 1).T
    r = i % 32
    a = ang[r % 16]
    out["rope_a"] = np.stack([np.cos(a), np.where(r < 16, -1, 1)[:, None] * np.sin(a)], 1)
    t = np.arange(T2)
    r = i % DH
    inv = 500000.0 ** (-np.arange(8, dtype=f) / 8)
    a = t[None, :] * inv[r % 8][:, None]
    on = (r < 16)[:, None]
    out["rope_q"] = np.stack([np.where(on, np.cos(a), 1.0), np.where(on, np.where(r < 8, -1, 1)[:, None] * np.sin(a), 0.0)], 1)
    inv = 10000.0 ** (-np.arange(P, dtype=f) / P)
    a = t[None, :] * inv[:, None]
    out["rope_r"] = np.stack([np.cos(a), np.sin(a)], 1)
    g = np.log1p(-np.exp2(-5.0 - np.arange(RET_HEADS, dtype=f)))
    d = np.arange(T2)[None, None, :] - i[:, None, None]
    out["decay_r"] = np.where(d >= 0, np.exp(np.maximum(d, 0) * g[None, :, None]), 0.0) / 16.0

    q = i[:, None]; k = i[None, :]
    prev, causal, seen = np.where(k > q, 0.0, NEG), np.where(k <= q, 0.0, NEG), np.zeros((P, META))
    out["swa_mask"] = np.concatenate([seen, prev, causal, seen, causal, causal[:, :META]], 1)

    n, k = np.arange(S, dtype=f)[:, None], np.arange(S, dtype=f)[None, :]
    w = 2 * np.pi * (k + 0.5) * n / (2 * S)
    tab = np.stack([np.cos(w), np.sin(w)]).reshape(2, ST, P, ST, P)
    out["dft"] = tab.transpose(3, 2, 0, 1, 4).reshape(ST, P, TILE)
    w = 2 * np.pi * (k + 0.5) * (n + 0.5) / (2 * S)
    out["dft_half"] = np.stack([np.cos(w), np.sin(w)]).reshape(2, ST, P, S).transpose(2, 0, 1, 3)
    tn = np.arange(S, dtype=np.float32) / np.float32(S - 1)
    bands = np.linspace(1e-4, 15, 16, dtype=np.float32)
    ang = (np.float32(2.0 * math.pi / S) * np.arange(S, dtype=np.float32)[:, None]) * bands[None, :]
    z = np.concatenate([tn[:, None], np.cos(ang), np.sin(ang)], 1).T
    out["z"] = np.concatenate([z, np.zeros((P - 33, S))], 0)
    deltas = np.abs(np.linspace(math.log(1e-2) / 1.5, math.log(1e-2) / 0.3, 256, dtype=np.float32))
    out["decay_h"] = np.exp(-tn[:, None] * deltas).reshape(ST, P, 256).transpose(1, 0, 2).reshape(P, 1024)
    t = np.arange(S)
    inv = []
    for w in (2, 4, 8, 16):
        inv.append(1.0 / (np.clip(t + w // 2, 0, S) - np.clip(t - w // 2, 0, S)))
    inv = np.repeat(np.stack(inv), DH, 0).reshape(2, P, S).transpose(1, 0, 2)
    out["pool_inv"] = inv
    return {k: np.ascontiguousarray(v, dtype=np.float32) for k, v in out.items()}


def lay_out(x, c, ctx, c_ctx, norm1_g, norm2_g, ada_w, ada_b, w_in, w_out, a_lambda, a_subln_g, b_rpb,
            pool_w, pool_scale, hy_short_w, hy_short_b, hy_f_w1, hy_f_b1, hy_f_w2, hy_f_b2, hy_f_w3,
            hy_f_b3, hy_skip, router_w, router_b, moe_w1, moe_w3, moe_w2, final_g, meta_tokens_2,
            mix_norm_ab_2, ab_w_in_2, lru_conv_w_2, lru_conv_b_2, lru_w_a_2, lru_b_a_2, lru_w_i_2,
            lru_b_i_2, lru_lambda_2, q_norm_2, k_norm_2, attn_sinks_2, ab_w_out_2, mix_norm_ret_2,
            ret_w_in_2, ret_w_out_2, ffn_norm_2, ffn_w_gu_2, ffn_w_down_2):
    import numpy as np
    k = shape_constants()

    def rows(v):
        return np.asarray(v).reshape(-1, P).T

    def every(v):
        v = np.asarray(v).reshape(1, -1)
        return np.repeat(v, P, 0)

    def padded(v):
        v = np.asarray(v)
        v = v.reshape(v.shape[0], -1)
        return np.concatenate([v, np.zeros((P - v.shape[0], v.shape[1]), v.dtype)], 0)

    def tiles(w):
        w = np.asarray(w)
        kk, m = w.shape
        return w.reshape(kk // P, P, m // P, P).transpose(2, 1, 0, 3).reshape(m // P, P, kk)

    def moving(w):
        w = np.asarray(w)
        n = w.shape[1]
        return w.reshape(4, 2, P, n // 512, 512).transpose(3, 0, 2, 1, 4).reshape(n // 512 * 4, P, TILE)

    def down(w):
        w = tiles(w)
        w = np.concatenate([w, np.zeros((KT, P, 24 * P - FF), w.dtype)], 2)
        return w.reshape(KT, P, 3, TILE).transpose(0, 2, 1, 3).reshape(24, P, TILE)

    def alternate(*ws):
        return np.stack(ws, 1).reshape(-1, P, ws[0].shape[-1])

    w_in0, w_out0, ada0 = (np.asarray(w)[0] for w in (w_in, w_out, ada_w))
    ada = tiles(ada0)
    hy = tiles(w_in0[:, 1792:2560])
    mixers = np.concatenate([tiles(w_in0[:, a:a + 256]) for a in (0, 256, 768, 1024, 1536)])
    values = moving(np.concatenate([w_in0[:, 512:768], w_in0[:, 1280:1536]], 1))
    w1, w3, w2 = (np.asarray(w)[0] for w in (moe_w1, moe_w3, moe_w2))
    moe = []
    for e in range(EXPERTS):
        moe.append(np.concatenate([tiles(w1[e]), tiles(w3[e]), w2[e].reshape(4, P, TILE)]))
    ab = np.asarray(ab_w_in_2)[0]
    q_heads = np.array([4 * kv + j for j in range(4) for kv in range(2)])
    q_cols = (q_heads[:, None] * DH + np.arange(DH)).ravel()
    ab_tiles = np.concatenate([tiles(ab[:, 0:1024]), tiles(ab[:, 1024:1536][:, q_cols]), tiles(ab[:, 1536:1664])])
    ab_v = tiles(ab[:, 1664:1792])
    gates = []
    for i in range(4):
        for w in (lru_w_a_2, lru_w_i_2):
            w = np.asarray(w)[0]
            m = np.zeros((P, P), w.dtype)
            m[:DH, :DH], m[DH:, DH:] = w[2 * i], w[2 * i + 1]
            gates.append(m)
    gates = np.stack(gates, 1).reshape(1, P, TILE)
    ab_o = np.asarray(ab_w_out_2)[0]
    ab_o = tiles(np.concatenate([ab_o[:512], ab_o[512:][q_cols]], 0))
    ffn = []
    for n in range(2):
        gu, dn = np.asarray(ffn_w_gu_2)[n], np.asarray(ffn_w_down_2)[n]
        ffn.append(np.concatenate([alternate(tiles(gu[:, :FF]), tiles(gu[:, FF:])), down(dn)]))
    ret = np.asarray(ret_w_in_2)[0]
    heads = []
    for h in range(RET_HEADS):
        heads += [tiles(ret[:, h * 256:h * 256 + 256]), tiles(ret[:, 1024 + h * 256:1280 + h * 256]),
                  moving(ret[:, 2048 + h * 512:2560 + h * 512]), tiles(ret[:, 4096 + h * 512:4608 + h * 512])]
    ro = np.asarray(ret_w_out_2)[0]
    ro = tiles(ro).reshape(KT, P, 2, TILE).transpose(0, 2, 1, 3).reshape(16, P, TILE)

    parts = {"dft": k["dft"], "mod1": ada[:16], "hyena": hy[[4, 5, 0, 1, 2, 3]], "mixers": mixers, "values": values,
             "mod2": ada[16:], "w_out": tiles(w_out0), "ab": ab_tiles, "ab_values": ab_v,
             "lru_gates": gates, "ab_out": ab_o, "ffn0": ffn[0], "ret": np.concatenate(heads), "ret_out": ro,
             "ffn1": ffn[1]}
    for name, n in STREAM:
        assert parts[name].shape == (n, P, TILE), (name, parts[name].shape)
    weights = np.concatenate([parts[name] for name, _ in STREAM], 0)

    small = {
        "c": np.stack([rows(np.asarray(c)[0]), rows(c_ctx)], 2), "norm1_g": rows(norm1_g), "norm2_g": rows(norm2_g),
        "final_g": rows(final_g), "norm_ab": rows(mix_norm_ab_2), "norm_ret": rows(mix_norm_ret_2),
        "norm_ffn": rows(ffn_norm_2), "ada_b": rows(ada_b), "a_lambda": every(a_lambda),
        "subln_g": np.tile(np.asarray(a_subln_g).reshape(DH, 1), (2, 1)), "pool_scale": rows(pool_scale),
        "short_w": np.asarray(hy_short_w)[0].reshape(3, 6, P).transpose(2, 1, 0), "short_b": rows(hy_short_b),
        "f_b1": padded(np.asarray(hy_f_b1).T), "f_b2": padded(np.asarray(hy_f_b2).T),
        "skip": np.asarray(hy_skip)[0].reshape(2, 2, P).transpose(2, 0, 1),
        "router_w": np.asarray(router_w).reshape(KT, P, EXPERTS).transpose(1, 0, 2), "router_b": every(router_b),
        "conv_w": np.asarray(lru_conv_w_2)[0].reshape(4, 4, P).transpose(2, 1, 0), "conv_b": rows(lru_conv_b_2),
        "b_a": rows(np.asarray(lru_b_a_2).reshape(-1)), "b_i": rows(np.asarray(lru_b_i_2).reshape(-1)),
        "lam": rows(lru_lambda_2), "q_norm": np.tile(np.asarray(q_norm_2).reshape(DH, 1), (2, 1)),
        "k_norm": np.tile(np.asarray(k_norm_2).reshape(DH, 1), (2, 1)),
        "sinks": every(np.asarray(attn_sinks_2)[0][q_heads]),
    }
    small = np.concatenate([small[name].reshape(P, n) for name, n in SMALL], 1)
    w3 = np.concatenate([np.asarray(hy_f_w3)[0], np.asarray(hy_f_b3)], 0)
    filt = np.concatenate([padded(np.asarray(hy_f_w1)[0]), padded(np.asarray(hy_f_w2)[0]), padded(w3), k["z"], k["decay_h"]], 1)

    rpb = np.asarray(b_rpb)[0]
    wide = np.pad(rpb, ((0, 0), (1, 1), (GRID - WIN_C, GRID - WIN_C)))
    qc, kc = np.arange(GRID)[:, None], np.arange(GRID)[None, :]
    picked = wide[:, :, kc - qc + GRID - 1]
    picked = picked.transpose(2, 0, 1, 3)
    bias = np.concatenate([picked[:, :, 1:16], picked[:, :, 0:15]], 0)

    pw = np.asarray(pool_w)[0]
    pool = np.zeros((P, 2, P), pw.dtype)
    for g in range(4):
        o = DH * (g % 2)
        pool[o:o + DH, g // 2, o:o + DH] = pw[g]

    def feature_major(v):
        v = np.asarray(v)
        return v.reshape(-1, KT, P).transpose(2, 1, 0)

    arrays = {
        "weights": weights, "experts": np.stack(moe), "small": small, "const": k["const"], "filter": filt,
        "x": feature_major(np.asarray(x)[0]), "ctx": feature_major(np.asarray(ctx)[0]),
        "meta": feature_major(meta_tokens_2), "bias": bias, "pool_w": pool, "pool_inv": k["pool_inv"],
        "rope_a": k["rope_a"], "rope_q": k["rope_q"], "rope_r": k["rope_r"], "decay_r": k["decay_r"],
        "swa_mask": k["swa_mask"], "dft_half": k["dft_half"],
    }
    return {n: np.ascontiguousarray(a) for n, a in arrays.items()}


def kernel(**inputs):
    import concourse.bacc as _bacc
    from concourse import mybir as _mybir
    from concourse.bass_utils import run_bass_kernel_spmd as _run

    nc = _bacc.Bacc("TRN2", target_bir_lowering=False, num_devices=1)
    arrays = lay_out(**inputs)
    args = {n: nc.dram_tensor(f"in_{n}", a.shape, _mybir.dt.from_np(a.dtype), kind="ExternalInput").ap()
            for n, a in arrays.items()}
    args["out"] = nc.dram_tensor("out", (P, KT, S), F32, kind="ExternalOutput").ap()
    two_blocks(nc, args)
    r = _run(nc, [{f"in_{n}": a for n, a in arrays.items()}], core_ids=[0])
    got = r.results[0]["out"]
    return got.transpose(2, 1, 0).reshape(1, S, D)
```

```python
import math
from contextlib import ExitStack

import concourse.bass as bass
from concourse import mybir

ALU = mybir.AluOpType
ACT = mybir.ActivationFunctionType
AX_X = mybir.AxisListType.X
F32 = mybir.dt.float32
U32 = mybir.dt.uint32
I32 = mybir.dt.int32

P = 128
D = 1024
KT = D // P
S = 512
C = 256
META = 16
T2 = META + S
HALF2 = T2 // 2
NKEY = C + S
ST = S // P
NKT = NKEY // P
GRID = 64
WIN_R, WIN_C = 8, 16
HEADS = 4
DH = 64
EXPERTS = 16
FF = 2816
FFT = FF // P
SWA_HEADS = 8
RET_HEADS = 4
LAM_INIT = 0.8 - 0.6 * math.exp(0.0)
EPS = 1e-6
NEG = -1e30
TWO_PI_HI = 6.28125
TWO_PI_LO = 2 * math.pi - TWO_PI_HI
ROUND = 1.5 * 2.0 ** 23
PI_BELOW = 3.1415925

RING = 12
TILE = 1024
STREAM = [
    ("mod1", 16),
    ("dft", 4),
    ("hyena", 6), ("mixers", 10), ("values", 4),
    ("mod2", 32),
    ("w_out", 8),
    ("ab", 13), ("ab_values", 1), ("lru_gates", 1), ("ab_out", 8),
    ("ffn0", 2 * FFT + 24),
    ("ret", 12 * RET_HEADS), ("ret_out", 16),
    ("ffn1", 2 * FFT + 24),
]
EXPERT_TILES = 12
JOBS = 24
MIN_JOBS = 2 * S // P
START, N_TILES = {}, 0
for _name, _n in STREAM:
    START[_name] = N_TILES
    N_TILES += _n

SMALL = [
    ("c", 16), ("norm1_g", 8), ("norm2_g", 8), ("final_g", 8), ("norm_ab", 8), ("norm_ret", 8),
    ("norm_ffn", 16), ("ada_b", 48), ("a_lambda", 128), ("subln_g", 1), ("pool_scale", 2),
    ("short_w", 18), ("short_b", 6), ("f_b1", 1), ("f_b2", 1), ("skip", 4), ("router_w", 128),
    ("router_b", 16), ("conv_w", 16), ("conv_b", 4), ("b_a", 4), ("b_i", 4), ("lam", 4),
    ("q_norm", 1), ("k_norm", 1), ("sinks", 8),
]
CONST = [("ident", 128), ("ones", 128), ("head_ones", 128), ("swap_a", 128), ("swap_q", 128),
         ("win_mask", 64), ("falling", 16), ("earlier", 128)]
FILTER = [("w1", 64), ("w2", 64), ("z", 512), ("w3", 1024), ("decay", 1024)]
FILTER_FIRST = 640


def offsets(parts):
    at, out = 0, {}
    for name, n in parts:
        out[name] = (at, n)
        at += n
    return out, at


class Product:

    def __init__(self, banks, order, after, released, order_step=0, free_step=0):
        self.bank, self.banks, self.order, self.after, self.released = banks[0], banks, order, after, released
        self.order_step, self.free_step = order_step, free_step


class Banks:

    def __init__(self):
        self.order = 0
        self.releases = [0] * 8
        self.last = [None] * 8
        self.turn = 0

    def take(self, *banks):
        after = sorted({self.last[b] for b in banks if self.last[b] is not None})
        first = banks[0]
        self.releases[first] += 1
        p = Product(banks, self.order, after, self.releases[first])
        for b in banks:
            self.last[b] = (first, self.releases[first])
        self.order += 1
        return p

    def many(self, n, banks=tuple(range(8))):
        out = []
        for _ in range(n):
            out.append(self.take(banks[self.turn % len(banks)]))
            self.turn += 1
        return out

    def settle(self):
        waits = sorted({x for x in self.last if x is not None})
        self.last = [(b, self.releases[b]) if self.releases[b] else None for b in range(8)]
        self.turn = 0
        return waits

    def loop(self, n, turns, banks):
        assert n % len(banks) == 0
        out = [self.take(banks[i % len(banks)]) for i in range(n)]
        for p in out:
            p.order_step, p.free_step = n, n // len(banks)
        self.order += n * (turns - 1)
        for b in banks:
            self.releases[b] += (turns - 1) * (n // len(banks))
            self.last[b] = (b, self.releases[b])
        self.turn = 0
        return out


def plan():
    b = Banks()
    r = {}
    r["f_h1"], r["f_h2"] = b.many(2)
    r["f_h3"] = b.many(8)
    r["f_norm"], = b.many(1)
    r["f_spec"] = b.many(4)
    r["ms_x"], r["ms_c"], r["mod1"] = b.many(3)
    r["f_spec"] += b.many(4)

    r["hy"] = b.many(6)
    for o in range(2):
        r["hy_t", o] = b.many(4)
        r["hy_f", o] = b.many(4)
        r["hy_i", o] = b.many(2)

    for name, n in (("aq", 2), ("ak", 4), ("rope", 4), ("bq", 2), ("bk", 4), ("pool", 2), ("v", NKT),
                    ("pool_w", 2)):
        r[name] = b.many(n)

    r["mod2"] = b.take(7)
    b.order -= 1
    pair = 0
    for i in range(-1, len(UNITS)):
        if i + 1 < len(UNITS):
            r["scores", i + 1] = []
            for _ in range(2 if UNITS[i + 1][0] == "A" else 1):
                r["scores", i + 1].append(b.take(2 * pair, 2 * pair + 1))
                pair = 1 - pair
        if i >= 0:
            r["T", i] = [b.take(4), b.take(5)]
            r["PV", i] = b.take(6)
    r["mod2"].order = b.order
    b.order += 1
    r["subln"] = [b.take(4), b.take(5)]

    r["before_w_out"] = b.settle()
    r["w_out"] = b.many(8)

    r["ms_2"], r["router"] = b.many(2)
    r["rows"] = b.many(8)
    r["rank"], = b.many(1)
    r["slots"], = b.many(1)
    r["before_jobs"] = b.settle()
    r["moe_out"] = b.many(8)
    r["ms_f"], = b.many(1)
    r["ms_ab"] = b.many(2)
    r["ab"] = b.many(26)
    r["ab_v"] = b.many(5)
    r["qk_ms"] = b.many(10)
    r["lru"] = b.many(16)
    r["qk_sw"] = b.many(10)
    r["before_swa"] = b.settle()
    for i in range(-1, len(GROUPS)):
        if i + 1 < len(GROUPS):
            r["swa_s", i + 1] = b.take(0, 1, 2, 3)
        if i >= 0:
            r["swa_t", i] = [b.take(4 + h % 2) for h in range(4)]
            r["swa_o", i] = b.take(6 + i % 2)
    r["before_ab_out"] = b.settle()
    r["ab_out"] = b.many(16)

    for n, halves in ((0, 2), (1, 1)):
        r["ffn_ms", n] = b.many(halves)
        r["before_ffn", n] = b.settle()
        r["ffn_loop", n] = b.loop(12 * halves, 3, range(6))
        r["ffn_rest", n] = b.many(8 * halves, tuple(range(6)))
        r["before_down", n] = b.settle()
        r["ffn_down", n] = b.loop(4 * halves, 2, range(4 * halves))
        if n == 0:
            r["ms_ret"] = b.many(2)
            r["before_ret"] = b.settle()
            body = b.loop(25, RET_HEADS, range(5))
            for name, k in (("q", 2), ("k", 4), ("v", 5), ("g", 4), ("s", 5), ("o", 4), ("ms", 1)):
                r["ret", name], body = body[:k], body[k:]
            r["ret_out"] = b.many(8)
    return r


UNITS = [(a, h, t) for a in "AB" for h in range(HEADS) for t in range(ST)]
GROUPS = [(t, a) for t in range(5) for a in range(2)]
HALVES2 = [(0, HALF2), (HALF2, HALF2)]


def swa_keys(t):
    if t == 0:
        return [(0, 0, META)]
    if t == 1:
        return [(0, 0, META + P)]
    return [(0, 0, META), (META, META + P * (t - 2), 2 * P)]


def swa_queries(t):
    return (0, META) if t == 0 else (META + P * (t - 1), P)


def swa_chunks(t):
    chunks = [(0, META, 0)]
    if t >= 1:
        chunks += [(META, P, max(t - 1, 1))]
    if t >= 2:
        chunks += [(META + P, P, t)]
    return chunks


SWA_MASKS = {0: (2 * META + 3 * P, META), 1: (META + 2 * P, META + P)}

ROOTS, _made = {}, 0
for _name, _n in (("ms_x", 1), ("ms_c", 1), ("subln", 2), ("ms_2", 1), ("ms_f", 1), ("ms_ab", 2), ("qk_ms", 10),
                  (("ffn_ms", 0), 2), ("ms_ret", 2), (("ffn_ms", 1), 1)):
    _made += _n
    ROOTS[_name] = _made


MIXED_1 = 4
MIXED_2 = MIXED_1 + 4


def two_blocks(nc, d):
    r = plan()
    s_off, s_n = offsets(SMALL)
    c_off, c_n = offsets(CONST)
    f_off, f_n = offsets(FILTER)
    with ExitStack() as ctx:
        def sb(name, *shape):
            return ctx.enter_context(nc.sbuf_tensor(name, [P, *shape], F32))

        def sem(name):
            return ctx.enter_context(nc.semaphore(name))

        ring = sb("ring", RING, TILE)
        x = sb("residual", KT, T2)
        h_flat = sb("normed", KT * NKEY)
        mix = sb("mixed", KT, T2)
        small = sb("small", s_n)
        const = sb("const_sb", c_n)
        rstd = sb("rstd", T2 + C)
        tiny = sb("tiny", 640)
        arena = sb("arena", 23552)
        ps = ctx.enter_context(nc.psum_tensor("products", [P, 8, 512], F32))
        h1 = h_flat[:, :].rearrange("p (k t) -> p k t", k=KT)
        h2 = h_flat[:, 0:KT * T2].rearrange("p (k t) -> p k t", k=KT)

        def par(name):
            o, n = s_off[name]
            return small[:, o:o + n]

        def con(name):
            o, n = c_off[name]
            return const[:, o:o + n]

        def piece(of, at, *shape):
            n = math.prod(shape)
            v = of[:, at:at + n]
            if len(shape) == 2:
                v = v.rearrange("p (a b) -> p a b", a=shape[0])
            if len(shape) == 3:
                v = v.rearrange("p (a b c) -> p a b c", a=shape[0], b=shape[1])
            if len(shape) == 4:
                v = v.rearrange("p (a b c e) -> p a b c e", a=shape[0], b=shape[1], c=shape[2])
            return v

        ident, ones, head_ones = con("ident"), con("ones"), con("head_ones")
        eps = tiny[:, 0:1]
        silu_c = piece(tiny, 2, KT, 2)
        mod1 = piece(tiny, 18, 16, 2)
        gain1 = piece(tiny, 50, KT, 2)
        mod2 = tiny[:, 66:98]
        gain2 = tiny[:, 98:106]
        conv_rs = tiny[:, 106:110]
        lam_t = tiny[:, 110:180]
        neg_lam = tiny[:, 180:181]
        sub_g = tiny[:, 181:182]
        neg_max = piece(tiny, 182, 2, 4)
        row_sum = piece(tiny, 190, 2, 4)
        row_inv = piece(tiny, 198, 2, 4)
        qk_gain = tiny[:, 206:208]
        lru_t = tiny[:, 208:244]
        lru_c = tiny[:, 244:248]
        neg_sink = tiny[:, 248:256]
        sink_d = piece(tiny, 256, 2, 4)
        sink_e = piece(tiny, 264, 2, 4)

        lane = tiny[:, 288:416]
        result_no = tiny[:, 416:424]
        partition = tiny[:, 424:425]
        pool_turn = tiny[:, 426:427]
        unused_row = tiny[:, 425:426]

        kc = piece(arena, 0, ST, 2, 256)
        ks = piece(arena, 2048, ST, 2, 256)
        dft = piece(arena, 4096, 2, ST, S)
        acc1 = piece(arena, 4096, 2, 2, TILE)
        sq_c = piece(arena, 15352, KT, C)
        filt = piece(arena, 8192, ST, 2, 2, 256)
        diff = piece(arena, 12288, ST, 2, 256)
        arg = piece(arena, 14336, 3, S)
        sin1, sin2 = h_flat[:, 4736:5248], h_flat[:, 5248:5760]
        ctx_raw = piece(h_flat, 0, KT, C)
        f_in = h_flat[:, 2048:2048 + f_n]

        def fil(name):
            o, n = f_off[name]
            return f_in[:, o:o + n]

        f_sq = mix[:, :, :].rearrange("p k t -> p (k t)")[:, 0:4096].rearrange(
            "p (a b c e) -> p a b c e", a=ST, b=2, c=2)
        hy_raw = piece(arena, 8192, 6, S + 2)
        hy = piece(arena, 11276, 6, S)
        sig_t = piece(arena, 8192, ST, 256)
        spec = piece(arena, 9216, 2, ST, 256)
        prod_t = piece(arena, 14348, 2, 2, 256)
        z1 = piece(arena, 15372, 2, S)
        y_t = piece(arena, 16396, S)
        bias = piece(arena, 17656, HEADS, 15, GRID)
        rope_a = piece(arena, 21496, 2, S)
        pool_inv = piece(arena, 22520, 2, S)
        pool_w = piece(arena, 17400, 2, P)
        aq = piece(arena, 0, 2, S)
        ak = piece(arena, 1024, 2, NKEY)
        bq = piece(arena, 2560, 2, S)
        bk = piece(arena, 3584, 2, NKEY)
        vals = piece(arena, 5120, NKT, 2, 256)
        o_a = piece(arena, 8192, 2, S)
        prob = piece(arena, 9216, 2, 2, NKEY)
        prob_t = piece(arena, 12288, 2, NKT, P)
        raw_a = piece(arena, 13824, 4, S)
        prob_sq = piece(arena, 13824, 2, S)
        sub_rs_t = arena[:, 14848:15872]
        acc2 = piece(h_flat, D, 4, TILE)
        pool_u = piece(arena, 9216, 2, S + 16)
        pool_s = [piece(arena, 10272 + 1056 * i, 2, S + 16) for i in range(4)]
        pool_y = piece(arena, 9216 + 1056 * 5, 2, S)
        sq_a = piece(arena, 0, KT, T2)
        rows = piece(arena, 0, ST, D)
        job_in = arena[:, 4096:5120]
        job_t = piece(arena, 5120, KT, P)
        silu_t = arena[:, 6144:6656]
        hid = piece(arena, 6656, 4, P)
        job_out = piece(arena, 7168, 2, S)
        got = piece(arena, 8192, 2, ST, D)
        both = piece(arena, 0, ST, D)
        rt = [piece(arena, 16384 + 64 * i, ST, EXPERTS) for i in range(18)]
        place = piece(arena, 17536, 2, ST)
        gate_c = piece(arena, 17552, 2, ST)
        job_e = arena[:, 17568:17568 + JOBS]
        job_i = arena[:, 17600:17600 + JOBS].bitcast(I32)
        n_jobs_i = arena[:, 17632:17633].bitcast(I32)
        slot_hot = piece(arena, 8192, 2 * ST, P)
        job_hot = piece(arena, 9216, 2 * ST, JOBS)
        job_of, slot_of = arena[:, 9408:9416], arena[:, 9416:9424]
        result_f, gather_f, slot_t = (arena[:, 9424 + JOBS * i:9424 + JOBS * (i + 1)] for i in range(3))
        gather_i = arena[:, 18100:18100 + JOBS].bitcast(U32)
        result_i = arena[:, 18130:18130 + JOBS].bitcast(U32)
        gather_now = arena[:, 18160:18161].bitcast(U32)
        result_now = arena[:, 18162:18163].bitcast(U32)
        token_rows = nc.dram_tensor("token_rows", (S, D), F32, kind="Internal").ap()
        results = nc.dram_tensor("results", (2 * S + P, D), F32, kind="Internal").ap()
        xr = piece(arena, 0, 4, 3 + T2)
        gate = piece(arena, 2124, 4, T2)
        qk = piece(arena, 4236, 5, T2)
        val2 = piece(arena, 6876, 5, P)
        xc = piece(arena, 7516, 4, T2)
        g_r = piece(arena, 9628, 4, T2)
        g_i = piece(arena, 11740, 4, T2)
        g_a = piece(arena, 13852, 4, T2)
        g_m = piece(arena, 15964, 4, T2)
        rope_q = piece(arena, 18076, 2, T2)
        swa_mask = arena[:, 19132:19564]
        qk_sq = piece(arena, 19564, 5, T2)
        qk_rs = piece(h_flat, 0, 5, T2)
        rope_t = piece(h_flat, 2640, 2, T2)
        prob2 = piece(h_flat, 3696, 2, 4, 272)
        prob2_t = piece(h_flat, 0, 2, 4, 384)
        act_w = piece(arena, 0, FFT, T2)
        silu_w = piece(arena, 11616, 6, T2)
        ret_y = piece(arena, 0, 16, S)
        ret_q = piece(arena, 8192, 2, S)
        ret_k = piece(arena, 9216, 2, T2)
        ret_v = piece(arena, 10272, 5, S)
        ret_g = piece(arena, 12832, 4, S)
        ret_o = piece(arena, 14880, 4, S)
        ret_sq = piece(arena, 16928, 4, S)
        decay_r = piece(arena, 18976, RET_HEADS, T2)
        rope_r = piece(arena, 21088, 2, T2)
        rot_t = piece(arena, 22144, 2, T2)
        ret_s = mix[:, 0:5, 0:S]

        landed = [sem(f"weights_in_{i}") for i in range(RING)]
        begun = sem("tile_begun")
        mod_read = sem("modulation_tiles_read")
        done = sem("products_done")
        bank_free = [sem(f"bank_free_{i}") for i in range(8)]
        dve_step = sem("dve_step")
        act_step = sem("act_step")
        small_in, const_in, filter_in, x_in, ctx_in = (sem(n + "_in") for n in ("small", "const", "filter", "x", "ctx"))
        dft_in, att_in, swa_in, ret_in = (sem(n + "_in") for n in ("dft", "att", "swa", "ret"))
        filter_rest_in = sem("filter_rest_in")
        eps_set = sem("eps_set")
        sin_arg, sin_ready, filter_sq, filter_rs, spec_in = (sem(n) for n in (
            "sin_arg", "sin_ready", "filter_squares", "filter_norms", "spectra_inputs"))
        silu_ready = sem("silu_c_ready")
        squares = sem("squares_ready")
        squares_summed = sem("squares_summed")
        rstd_ready = sem("rstd_ready")
        scaled = sem("h_scaled")
        h_ready = sem("h_ready")
        mod1_ready, mod2_ready = sem("mod1_ready"), sem("mod2_ready")
        conv_ready, spec_ready, z_ready = sem("conv_ready"), sem("spectrum_ready"), sem("z_ready")
        roped, pooled = sem("roped"), sem("pooled")
        max_ready, exp_ready, prob_ready = sem("max_ready"), sem("exp_ready"), sem("prob_ready")
        bias_set, lam_arg, lam_exp = sem("bias_set"), sem("lam_arg"), sem("lam_exp")
        sub_sq = sem("o_a_squares")
        mixed = sem("mixed_ready")
        route_exp, chosen, jobs_ready = (sem(n) for n in ("router_exp", "experts_chosen", "jobs_ready"))
        passed = sem("waits_passed")
        rows_stored, places, gather_set, result_set = (sem(n) for n in (
            "token_rows_stored", "places_ready", "gather_indices_set", "result_indices_set"))
        e_landed = [sem(f"expert_tile_in_{i}") for i in range(RING)]
        e_begun = sem("expert_tile_begun")
        e_done = sem("job_products_done")
        job_read, job_turned = sem("job_rows_in"), sem("job_rows_turned")
        silu_out, hid_ready = sem("silu_ready"), sem("hidden_ready")
        y_ready, y_stored = sem("job_results_ready"), sem("job_results_stored")
        gathered, combined = [sem(f"results_in_{i}") for i in range(ST)], sem("results_combined")
        x_normed = sem("x_normed")
        xc_ready, lru_y, lru_e, lru_cr, lru_m, lru_s = (sem(n) for n in (
            "xc_ready", "lru_abs", "lru_exp", "lru_c_ready", "lru_mult_arg", "lru_mult"))
        lru_act = sem("lru_activated")
        qk_sqr, qk_n, qk_rot = (sem(n) for n in ("qk_squares", "qk_normed", "qk_roped"))
        swa_max, swa_exp, swa_prob = sem("swa_max"), sem("swa_exp"), sem("swa_prob")
        wide_silu = sem("wide_silu")
        ret_qk, ret_sc, ret_or, ret_sqr, ret_rs, ret_yr = (sem(n) for n in (
            "ret_qk_ready", "ret_scores", "ret_o_ready", "ret_squares", "ret_rstd", "ret_y_ready"))
        stored = sem("stored")
        block = ctx.enter_context(nc.Block())

        def bank(p, n=512):
            return ps[:, p.bank, 0:n]

        def wide(p, n):
            return ps[:, p.bank:p.bank + len(p.banks), :].rearrange("p b n -> p (b n)")[:, 0:n]

        def plus(value, step, it):
            return value + it * step if it is not None and step else value

        def ready(eng, p, it=None):
            eng.wait_ge(done, plus(p.order + 1, p.order_step, it))

        def read(eng, p, it=None):
            eng.wait_ge(bank_free[p.bank], plus(p.released, p.free_step, it))

        def read_last(eng, p, turns):
            eng.wait_ge(bank_free[p.bank], p.released + p.free_step * (turns - 1))

        def bcast(ap, axis, n):
            a = ap.unsqueeze(axis)
            shape = list(a.shape)
            shape[axis] = n
            return a.to_broadcast(shape)

        def store(sp):
            for k in range(KT):
                read(sp, r["ffn_down", 1][k % 4], k // 4)
                sp.dma_start(d["out"][:, k], x[:, k, META:T2]).then_inc(stored, 16)
            sp.wait_ge(stored, 16 * KT)

        class Steps:

            def __init__(self, eng, step):
                self.eng, self.step, self.n, self.it, self.per = eng, step, 0, None, 0

            def link(self, ins):
                ins.then_inc(self.step, 1)
                self.n += 1
                self.eng.wait_ge(self.step, plus(self.n, self.per, self.it))

            def loop(self, it, per):
                self.it, self.per, self.first = it, per, self.n

            def end(self, turns):
                assert self.n - self.first == self.per, (self.n - self.first, self.per)
                self.n += self.per * (turns - 1)
                self.it, self.per = None, 0

        @block.sync
        def _(sp):
            mod1_end = START["mod1"] + 16
            mod2, mod2_end = START["mod2"], START["mod2"] + 32

            def read_by(t):
                if t < mod1_end:
                    return mod_read, t + 1
                if t < mod2:
                    return begun, t - mod1_end + 2
                if t < mod2_end:
                    return mod_read, 16 + t - mod2 + 1
                return begun, t - mod1_end - 32 + 3

            def load(n):
                if n >= RING:
                    sem_, value = read_by(n - RING)
                    sp.wait_ge(sem_, value)
                sp.dma_start(ring[:, n % RING, :], d["weights"][n]).then_inc(landed[n % RING], 16)

            def stream(first, last):
                turns = (last - first) // RING
                if turns:
                    with sp.Fori(0, turns) as it:
                        for s in range(RING):
                            n = first + s
                            sem_, value = read_by(n - RING)
                            sp.wait_ge(sem_, it * RING + value)
                            sp.dma_start(ring[:, n % RING, :], d["weights"][it * RING + n]).then_inc(landed[n % RING], 16)
                for n in range(first + turns * RING, last):
                    load(n)

            before = START["ab"]
            for n in range(RING):
                if n == 3:
                    sp.wait_ge(filter_rest_in, 16)
                load(n)
            stream(RING, mod1_end + RING)
            stream(mod1_end + RING, mod2 + RING)
            stream(mod2 + RING, before)
            slots = [(before + i) % RING for i in range(EXPERT_TILES)]
            for t in range(ST):
                read(sp, r["rows"][2 * t])
                read(sp, r["rows"][2 * t + 1])
                sp.dma_start(token_rows[t * P:(t + 1) * P, :], rows[:, t, :]).then_inc(rows_stored, 16)
            sp.wait_ge(jobs_ready, 1)
            n_jobs = sp.value_load(n_jobs_i[0:1, 0:1], min_val=MIN_JOBS, max_val=JOBS - 1)
            e = sp.value_load(job_i[0:1, 0:1], min_val=0, max_val=EXPERTS - 1)
            for i, s in enumerate(slots):
                if i == 4:
                    sp.wait_ge(job_read, 16)
                sp.dma_start(ring[:, s, :], d["experts"][e, i]).then_inc(e_landed[s], 16)
            with sp.Fori(1, n_jobs) as it:
                e = sp.value_load(job_i[0:1, bass.ds(it, 1)], min_val=0, max_val=EXPERTS - 1)
                for i, s in enumerate(slots):
                    sp.wait_ge(e_begun, it * EXPERT_TILES + (i - EXPERT_TILES + 2))
                    sp.dma_start(ring[:, s, :], d["experts"][e, i]).then_inc(e_landed[s], 16)
            sp.wait_ge(y_stored, n_jobs * 16)
            for t in range(ST):
                for c in range(2):
                    at = (c * ST + t) * P
                    sp.dma_start(got[:, c, t, :], results[at:at + P, :]).then_inc(gathered[t], 16)
            sp.wait_ge(e_done, n_jobs * 5 + 2)
            for n in range(before, before + RING):
                sp.dma_start(ring[:, n % RING, :], d["weights"][n]).then_inc(landed[n % RING], 16)
            stream(before + RING, N_TILES)
            store(sp)

        @block.gpsimd
        def _(pool):
            pool.dma_start(small[:, :], d["small"]).then_inc(small_in, 16)
            pool.dma_start(f_in[:, 0:FILTER_FIRST], d["filter"][:, 0:FILTER_FIRST]).then_inc(filter_in, 16)
            pool.dma_start(f_in[:, FILTER_FIRST:f_n], d["filter"][:, FILTER_FIRST:f_n]).then_inc(filter_rest_in, 16)
            pool.dma_start(const[:, :], d["const"]).then_inc(const_in, 16)
            pool.dma_start(x[:, :, META:T2], d["x"]).then_inc(x_in, 16)
            pool.dma_start(ctx_raw, d["ctx"]).then_inc(ctx_in, 16)
            pool.dma_start(x[:, :, 0:META], d["meta"]).then_inc(x_in, 16)
            for to, name in ((bias, "bias"), (rope_a, "rope_a"), (pool_inv, "pool_inv"), (pool_w, "pool_w")):
                pool.dma_start(to, d[name]).then_inc(att_in, 16)
            ready(pool, r["mod1"])
            pool.dma_start(dft, d["dft_half"]).then_inc(dft_in, 16)
            pool.wait_ge(jobs_ready, 1)
            n_jobs = pool.value_load(n_jobs_i[0:1, 0:1], min_val=MIN_JOBS, max_val=JOBS - 1)

            def waited():
                pool.tensor_tensor(pool_turn, ones[:, 0:1], ones[:, 0:1], ALU.mult).then_inc(passed, 1)

            def gather():
                pool.indirect_dma_start(out=job_in, out_offset=None, in_=token_rows,
                                        in_offset=bass.IndirectOffsetOnAxis(ap=gather_now, axis=0)).then_inc(job_read, 16)

            pool.wait_ge(const_in, 16)
            pool.wait_ge(rows_stored, 16 * ST)
            pool.wait_ge(gather_set, 1)
            waited()
            gather()
            with pool.Fori(0, n_jobs) as it:
                pool.wait_ge(e_done, it * 5 + 2)
                pool.wait_ge(gather_set, it + 2)
                pool.wait_ge(passed, it * 2 + 1)
                waited()
                gather()
                pool.wait_ge(y_ready, it * 2 + 2)
                pool.wait_ge(result_set, it + 1)
                pool.wait_ge(passed, it * 2 + 2)
                waited()
                pool.indirect_dma_start(out=results, out_offset=bass.IndirectOffsetOnAxis(ap=result_now, axis=0),
                                        in_=job_out.rearrange("p a b -> p (a b)"), in_offset=None).then_inc(y_stored, 16)
                pool.wait_ge(y_stored, it * 16 + 16)
            read(pool, r["moe_out"][-1])
            pool.dma_start(rope_q, d["rope_q"]).then_inc(swa_in, 16)
            pool.dma_start(swa_mask, d["swa_mask"]).then_inc(swa_in, 16)
            read_last(pool, r["ffn_down", 0][-1], 2)
            pool.dma_start(rope_r, d["rope_r"]).then_inc(ret_in, 16)
            pool.dma_start(decay_r, d["decay_r"]).then_inc(ret_in, 16)

        @block.tensor
        def _(pe):
            made = [0]
            tile_no = [0]

            def fill(p, it=None):
                for b, v in p.after:
                    pe.wait_ge(bank_free[b], plus(v, p.free_step, it))

            def finish(p, ins):
                assert p.order == made[0], (p.order, made[0])
                made[0] += 1
                ins.then_inc(done, 1)

            def weights(name, i, it=None):
                n = START[name] + i
                assert n == tile_no[0], (name, i, n, tile_no[0])
                tile_no[0] += 1
                pe.wait_ge(landed[n % RING], plus(16 * (n // RING + 1), 16, it))
                return ring[:, n % RING, :]

            def begin(ins):
                ins.then_inc(begun, 1)

            def linear(w, acts, products, pieces, before=None, it=None, tile_first=True):
                kt = w.shape[1]
                for j, (p, (at, n)) in enumerate(zip(products, pieces)):
                    fill(p, it)
                    for k in range(kt):
                        if before is not None and j == 0:
                            before(k)
                        m = pe.matmul(bank(p, n), w[:, k, :], acts[:, k, at:at + n], start=(k == 0), stop=(k == kt - 1))
                        if tile_first and j == 0 and k == 0:
                            begin(m)
                    finish(p, m)

            def k8(w):
                return w.rearrange("p (k m) -> p k m", k=KT)

            def mean_square(sq, products, pieces, base, it=None):
                for p in products:
                    fill(p, it)
                for k in range(KT):
                    pe.wait_ge(squares, base + k + 1)
                    for p, (at, n) in zip(products, pieces):
                        m = pe.matmul(bank(p, n), ones, sq[:, k, at:at + n], start=(k == 0), stop=(k == KT - 1))
                        if k == KT - 1:
                            finish(p, m)

            def summed_square(sq, products, pieces, count):
                pe.wait_ge(squares_summed, count)
                for p, (at, n) in zip(products, pieces):
                    fill(p)
                    finish(p, pe.matmul(bank(p, n), ones, sq[:, 0, at:at + n], start=True, stop=True))

            def filters():
                pe.wait_ge(filter_in, 16)
                p = r["f_h1"]
                fill(p)
                finish(p, pe.matmul(bank(p)[0:64], fil("w1")[0:33], fil("z")[0:33], start=True, stop=True))
                p = r["f_h2"]
                fill(p)
                pe.wait_ge(sin_ready, 1)
                finish(p, pe.matmul(bank(p)[0:64], fil("w2")[0:64], sin1[0:64], start=True, stop=True))
                pe.wait_ge(sin_ready, 2)
                pe.wait_ge(eps_set, 1)
                pe.wait_ge(filter_rest_in, 16)
                for i, p in enumerate(r["f_h3"]):
                    tt, half = i // 2, i % 2
                    fill(p)
                    finish(p, pe.matmul(bank(p), sin2[0:65, tt * P:(tt + 1) * P],
                                        fil("w3")[0:65, half * 512:(half + 1) * 512], start=True, stop=True))
                p = r["f_norm"]
                fill(p)
                pe.wait_ge(filter_sq, ST)
                pe.wait_ge(const_in, 16)
                for o in range(2):
                    for c in range(2):
                        for i in range(2 * ST):
                            m = pe.matmul(ps[:, p.bank, 2 * o + c:2 * o + c + 1], f_sq[:, i // 2, o, i % 2, c * P:(c + 1) * P],
                                          ones[:, 0:1], start=(i == 0), stop=(i == 2 * ST - 1))
                finish(p, m)
                pe.wait_ge(spec_in, 1)
                tile_no[0] += 16
                spectra(0, 2)

            def spectra(first, last):
                for kt in range(first, last):
                    w = weights("dft", kt).rearrange("p (c t k) -> p c t k", c=2, t=ST)
                    for c in range(2):
                        p = r["f_spec"][2 * kt + c]
                        fill(p)
                        for tt in range(ST):
                            m = pe.matmul(bank(p), w[:, c, tt, :], filt[:, tt, :, 0, :] if c == 0 else diff[:, tt],
                                          start=(tt == 0), stop=(tt == ST - 1))
                            if c == 0 and tt == 0:
                                begin(m)
                        finish(p, m)

            def modulation():
                sq = mix[:, :, :]
                mean_square(sq, [r["ms_x"]], [(0, S)], 0)
                mean_square(sq_c, [r["ms_c"]], [(0, C)], KT)
                p = r["mod1"]
                fill(p)
                pe.wait_ge(mod_read, 16)
                for i in range(16):
                    for v in range(2):
                        m = pe.matmul(ps[:, p.bank, 2 * i + v:2 * i + v + 1], acc1[:, i // 8, v, (i % 8) * P:(i % 8 + 1) * P],
                                      ones[:, 0:1], start=True, stop=True)
                finish(p, m)
                spectra(2, ST)

            def hyena():
                for i in range(6):
                    w = k8(weights("hyena", i))
                    linear(w, h1, [r["hy"][i]], [(C, S)], before=(lambda k: pe.wait_ge(h_ready, KT + k + 1)) if i == 0 else None)
                pe.wait_ge(dft_in, 16)
                for o in range(2):
                    for tt in range(ST):
                        p = r["hy_t", o][tt]
                        fill(p)
                        for c in range(2):
                            if o == 0:
                                pe.wait_ge(conv_ready, c + 1)
                            else:
                                pe.wait_ge(z_ready, c + 1)
                            sig = hy[:, c] if o == 0 else z1[:, c]
                            m = pe.transpose(ps[:, p.bank, c * P:(c + 1) * P], sig[:, tt * P:(tt + 1) * P], ident)
                        finish(p, m)
                    for kt in range(ST):
                        p = r["hy_f", o][kt]
                        fill(p)
                        for c in range(2):
                            for tt in range(ST):
                                if kt == 0 and c == 0:
                                    read(pe, r["hy_t", o][tt])
                                m = pe.matmul(ps[:, p.bank, c * 256:(c + 1) * 256], dft[:, c, tt, kt * P:(kt + 1) * P],
                                              sig_t[:, tt], start=(tt == 0), stop=(tt == ST - 1))
                        finish(p, m)
                    for c in range(2):
                        p = r["hy_i", o][c]
                        fill(p)
                        for kt in range(ST):
                            if c == 0:
                                pe.wait_ge(spec_ready, ST * o + kt + 1)
                            for part in range(2):
                                m = pe.matmul(bank(p), spec[:, part, kt, c * P:(c + 1) * P], dft[:, part, kt, :],
                                              start=(kt == 0 and part == 0), stop=(kt == ST - 1 and part == 1))
                        finish(p, m)

            def projections():
                for i in range(2):
                    linear(k8(weights("mixers", i)), h1, [r["aq"][i]], [(C, S)])
                for i in range(2):
                    linear(k8(weights("mixers", 2 + i)), h1, r["ak"][2 * i:2 * i + 2], [(C, S), (0, C)])
                for i in range(4):
                    p = r["rope"][i]
                    fill(p)
                    read(pe, r["aq"][i] if i < 2 else r["ak"][2 * (i - 2)])
                    finish(p, pe.matmul(bank(p), con("swap_a"), raw_a[:, i], start=True, stop=True))
                for i in range(2):
                    linear(k8(weights("mixers", 4 + i)), h1, [r["bq"][i]], [(C, S)])
                for i in range(2):
                    linear(k8(weights("mixers", 6 + i)), h1, r["bk"][2 * i:2 * i + 2], [(C, S), (0, C)])
                for i in range(2):
                    linear(k8(weights("mixers", 8 + i)), h1, [r["pool"][i]], [(C, S)])
                w = [weights("values", j).rearrange("p (k n) -> p k n", k=2) for j in range(4)]
                for t in range(NKT):
                    token_major(r["v"][t], lambda k, t=t: h1[:, k, t * P:(t + 1) * P], w, P, t == NKT - 1)
                for i in range(2):
                    p = r["pool_w"][i]
                    fill(p)
                    pe.wait_ge(att_in, 64)
                    pe.wait_ge(pooled, i + 1)
                    finish(p, pe.matmul(bank(p), pool_w[:, i, :], pool_y[:, i], start=True, stop=True))

            def token_major(p, acts, w, n_tok, last, it=None):
                fill(p, it)
                for k in range(KT):
                    m = pe.matmul(ps[0:n_tok, p.bank, :], acts(k), w[k // 2][:, k % 2, :], start=(k == 0), stop=(k == KT - 1))
                    if last and k % 2 == 0:
                        begin(m)
                finish(p, m)

            def attentions():
                def scores(i):
                    kind, h, t = UNITS[i]
                    for c, p in enumerate(r["scores", i]):
                        fill(p)
                        if kind == "A":
                            o, n, q, k = 64 * (h % 2) + 32 * c, 32, aq, ak
                            if i == 0 and c == 0:
                                pe.wait_ge(roped, 4)
                                read(pe, r["ak"][3])
                                read(pe, r["ak"][1])
                        else:
                            o, n, q, k = 64 * (h % 2), 64, bq, bk
                        for at, width in ((0, 512), (512, 256)):
                            m = pe.matmul(wide(p, NKEY)[:, at:at + width], q[o:o + n, h // 2, t * P:(t + 1) * P],
                                          k[o:o + n, h // 2, at:at + width], start=True, stop=True)
                            if i == 0 and c == 0 and at == 0:
                                begin(m)
                        finish(p, m)

                read(pe, r["bq"][1])
                for j in range(4):
                    read(pe, r["bk"][j])
                for j in range(NKT):
                    read(pe, r["v"][j])
                fill(r["mod2"])
                scores(0)
                for i, (kind, h, t) in enumerate(UNITS):
                    if i + 1 < len(UNITS):
                        scores(i + 1)
                    pe.wait_ge(prob_ready, i + 1)
                    for j, p in enumerate(r["T", i]):
                        fill(p)
                        for kt in range(4 * j, min(4 * j + 4, NKT)):
                            m = pe.transpose(ps[:, p.bank, (kt % 4) * P:(kt % 4 + 1) * P], prob[:, i % 2, 0, kt * P:(kt + 1) * P], ident)
                        finish(p, m)
                    p = r["PV", i]
                    fill(p)
                    o = DH * (h % 2)
                    for kt in range(NKT):
                        if kt % 4 == 0:
                            read(pe, r["T", i][kt // 4])
                        m = pe.matmul(ps[o:o + DH, p.bank, 0:P], vals[:, kt, 0 if kind == "A" else 1, h * DH:(h + 1) * DH],
                                      prob_t[:, i % 2, kt, :], start=(kt == 0), stop=(kt == NKT - 1))
                    finish(p, m)
                p = r["mod2"]
                for i in range(32):
                    if i % 8 == 0:
                        pe.wait_ge(mod_read, 16 + i + 8)
                    m = pe.matmul(ps[:, p.bank, i:i + 1], acc2[:, i // 8, (i % 8) * P:(i % 8 + 1) * P], ones[:, 0:1],
                                  start=True, stop=True)
                finish(p, m)
                tile_no[0] += 32
                for c, p in enumerate(r["subln"]):
                    fill(p)
                    pe.wait_ge(sub_sq, 1)
                    finish(p, pe.matmul(bank(p), head_ones, prob_sq[:, c], start=True, stop=True))

            def first_out():
                for b, v in r["before_w_out"]:
                    pe.wait_ge(bank_free[b], v)
                pe.wait_ge(mixed, MIXED_1)
                for i in range(8):
                    linear(k8(weights("w_out", i)), mix[:, :, 0:S], [r["w_out"][i]], [(0, S)])

            def router():
                summed_square(sq_a, [r["ms_2"]], [(0, S)], 1)
                p = r["router"]
                fill(p)
                rw = par("router_w").rearrange("p (k e) -> p k e", k=KT)
                for tt in range(ST):
                    for k in range(KT):
                        if tt == 0:
                            pe.wait_ge(h_ready, 2 * KT + k + 1)
                        m = pe.matmul(ps[:, p.bank, tt * EXPERTS:(tt + 1) * EXPERTS], h2[:, k, tt * P:(tt + 1) * P], rw[:, k, :],
                                      start=(k == 0), stop=(k == KT - 1))
                finish(p, m)
                for i, p in enumerate(r["rows"]):
                    fill(p)
                    for k in range(4):
                        f, t = 4 * (i % 2) + k, i // 2
                        m = pe.transpose(ps[:, p.bank, k * P:(k + 1) * P], h2[:, f, t * P:(t + 1) * P], ident)
                    finish(p, m)
                ranks()

            def ranks():
                p = r["rank"]
                fill(p)
                pe.wait_ge(chosen, 1)
                for t in range(ST):
                    for u in range(t + 1):
                        pe.matmul(ps[:, p.bank, t * EXPERTS:(t + 1) * EXPERTS], con("earlier") if u == t else ones, rt[11][:, u, :],
                                  start=(u == 0), stop=(u == t))
                for u in range(ST):
                    m = pe.matmul(ps[:, p.bank, 64:64 + EXPERTS], ones, rt[11][:, u, :], start=(u == 0), stop=(u == ST - 1))
                finish(p, m)
                p = r["slots"]
                fill(p)
                pe.wait_ge(places, 1)
                for i in range(2 * ST):
                    m = pe.matmul(ps[:, p.bank, 0:JOBS], slot_hot[:, i, :], job_hot[:, i, :], start=(i == 0), stop=(i == 2 * ST - 1))
                finish(p, m)

            def experts():
                for b, v in r["before_jobs"]:
                    pe.wait_ge(bank_free[b], v)
                pe.wait_ge(jobs_ready, 1)
                n_jobs = pe.value_load(n_jobs_i[0:1, 0:1], min_val=MIN_JOBS, max_val=JOBS - 1)
                slots = [(START["ab"] + i) % RING for i in range(EXPERT_TILES)]

                def turn():
                    for k in range(KT):
                        m = pe.transpose(ps[:, 2 + k // 4, (k % 4) * P:(k % 4 + 1) * P], job_in[:, k * P:(k + 1) * P], ident)
                        if k % 4 == 3:
                            m.then_inc(e_done, 1)

                pe.wait_ge(job_read, 16)
                turn()
                with pe.Fori(0, n_jobs) as it:
                    pe.wait_ge(job_turned, it * 2 + 2)
                    for side in range(2):
                        for m_ in range(4):
                            s = slots[4 * side + m_]
                            pe.wait_ge(e_landed[s], it * 16 + 16)
                            w = k8(ring[:, s, :])
                            for k in range(KT):
                                m = pe.matmul(ps[:, side, m_ * P:(m_ + 1) * P], w[:, k, :], job_t[:, k, :],
                                              start=(k == 0), stop=(k == KT - 1))
                                if k == 0:
                                    m.then_inc(e_begun, 1)
                        m.then_inc(e_done, 1)
                    pe.wait_ge(job_read, it * 16 + 32)
                    turn()
                    pe.wait_ge(hid_ready, it + 1)
                    for k in range(4):
                        s = slots[8 + k]
                        pe.wait_ge(e_landed[s], it * 16 + 16)
                        for half in range(2):
                            m = pe.matmul(ps[:, 4 + half, :], hid[:, k, :], ring[:, s, half * 512:(half + 1) * 512],
                                          start=(k == 0), stop=(k == 3))
                            if half == 0:
                                m.then_inc(e_begun, 1)
                    m.then_inc(e_done, 1)
                for p in r["moe_out"]:
                    fill(p)
                for t in range(ST):
                    pe.wait_ge(combined, t + 1)
                    for k, p in enumerate(r["moe_out"]):
                        m = pe.transpose(ps[:, p.bank, t * P:(t + 1) * P], both[:, t, k * P:(k + 1) * P], ident)
                        if t == ST - 1:
                            finish(p, m)

            def ab_in():
                mean_square(mix[:, :, :], [r["ms_f"]], [(0, S)], 3 * KT)
                mean_square(mix[:, :, :], r["ms_ab"], HALVES2, 4 * KT)
                for i in range(13):
                    linear(k8(weights("ab", i)), h2, r["ab"][2 * i:2 * i + 2], HALVES2,
                           before=(lambda k: pe.wait_ge(h_ready, 3 * KT + k + 1)) if i == 0 else None)
                w = k8(weights("ab_values", 0))
                for t, p in enumerate(r["ab_v"]):
                    at, n = swa_queries(t)
                    fill(p)
                    for k in range(KT):
                        m = pe.matmul(ps[0:n, p.bank, 0:P], h2[:, k, at:at + n], w[:, k, :], start=(k == 0), stop=(k == KT - 1))
                        if t == 0 and k == 0:
                            begin(m)
                    finish(p, m)

            def lru():
                for i in range(5):
                    pe.wait_ge(qk_sqr, i + 1)
                    for j, (at, n) in enumerate(HALVES2):
                        p = r["qk_ms"][2 * i + j]
                        fill(p)
                        finish(p, pe.matmul(bank(p, n), head_ones, qk_sq[:, i, at:at + n], start=True, stop=True))
                w = weights("lru_gates", 0).rearrange("p (i g m) -> p i g m", i=4, g=2)
                for i in range(4):
                    pe.wait_ge(xc_ready, i + 1)
                    for g in range(2):
                        for j, (at, n) in enumerate(HALVES2):
                            p = r["lru"][4 * i + 2 * g + j]
                            fill(p)
                            m = pe.matmul(bank(p, n), w[:, i, g, :], xc[:, i, at:at + n], start=True, stop=True)
                            finish(p, m)

            def swa():
                for i in range(5):
                    pe.wait_ge(qk_n, i + 1)
                    for j, (at, n) in enumerate(HALVES2):
                        p = r["qk_sw"][2 * i + j]
                        fill(p)
                        finish(p, pe.matmul(bank(p, n), con("swap_q"), qk[:, i, at:at + n], start=True, stop=True))
                for b, v in r["before_swa"]:
                    pe.wait_ge(bank_free[b], v)
                pe.wait_ge(qk_rot, 5)

                def scores(i):
                    t, a = GROUPS[i]
                    q0, nq = swa_queries(t)
                    p = r["swa_s", i]
                    fill(p)
                    for hh in range(4):
                        j, kv = 2 * a + hh // 2, hh % 2
                        o = DH * kv
                        for col, key, n in swa_keys(t):
                            m = pe.matmul(ps[0:nq, hh, col:col + n], qk[o:o + DH, j, q0:q0 + nq], qk[o:o + DH, 4, key:key + n],
                                          start=True, stop=True)
                    finish(p, m)

                scores(0)
                for i, (t, a) in enumerate(GROUPS):
                    if i + 1 < len(GROUPS):
                        scores(i + 1)
                    q0, nq = swa_queries(t)
                    pe.wait_ge(swa_prob, i + 1)
                    for hh, p in enumerate(r["swa_t", i]):
                        fill(p)
                        for c, (col, n, _) in enumerate(swa_chunks(t)):
                            m = pe.transpose(ps[0:n, p.bank, c * P:c * P + nq], prob2[0:nq, i % 2, hh, col:col + n], ident[0:nq, 0:nq])
                        finish(p, m)
                    p = r["swa_o", i]
                    fill(p)
                    chunks = swa_chunks(t)
                    for hh in range(4):
                        if hh < 2:
                            read(pe, r["swa_t", i][2 + hh])
                        o = DH * (hh % 2)
                        for c, (col, n, vt) in enumerate(chunks):
                            m = pe.matmul(ps[o:o + DH, p.bank, (hh // 2) * P:(hh // 2) * P + nq], val2[0:n, vt, o:o + DH],
                                          prob2_t[0:n, i % 2, hh, c * P:c * P + nq], start=(c == 0), stop=(c == len(chunks) - 1))
                    finish(p, m)

            def ab_out():
                for b, v in r["before_ab_out"]:
                    pe.wait_ge(bank_free[b], v)
                pe.wait_ge(mixed, MIXED_2)
                for i in range(8):
                    w = k8(weights("ab_out", i))
                    linear(w, mix[:, :, :], r["ab_out"][2 * i:2 * i + 2], HALVES2, tile_first=True)

            def ffn(n):
                pieces = HALVES2 if n == 0 else [(0, S)]
                np_ = len(pieces)
                name = f"ffn{n}"
                summed_square(sq_a if n == 0 else mix[:, :, :], r["ffn_ms", n], pieces, 2 if n == 0 else 4)
                for b, v in r["before_ffn", n]:
                    pe.wait_ge(bank_free[b], v)
                for k in range(KT):
                    pe.wait_ge(h_ready, (4 if n == 0 else 6) * KT + k + 1)
                with pe.Fori(0, 3) as it:
                    for i in range(12):
                        linear(k8(weights(name, i, it)), h2, r["ffn_loop", n][np_ * i:np_ * (i + 1)], pieces, it=it)
                made[0] += 12 * np_ * 2
                tile_no[0] += 24
                for i in range(8):
                    linear(k8(weights(name, 36 + i)), h2, r["ffn_rest", n][np_ * i:np_ * (i + 1)], pieces)
                for b, v in r["before_down", n]:
                    pe.wait_ge(bank_free[b], v)
                with pe.Fori(0, 2) as it:
                    for m_ in range(4):
                        w = [k8(weights(name, 44 + 3 * m_ + s, it)) for s in range(3)]
                        for j, (at, n_) in enumerate(pieces):
                            p = r["ffn_down", n][np_ * m_ + j]
                            fill(p, it)
                            for k in range(FFT):
                                m = pe.matmul(bank(p, n_), w[k // 8][:, k % 8, :], act_w[:, k, at:at + n_],
                                              start=(k == 0), stop=(k == FFT - 1))
                                if j == np_ - 1 and k % 8 == 0:
                                    begin(m)
                            finish(p, m)
                made[0] += 4 * np_
                tile_no[0] += 12

            def retention():
                summed_square(mix[:, :, :], r["ms_ret"], HALVES2, 3)
                for b, v in r["before_ret"]:
                    pe.wait_ge(bank_free[b], v)
                for k in range(KT):
                    pe.wait_ge(h_ready, 5 * KT + k + 1)
                with pe.Fori(0, RET_HEADS) as it:
                    for i in range(2):
                        linear(k8(weights("ret", i, it)), h2, [r["ret", "q"][i]], [(META, S)], it=it)
                    for i in range(2):
                        linear(k8(weights("ret", 2 + i, it)), h2, r["ret", "k"][2 * i:2 * i + 2], HALVES2, it=it)
                    w = [weights("ret", 4 + j, it).rearrange("p (k n) -> p k n", k=2) for j in range(4)]
                    for t, p in enumerate(r["ret", "v"]):
                        n = P if t < 4 else META
                        token_major(p, lambda k, t=t, n=n: h2[:, k, t * P:t * P + n], w, n, t == 4, it)
                    for i in range(4):
                        linear(k8(weights("ret", 8 + i, it)), h2, [r["ret", "g"][i]], [(META, S)], it=it)
                    pe.wait_ge(ret_qk, it + 1)
                    for t, p in enumerate(r["ret", "s"]):
                        n = P if t < 4 else META
                        at = max(P * t - META, 0)
                        fill(p, it)
                        for c in range(2):
                            m = pe.matmul(ps[0:n, p.bank, at:S], ret_k[:, c, t * P:t * P + n], ret_q[:, c, at:S],
                                          start=(c == 0), stop=(c == 1))
                        finish(p, m)
                    assert r["ret", "o"][0].bank == r["ret", "s"][0].bank == r["ret", "v"][4].bank
                    for i, p in enumerate(r["ret", "o"]):
                        fill(p, it)
                        for t in range(5):
                            n = P if t < 4 else META
                            at = max(P * t - META, 0)
                            if i == 0 and t > 0:
                                read(pe, r["ret", "s"][t], it)
                            m = pe.matmul(ps[:, p.bank, at:S], ret_v[0:n, t, i * P:(i + 1) * P], ret_s[0:n, t, at:S],
                                          start=(t == 0), stop=(t == 4), skip_group_check=True)
                        finish(p, m)
                    p, = r["ret", "ms"]
                    fill(p, it)
                    for i in range(4):
                        pe.wait_ge(ret_sqr, it * 4 + i + 1)
                        m = pe.matmul(bank(p), ones, ret_sq[:, i], start=(i == 0), stop=(i == 3))
                    finish(p, m)
                made[0] += 25 * (RET_HEADS - 1)
                tile_no[0] += 12 * (RET_HEADS - 1)

            def ret_out():
                pe.wait_ge(ret_yr, RET_HEADS)
                for i in range(8):
                    w = [k8(weights("ret_out", 2 * i + s)) for s in range(2)]
                    p = r["ret_out"][i]
                    fill(p)
                    for k in range(16):
                        m = pe.matmul(bank(p), w[k // 8][:, k % 8, :], ret_y[:, k], start=(k == 0), stop=(k == 15))
                        if k % 8 == 0:
                            begin(m)
                    finish(p, m)

            filters()
            modulation()
            hyena()
            projections()
            attentions()
            first_out()
            router()
            experts()
            ab_in()
            lru()
            swa()
            ab_out()
            ffn(0)
            retention()
            ret_out()
            ffn(1)

        @block.scalar
        def _(act):
            me = Steps(act, act_step)

            def squares_of(src, dst, n, before=None):
                for k in range(KT):
                    if before is not None:
                        before(k)
                    act.activation(dst[:, k, 0:n], src[:, k], ACT.Square, scale=D ** -0.5).then_inc(squares, 1)

            def root(p_list, pieces, out):
                for p, (at, n) in zip(p_list, pieces):
                    ready(act, p)
                    act.activation(out[:, at:at + n], bank(p, n), ACT.Ln, bias=eps).then_inc(bank_free[p.bank], 1)
                for p, (at, n) in zip(p_list, pieces):
                    read(act, p)
                    act.activation(out[:, at:at + n], out[:, at:at + n], ACT.Exp, scale=-0.5).then_inc(rstd_ready, 1)

            def copy(p, out, src, scale=1.0, it=None):
                ready(act, p, it)
                act.activation(out, src, ACT.Copy, scale=scale).then_inc(bank_free[p.bank], 1)

            def filters():
                act.wait_ge(small_in, 16)
                act.activation(silu_c, par("c").rearrange("p (k v) -> p k v", k=KT), ACT.Silu).then_inc(silu_ready, 1)
                for i, out in enumerate((sin1, sin2)):
                    act.wait_ge(sin_arg, i + 1)
                    act.activation(out[0:64], arg[0:64, 0], ACT.Sin).then_inc(sin_ready, 1)
                for tt in range(ST):
                    read(act, r["f_h3"][2 * tt])
                    read(act, r["f_h3"][2 * tt + 1])
                    act.activation(f_sq[:, tt], filt[:, tt], ACT.Square).then_inc(filter_sq, 1)
                p = r["f_norm"]
                ready(act, p)
                act.wait_ge(eps_set, 1)
                act.activation(conv_rs, ps[:, p.bank, 0:4], ACT.Ln, bias=eps).then_inc(bank_free[p.bank], 1)
                read(act, p)
                act.activation(conv_rs, conv_rs, ACT.Exp, scale=-0.5).then_inc(filter_rs, 1)
                act.wait_ge(x_in, 32)
                squares_of(x[:, :, META:T2], mix, S)
                act.wait_ge(ctx_in, 16)
                squares_of(ctx_raw, sq_c, C)
                spectra(0, 2)

            def spectra(first, last):
                for i, p in enumerate(r["f_spec"]):
                    if first <= i // 2 < last:
                        copy(p, (kc, ks)[i % 2][:, i // 2], bank(p).rearrange("p (o c) -> p o c", o=2), scale=1.0 / S)

            def modulation():
                root([r["ms_x"]], [(0, S)], rstd)
                root([r["ms_c"]], [(0, C)], rstd[:, T2:T2 + C])
                act.wait_ge(mod1_ready, 1)
                for j, k in enumerate([7, 6, 5, 4, 3, 2, 1, 0]):
                    act.wait_ge(scaled, KT)
                    act.activation(h1[:, k, 0:C], h1[:, k, 0:C], ACT.Identity, bias=mod1[:, k, 1:2]).then_inc(h_ready, 1)
                for k in range(KT):
                    act.wait_ge(scaled, KT + k + 1)
                    act.activation(h1[:, k, C:], h1[:, k, C:], ACT.Identity, bias=mod1[:, k, 0:1]).then_inc(h_ready, 1)
                spectra(2, ST)

            def hyena():
                for i in range(6):
                    copy(r["hy"][i], hy_raw[:, i, 1:S + 1], bank(r["hy"][i]))
                for o in range(2):
                    for tt, p in enumerate(r["hy_t", o]):
                        if o == 0 and tt == 0:
                            act.wait_ge(conv_ready, 6)
                        copy(p, sig_t[:, tt], bank(p, 256))

            def projections():
                scale = 32 ** -0.5
                act.wait_ge(mixed, 2)
                for i in range(2):
                    copy(r["aq"][i], raw_a[:, i], bank(r["aq"][i]), scale)
                for i in range(2):
                    copy(r["ak"][2 * i], raw_a[:, 2 + i], bank(r["ak"][2 * i]))
                    copy(r["ak"][2 * i + 1], ak[:, i, 0:C], bank(r["ak"][2 * i + 1], C))
                for i in range(2):
                    copy(r["bq"][i], bq[:, i], bank(r["bq"][i]), DH ** -0.5)
                for i in range(2):
                    copy(r["bk"][2 * i], bk[:, i, C:], bank(r["bk"][2 * i]))
                    copy(r["bk"][2 * i + 1], bk[:, i, 0:C], bank(r["bk"][2 * i + 1], C))
                for i in range(2):
                    copy(r["pool"][i], pool_u[:, i, 8:8 + S], bank(r["pool"][i]))
                for t in range(NKT):
                    copy(r["v"][t], vals[:, t], bank(r["v"][t]).rearrange("p (a c) -> p a c", a=2))

            def attentions():
                act.wait_ge(lam_arg, 1)
                act.activation(lam_t[:, 66:68], lam_t[:, 64:66], ACT.Exp).then_inc(lam_exp, 1)
                unit = [0]

                def exps(i):
                    for c, p in enumerate(r["scores", i]):
                        unit[0] += 1
                        act.wait_ge(max_ready, unit[0])
                        act.activation(prob[:, i % 2, c], wide(p, NKEY), ACT.Exp, bias=neg_max[:, i % 2, c:c + 1],
                                       accum_out=row_sum[:, i % 2, c:c + 1]).then_inc(bank_free[p.bank], 1)

                exps(0)
                for i in range(len(UNITS)):
                    for j, p in enumerate(r["T", i]):
                        n = 4 if j == 0 else 2
                        copy(p, prob_t[:, i % 2, 4 * j:4 * j + n], bank(p, n * P).rearrange("p (k q) -> p k q", k=n))
                    if i + 1 < len(UNITS):
                        exps(i + 1)
                read(act, r["PV", HEADS * ST - 1])
                act.activation(prob_sq, o_a, ACT.Square, scale=DH ** -0.5).then_inc(sub_sq, 1)
                root(r["subln"], [(0, S), (S, S)], sub_rs_t)

            def router():
                squares_of(x[:, :, META:T2], sq_a, S, lambda k: read(act, r["w_out"][k]))
                root([r["ms_2"]], [(0, S)], rstd)
                act.wait_ge(mod2_ready, 1)
                for k in range(KT):
                    act.wait_ge(scaled, 2 * KT + k + 1)
                    act.activation(h2[:, k, 0:S], h2[:, k, 0:S], ACT.Identity, bias=mod2[:, 8 + k:9 + k]).then_inc(h_ready, 1)
                read(act, r["router"])
                act.activation(rt[1], rt[0], ACT.Exp).then_inc(route_exp, 1)
                for i, p in enumerate(r["rows"]):
                    copy(p, rows[:, i // 2, (i % 2) * 512:(i % 2 + 1) * 512], bank(p))

            def experts():
                act.wait_ge(jobs_ready, 1)
                n_jobs = act.value_load(n_jobs_i[0:1, 0:1], min_val=MIN_JOBS, max_val=JOBS - 1)

                def turned(at, it):
                    for h in range(2):
                        act.wait_ge(e_done, plus(at + h, 5, it))
                        act.activation(job_t[:, 4 * h:4 * h + 4], ps[:, 2 + h, :].rearrange("p (k t) -> p k t", k=4), ACT.Copy)\
                           .then_inc(job_turned, 1)

                turned(1, None)
                with act.Fori(0, n_jobs) as it:
                    act.wait_ge(e_done, it * 5 + 3)
                    act.activation(silu_t, ps[:, 0, :], ACT.Silu).then_inc(silu_out, 1)
                    turned(5, it)
                    act.wait_ge(e_done, it * 5 + 7)
                    for h in range(2):
                        act.activation(job_out[:, h], ps[:, 4 + h, :], ACT.Copy).then_inc(y_ready, 1)

            def ab_in():
                squares_of(x[:, :, META:T2], mix, S, lambda k: read(act, r["moe_out"][k]))
                root([r["ms_f"]], [(0, S)], rstd)
                squares_of(x[:, :, :], mix, T2, lambda k: act.wait_ge(x_normed, k + 1))
                root(r["ms_ab"], HALVES2, rstd)
                for i in range(13):
                    for j, (at, n) in enumerate(HALVES2):
                        p = r["ab"][2 * i + j]
                        if i < 4:
                            copy(p, xr[:, i, 3 + at:3 + at + n], bank(p, n))
                        elif i < 8:
                            ready(act, p)
                            act.activation(gate[:, i - 4, at:at + n], bank(p, n), ACT.Gelu_apprx_tanh).then_inc(bank_free[p.bank], 1)
                        else:
                            copy(p, qk[:, i - 8, at:at + n], bank(p, n))
                    if i >= 8:
                        read(act, r["ab"][2 * i])
                        read(act, r["ab"][2 * i + 1])
                        act.activation(qk_sq[:, i - 8], qk[:, i - 8], ACT.Square, scale=DH ** -0.5).then_inc(qk_sqr, 1)
                for t, p in enumerate(r["ab_v"]):
                    n = swa_queries(t)[1]
                    copy(p, val2[0:n, t], ps[0:n, p.bank, 0:P])
                root(r["qk_ms"], [(T2 * i + at, n) for i in range(5) for at, n in HALVES2],
                     qk_rs.rearrange("p i t -> p (i t)"))

            def lru():
                act.wait_ge(lru_y, 1)
                act.activation(lru_t[:, 4:8], lru_t[:, 0:4], ACT.Exp, scale=-1.0).then_inc(lru_e, 1)
                for i in range(4):
                    for g, (out, b) in enumerate(((g_r, "b_a"), (g_i, "b_i"))):
                        for j, (at, n) in enumerate(HALVES2):
                            p = r["lru"][4 * i + 2 * g + j]
                            ready(act, p)
                            act.activation(out[:, i, at:at + n], bank(p, n), ACT.Sigmoid, bias=par(b)[:, i:i + 1])\
                               .then_inc(bank_free[p.bank], 1)
                for p in r["lru"][-8:]:
                    read(act, p)
                act.wait_ge(lru_cr, 1)
                for i in range(4):
                    act.activation(g_a[:, i], g_r[:, i], ACT.Exp, scale=lru_c[:, i:i + 1]).then_inc(lru_act, 1)
                for i in range(4):
                    act.activation(g_r[:, i], g_r[:, i], ACT.Tanh, scale=lru_c[:, i:i + 1]).then_inc(lru_act, 1)
                for i in range(4):
                    act.wait_ge(lru_m, i + 1)
                    act.activation(g_m[:, i], g_m[:, i], ACT.Sqrt, scale=-1.0).then_inc(lru_s, 1)

            def swa():
                swa_exps(0)
                for i, (t, a) in enumerate(GROUPS):
                    nq = swa_queries(t)[1]
                    n = len(swa_chunks(t))
                    for hh, p in enumerate(r["swa_t", i]):
                        ready(act, p)
                        to = prob2_t[:, i % 2, hh, :].rearrange("p (c q) -> p c q", c=3)
                        of = ps[:, p.bank, 0:384].rearrange("p (c q) -> p c q", c=3)
                        last = act.activation(to[0:META, 0, 0:nq], of[0:META, 0, 0:nq], ACT.Copy)
                        if n > 1:
                            last = act.activation(to[:, 1:n, 0:nq], of[:, 1:n, 0:nq], ACT.Copy)
                        last.then_inc(bank_free[p.bank], 1)
                    if i + 1 < len(GROUPS):
                        swa_exps(i + 1)

            def swa_exps(i):
                t, a = GROUPS[i]
                nq, (col, _, n) = swa_queries(t)[1], swa_keys(t)[-1]
                p = r["swa_s", i]
                act.wait_ge(swa_max, i + 1)
                act.activation(sink_e[0:nq, i % 2], sink_d[0:nq, i % 2], ACT.Exp).then_inc(swa_exp, 1)
                for hh in range(4):
                    ins = act.activation(prob2[0:nq, i % 2, hh, 0:col + n], ps[0:nq, hh, 0:col + n], ACT.Exp,
                                         bias=neg_max[0:nq, i % 2, hh:hh + 1], accum_out=row_sum[0:nq, i % 2, hh:hh + 1])
                ins.then_inc(bank_free[p.bank], 1)

            def ffn(n):
                t0, pieces = (0, HALVES2) if n == 0 else (META, [(0, S)])
                np_ = len(pieces)
                last = r["ab_out"] if n == 0 else r["ret_out"]

                def whole(k):
                    for p in last[np_ * k:np_ * (k + 1)]:
                        read(act, p)

                squares_of(x[:, :, t0:T2], sq_a if n == 0 else mix, T2 if n == 0 else S, whole)
                root(r["ffn_ms", n], pieces, rstd)
                with act.Fori(0, 3) as it:
                    for i in range(6):
                        for j, (at, w) in enumerate(pieces):
                            p = r["ffn_loop", n][np_ * 2 * i + j]
                            ready(act, p, it)
                            act.activation(silu_w[:, i, at:at + w], bank(p, w), ACT.Silu).then_inc(bank_free[p.bank], 1)
                for i in range(4):
                    for j, (at, w) in enumerate(pieces):
                        p = r["ffn_rest", n][np_ * 2 * i + j]
                        ready(act, p)
                        act.activation(silu_w[:, i, at:at + w], bank(p, w), ACT.Silu).then_inc(bank_free[p.bank], 1)

            def retention():
                def whole(k):
                    for p in r["ffn_down", 0][2 * (k % 4):2 * (k % 4) + 2]:
                        read(act, p, k // 4)

                squares_of(x[:, :, :], mix, T2, whole)
                root(r["ms_ret"], HALVES2, rstd)
                with act.Fori(0, RET_HEADS) as it:
                    for t, p in enumerate(r["ret", "v"]):
                        n = P if t < 4 else META
                        copy(p, ret_v[0:n, t], ps[0:n, p.bank, :], it=it)
                    for i, p in enumerate(r["ret", "g"]):
                        ready(act, p, it)
                        act.activation(ret_g[:, i], bank(p), ACT.Silu).then_inc(bank_free[p.bank], 1)
                    for i, p in enumerate(r["ret", "o"]):
                        copy(p, ret_o[:, i], bank(p), it=it)
                        read(act, p, it)
                        act.activation(ret_sq[:, i], ret_o[:, i], ACT.Square).then_inc(ret_sqr, 1)
                    p, = r["ret", "ms"]
                    ready(act, p, it)
                    act.activation(rstd[:, 0:S], bank(p), ACT.Ln, bias=eps, scale=1.0 / 512).then_inc(bank_free[p.bank], 1)
                    read(act, p, it)
                    act.activation(rstd[:, 0:S], rstd[:, 0:S], ACT.Exp, scale=-0.5).then_inc(ret_rs, 1)

            filters()
            modulation()
            hyena()
            projections()
            attentions()
            router()
            experts()
            ab_in()
            lru()
            swa()
            ffn(0)
            retention()
            ffn(1)

        @block.vector
        def _(dve):
            me = Steps(dve, dve_step)
            link = me.link
            tt_ = dve.tensor_tensor
            ts = dve.tensor_scalar
            stt = dve.scalar_tensor_tensor

            def add_square(sq, k, base, w):
                dve.wait_ge(squares, base + k + 1)
                if k > 0:
                    ins = tt_(sq[:, 0, 0:w], sq[:, 0, 0:w], sq[:, k, 0:w], ALU.add)
                    if k == KT - 1:
                        ins.then_inc(squares_summed, 1)
                    else:
                        link(ins)

            def norm(gain, src, dst, n, rs, sem_, root):
                dve.wait_ge(rstd_ready, ROOTS[root])
                for k in range(KT):
                    stt(dst[:, k, 0:n], src[:, k, 0:n], gain[:, k:k + 1], rs, ALU.mult, ALU.mult).then_inc(sem_, 1)

            first_sum = [0]

            def mod_terms(first, last):
                for i in range(first, last):
                    n = START["mod1"] + i if i < 16 else START["mod2"] + i - 16
                    w = ring[:, n % RING, :]
                    part, k = i // 8, i % 8
                    dve.wait_ge(landed[n % RING], 16 * (n // RING + 1))
                    for v in range(2 if i < 16 else 1):
                        acc = acc1[:, part, v] if i < 16 else acc2[:, part - 2]
                        last_v = v == 1 or i >= 16
                        if k == 0:
                            ins = ts(acc, w, silu_c[:, k, v:v + 1], None, ALU.mult)
                        else:
                            if last_v:
                                dve.wait_ge(mod_read, i)
                            else:
                                dve.wait_ge(dve_step, first_sum[0])
                            ins = stt(acc, w, silu_c[:, k, v:v + 1], acc, ALU.mult, ALU.add)
                        if last_v:
                            ins.then_inc(mod_read, 1)
                        else:
                            ins.then_inc(dve_step, 1)
                            me.n += 1
                            first_sum[0] = me.n

            def filters():
                dve.memset(eps, EPS)
                dve.memset(sin2[64:65], 1.0).then_inc(eps_set, 1)
                dve.wait_ge(small_in, 16)
                dve.wait_ge(silu_ready, 1)
                for i, p in enumerate((r["f_h1"], r["f_h2"])):
                    b = par(("f_b1", "f_b2")[i])
                    a, n, t = (arg[0:64, j] for j in range(3))
                    ready(dve, p)
                    if i == 1:
                        dve.wait_ge(sin_ready, 1)
                    ts(a, bank(p)[0:64], b[0:64], None, ALU.add).then_inc(bank_free[p.bank], 1)
                    read(dve, p)
                    link(ts(n, a, 1.0 / (2 * math.pi), ROUND, ALU.mult, ALU.add))
                    link(ts(n, n, ROUND, None, ALU.subtract))
                    link(stt(t, n, -TWO_PI_HI, a, ALU.mult, ALU.add))
                    link(stt(t, n, -TWO_PI_LO, t, ALU.mult, ALU.add))
                    ts(a, t, PI_BELOW, -PI_BELOW, ALU.min, ALU.max).then_inc(sin_arg, 1)
                    mod_terms(i, i + 1)
                decay = fil("decay").rearrange("p (t c) -> p t c", t=ST)
                for i, p in enumerate(r["f_h3"]):
                    tt, o = i // 2, i % 2
                    ready(dve, p)
                    tt_(filt[:, tt, o], bank(p).rearrange("p (d c) -> p d c", d=2), bcast(decay[:, tt], 1, 2), ALU.mult)\
                        .then_inc(bank_free[p.bank], 1)
                    if o == 1:
                        mod_terms(2 + tt, 3 + tt)
                dve.wait_ge(filter_sq, ST)
                link(dve.memset(filt[0:1, 0, :, 1, :], 0.0))
                for tt in range(ST):
                    ins = tt_(diff[:, tt], filt[:, tt, :, 0, :], filt[:, tt, :, 1, :], ALU.subtract)
                link(ins)
                for tt in range(ST):
                    ins = tt_(filt[:, tt, :, 0, :], filt[:, tt, :, 0, :], filt[:, tt, :, 1, :], ALU.add)
                ins.then_inc(spec_in, 1)
                mod_terms(6, 16)

            def modulation():
                p = r["mod1"]
                ready(dve, p)
                tt_(mod1, ps[:, p.bank, 0:32].rearrange("p (m v) -> p m v", m=16), bcast(par("ada_b")[:, 0:16], 2, 2), ALU.add)\
                    .then_inc(bank_free[p.bank], 1)
                read(dve, p)
                stt(gain1, mod1[:, 8:16], 1.0, bcast(par("norm1_g"), 2, 2), ALU.add, ALU.mult).then_inc(mod1_ready, 1)
                dve.wait_ge(mod1_ready, 1)
                dve.wait_ge(rstd_ready, ROOTS["ms_c"])
                for j, k in enumerate(range(KT - 1, -1, -1)):
                    stt(h1[:, k, 0:C], ctx_raw[:, k], gain1[:, k, 1:2], rstd[:, T2:T2 + C], ALU.mult, ALU.mult).then_inc(scaled, 1)
                    dve.wait_ge(scaled, j + 1)
                norm(gain1[:, :, 0], x[:, :, META:T2], h1[:, :, C:], S, rstd[:, 0:S], scaled, "ms_x")

            def hyena():
                sw = par("short_w").rearrange("p (i j) -> p i j", i=6)
                sbias = par("short_b")
                ready(dve, r["hy"][0])
                for i in range(6):
                    dve.memset(hy_raw[:, i, 0:1], 0.0)
                    ins = dve.memset(hy_raw[:, i, S + 1:S + 2], 0.0)
                link(ins)
                for i in range(6):
                    c = (i + 4) % 6
                    read(dve, r["hy"][i])
                    out = hy[:, i]
                    link(ts(out, hy_raw[:, i, 1:S + 1], sw[:, c, 1:2], sbias[:, c:c + 1], ALU.mult, ALU.add))
                    link(stt(out, hy_raw[:, i, 0:S], sw[:, c, 0:1], out, ALU.mult, ALU.add))
                    stt(out, hy_raw[:, i, 2:S + 2], sw[:, c, 2:3], out, ALU.mult, ALU.add).then_inc(conv_ready, 1)
                dve.wait_ge(conv_ready, 6)
                dve.wait_ge(filter_rs, 1)
                skip = par("skip").rearrange("p (o c) -> p o c", o=2)
                for q in r["f_spec"]:
                    read(dve, q)
                for o in range(2):
                    for kt, p in enumerate(r["hy_f", o]):
                        ready(dve, p)
                        u = ps[:, p.bank, :].rearrange("p (s c) -> p s c", s=2)
                        tt_(prod_t[:, 0], u, bcast(kc[:, kt, o], 1, 2), ALU.mult)
                        tt_(prod_t[:, 1], u, bcast(ks[:, kt, o], 1, 2), ALU.mult).then_inc(bank_free[p.bank], 1)
                        read(dve, p)
                        tt_(spec[:, 0, kt], prod_t[:, 0, 0], prod_t[:, 1, 1], ALU.subtract)
                        tt_(spec[:, 1, kt], prod_t[:, 0, 1], prod_t[:, 1, 0], ALU.add).then_inc(spec_ready, 1)
                        dve.wait_ge(spec_ready, ST * o + kt + 1)
                    for c, p in enumerate(r["hy_i", o]):
                        sig = hy[:, c] if o == 0 else z1[:, c]
                        ready(dve, p)
                        ts(y_t, bank(p), conv_rs[:, 2 * o + c:2 * o + c + 1], None, ALU.mult).then_inc(bank_free[p.bank], 1)
                        read(dve, p)
                        link(stt(y_t, sig, skip[:, o, c:c + 1], y_t, ALU.mult, ALU.add))
                        out = z1[:, c] if o == 0 else mix[:, 6 + c, 0:S]
                        tt_(out, y_t, hy[:, 2 + 2 * o + c], ALU.mult).then_inc(z_ready if o == 0 else mixed, 1)
                        dve.wait_ge(z_ready if o == 0 else mixed, c + 1)

            def projections():
                dve.wait_ge(mixed, 2)
                dve.wait_ge(att_in, 64)
                dve.memset(pool_u[:, :, 0:8], 0.0)
                link(dve.memset(pool_u[:, :, S + 8:S + 16], 0.0))
                for i in range(4):
                    p = r["rope"][i]
                    to = aq[:, i] if i < 2 else ak[:, i - 2, C:]
                    read(dve, r["aq"][i] if i < 2 else r["ak"][2 * (i - 2)])
                    ready(dve, p)
                    tt_(y_t, bank(p), rope_a[:, 1], ALU.mult).then_inc(bank_free[p.bank], 1)
                    link(tt_(to, raw_a[:, i], rope_a[:, 0], ALU.mult))
                    tt_(to, to, y_t, ALU.add).then_inc(roped, 1)
                    dve.wait_ge(roped, i + 1)
                for i in range(2):
                    read(dve, r["pool"][i])
                src = pool_u
                for j, w in enumerate((2, 4, 8, 16)):
                    n = S + 16 - w + 1
                    link(tt_(pool_s[j][:, :, 0:n], src[:, :, 0:n], src[:, :, w // 2:w // 2 + n], ALU.add))
                    src = pool_s[j]
                for i in range(2):
                    for g in range(2):
                        w = 2 << (2 * i + g)
                        o = DH * g
                        mean = pool_s[2 * i + g][o:o + DH, i, 8 - w // 2:8 - w // 2 + S]
                        link(tt_(mean, mean, pool_inv[o:o + DH, i], ALU.mult))
                        ins = tt_(pool_y[o:o + DH, i], mean, pool_u[o:o + DH, i, 8:8 + S], ALU.subtract)
                    ins.then_inc(pooled, 1)
                for i, p in enumerate(r["pool_w"]):
                    ready(dve, p)
                    ts(mix[:, 4 + i, 0:S], bank(p), par("pool_scale")[:, i:i + 1], None, ALU.mult).then_inc(bank_free[p.bank], 1)

            def attentions():
                link(dve.tensor_tensor_scan(lane, ones, ones, -1.0, ALU.mult, ALU.add))
                link(dve.tensor_reduce(partition, con("earlier"), AX_X, ALU.add))
                link(ts(partition, partition, -1.0, float(P - 1), ALU.mult, ALU.add))
                link(ts(unused_row, partition, float(2 * S + 1), None, ALU.add))
                link(ts(result_no, lane[:, 0:2 * ST], float(P), 1.0, ALU.mult, ALU.add))
                link(ts(result_no, result_no, partition, None, ALU.add))
                ready(dve, r["v"][-1])
                for h in range(HEADS):
                    ins = tt_(bias[:, h], bias[:, h], bcast(con("win_mask"), 1, 15), ALU.add)
                link(ins)
                al = par("a_lambda").rearrange("p (v c) -> p v c", v=4)
                link(tt_(lam_t[:, 0:64].rearrange("p (a c) -> p a c", a=2), al[:, 0:4:2], al[:, 1:4:2], ALU.mult))
                dve.tensor_reduce(lam_t[:, 64:66], lam_t[:, 0:64].rearrange("p (a c) -> p a c", a=2), AX_X, ALU.add)\
                    .then_inc(lam_arg, 1)
                dve.wait_ge(lam_exp, 1)
                link(tt_(neg_lam, lam_t[:, 67:68], lam_t[:, 66:67], ALU.subtract))
                link(ts(neg_lam, neg_lam, -LAM_INIT, None, ALU.add))
                link(ts(sub_g, par("subln_g"), 1.0 - LAM_INIT, None, ALU.mult))

                def maxima(i):
                    kind, h, t = UNITS[i]
                    for c, p in enumerate(r["scores", i]):
                        ready(dve, p)
                        s = wide(p, NKEY)
                        if kind == "B":
                            b = bias[:, h, 7 - 2 * t:15 - 2 * t, :].rearrange("p a b -> p (a b)")
                            link(tt_(s[:, C:NKEY], s[:, C:NKEY], b, ALU.add))
                        dve.tensor_reduce(neg_max[:, i % 2, c:c + 1], s, AX_X, ALU.max, negate=True).then_inc(max_ready, 1)

                def take_o(i):
                    kind, h, t = UNITS[i]
                    p = r["PV", i]
                    o = DH * (h % 2)
                    ready(dve, p)
                    to = o_a[o:o + DH, h // 2] if kind == "A" else mix[o:o + DH, 2 + h // 2]
                    dve.tensor_copy(to[:, t * P:(t + 1) * P], ps[o:o + DH, p.bank, 0:P]).then_inc(bank_free[p.bank], 1)

                maxima(0)
                for i, (kind, h, t) in enumerate(UNITS):
                    n = 2 if kind == "A" else 1
                    for p in r["scores", i]:
                        read(dve, p)
                    inv = row_inv[:, i % 2]
                    link(dve.reciprocal(inv[:, 0:n], row_sum[:, i % 2, 0:n]))
                    p0, p1 = prob[:, i % 2, 0], prob[:, i % 2, 1]
                    if kind == "A":
                        link(tt_(inv[:, 1:2], inv[:, 1:2], neg_lam, ALU.mult))
                        link(ts(p1, p1, inv[:, 1:2], None, ALU.mult))
                        stt(p0, p0, inv[:, 0:1], p1, ALU.mult, ALU.add).then_inc(prob_ready, 1)
                    else:
                        ts(p0, p0, inv[:, 0:1], None, ALU.mult).then_inc(prob_ready, 1)
                    if i + 1 < len(UNITS):
                        maxima(i + 1)
                    if i >= 1:
                        take_o(i - 1)
                    mod_terms(16 + i, 17 + i)
                take_o(len(UNITS) - 1)
                dve.wait_ge(rstd_ready, ROOTS["subln"])
                for c in range(2):
                    stt(mix[:, c, 0:S], o_a[:, c], sub_g, sub_rs_t[:, c * S:(c + 1) * S], ALU.mult, ALU.mult).then_inc(mixed, 1)

            def first_out():
                p = r["mod2"]
                ready(dve, p)
                tt_(mod2, ps[:, p.bank, 0:32], par("ada_b")[:, 16:48], ALU.add).then_inc(bank_free[p.bank], 1)
                read(dve, p)
                stt(gain2, mod2[:, 16:24], 1.0, par("norm2_g"), ALU.add, ALU.mult).then_inc(mod2_ready, 1)
                dve.wait_ge(mod2_ready, 1)
                for i, p in enumerate(r["w_out"]):
                    ready(dve, p)
                    xi = x[:, i, META:T2]
                    stt(xi, bank(p), mod2[:, i:i + 1], xi, ALU.mult, ALU.add).then_inc(bank_free[p.bank], 1)
                    if i > 0:
                        add_square(sq_a, i - 1, 2 * KT, S)
                add_square(sq_a, KT - 1, 2 * KT, S)

            def router():
                norm(gain2, x[:, :, META:T2], h2, S, rstd[:, 0:S], scaled, "ms_2")
                p = r["router"]
                ready(dve, p)
                shifted, e_, score, sel, gs, oh, tmp, selm, o1, o2 = (rt[j] for j in range(10))
                lg = ps[:, p.bank, 0:64].rearrange("p (t e) -> p t e", t=ST)
                col = [rt[13 + j // 4][:, j % 4, 0:4] for j in range(12)]
                falling = con("falling")
                fall = bcast(falling, 1, ST)
                link(dve.tensor_reduce(col[0], lg, AX_X, ALU.max))
                tt_(shifted, lg, bcast(col[0], 2, EXPERTS), ALU.subtract).then_inc(bank_free[p.bank], 1)
                read(dve, p)
                dve.wait_ge(route_exp, 1)
                link(dve.tensor_reduce(col[1], e_, AX_X, ALU.add))
                link(dve.reciprocal(col[2], col[1]))
                link(tt_(score, e_, bcast(col[2], 2, EXPERTS), ALU.mult))
                link(tt_(sel, score, bcast(par("router_b"), 1, ST), ALU.add))
                s4 = sel.rearrange("p t (g e) -> p t g e", g=4)
                g1, g2 = gs[:, :, 0:4], gs[:, :, 4:8]
                first = True
                for a in range(4):
                    for b in range(a + 1, 4):
                        link(tt_(g1 if first else g2, s4[:, :, :, a], s4[:, :, :, b], ALU.add))
                        if not first:
                            link(tt_(g1, g1, g2, ALU.max))
                        first = False
                link(dve.tensor_reduce(col[3], g1, AX_X, ALU.max))
                link(tt_(g2, g1, bcast(col[3], 2, 4), ALU.is_equal))
                link(tt_(g2, g2, bcast(falling[:, EXPERTS - 4:EXPERTS], 1, ST), ALU.mult))
                link(dve.tensor_reduce(col[4], g2, AX_X, ALU.max))
                link(tt_(g2, g2, bcast(col[4], 2, 4), ALU.is_equal))
                link(dve.tensor_copy(oh.rearrange("p t (g e) -> p t g e", g=4), bcast(g2, 3, 4)))
                link(tt_(selm, sel, oh, ALU.mult))
                link(ts(tmp, oh, 1.0, -NEG, ALU.subtract, ALU.mult))
                link(tt_(selm, selm, tmp, ALU.add))
                for o, c in ((o1, 5), (o2, 7)):
                    link(dve.tensor_reduce(col[c], selm, AX_X, ALU.max))
                    link(tt_(o, selm, bcast(col[c], 2, EXPERTS), ALU.is_equal))
                    link(tt_(o, o, fall, ALU.mult))
                    link(dve.tensor_reduce(col[c + 1], o, AX_X, ALU.max))
                    link(tt_(o, o, bcast(col[c + 1], 2, EXPERTS), ALU.is_equal))
                    if c == 5:
                        link(stt(selm.rearrange("p t e -> p (t e)"), o.rearrange("p t e -> p (t e)"), 2 * NEG,
                                 selm.rearrange("p t e -> p (t e)"), ALU.mult, ALU.add))
                oh2, rank = rt[11], rt[12]
                tt_(oh2, o1, o2, ALU.add).then_inc(chosen, 1)
                for o, c in ((o1, 8), (o2, 9)):
                    link(tt_(tmp, o, score, ALU.mult))
                    link(dve.tensor_reduce(col[c], tmp, AX_X, ALU.add))
                link(tt_(col[10], col[8], col[9], ALU.add))
                link(dve.reciprocal(col[11], col[10]))
                for c in range(2):
                    link(tt_(gate_c[:, c], col[8 + c], col[11], ALU.mult))
                p = r["rank"]
                ready(dve, p)
                count, n_job, end, first = (rt[16][:, j] for j in range(4))
                dve.tensor_copy(count, ps[:, p.bank, 64:64 + EXPERTS])
                dve.tensor_copy(rank, ps[:, p.bank, 0:64].rearrange("p (t e) -> p t e", t=ST)).then_inc(bank_free[p.bank], 1)
                read(dve, p)
                link(ts(n_job, count, 1.0, None, ALU.is_ge))
                for k in range(1, S // P):
                    link(stt(n_job, count, float(k * P + 1), n_job, ALU.is_ge, ALU.add))
                link(dve.tensor_tensor_scan(end, ones[:, 0:EXPERTS], n_job, 0.0, ALU.mult, ALU.add))
                link(tt_(first, end, n_job, ALU.subtract))
                over = piece(arena, 17700, JOBS, EXPERTS)
                link(tt_(over, bcast(end, 1, JOBS), bcast(lane[:, 0:JOBS], 2, EXPERTS), ALU.is_le))
                link(dve.tensor_reduce(job_e, over, AX_X, ALU.add))
                link(ts(job_e, job_e, float(EXPERTS - 1), None, ALU.min))
                link(dve.tensor_copy(job_i, job_e))
                dve.tensor_copy(n_jobs_i, end[:, EXPERTS - 1:EXPERTS]).then_inc(jobs_ready, 1)
                link(ts(first, first, float(P), None, ALU.mult))
                link(tt_(rank, rank, bcast(first, 1, ST), ALU.add))
                for c, o in enumerate((o1, o2)):
                    link(tt_(tmp, o, rank, ALU.mult))
                    link(dve.tensor_reduce(place[:, c], tmp, AX_X, ALU.add))
                flat = place.rearrange("p c t -> p (c t)")
                link(ts(job_of, flat, 1.0 / P, -(P - 1) / (2.0 * P), ALU.mult, ALU.add))
                link(ts(job_of, job_of, ROUND, None, ALU.add))
                link(ts(job_of, job_of, ROUND, None, ALU.subtract))
                link(stt(slot_of, job_of, -float(P), flat, ALU.mult, ALU.add))
                link(tt_(job_hot, bcast(lane[:, 0:JOBS], 1, 2 * ST), bcast(job_of, 2, JOBS), ALU.is_equal))
                link(tt_(job_hot, job_hot, bcast(result_no, 2, JOBS), ALU.mult))
                tt_(slot_hot, bcast(lane, 1, 2 * ST), bcast(slot_of, 2, P), ALU.is_equal).then_inc(places, 1)
                p = r["slots"]
                ready(dve, p)
                dve.tensor_copy(result_f, ps[:, p.bank, 0:JOBS]).then_inc(bank_free[p.bank], 1)
                read(dve, p)
                link(ts(slot_t, result_f, 0.0, None, ALU.is_equal))
                link(ts(slot_t, slot_t, unused_row, -1.0, ALU.mult, ALU.add))
                link(tt_(result_f, result_f, slot_t, ALU.add))
                link(ts(slot_t, result_f, float(S), -float(S), ALU.is_ge, ALU.mult))
                link(tt_(gather_f, result_f, slot_t, ALU.add))
                link(ts(slot_t, result_f, float(2 * S), -float(S), ALU.is_ge, ALU.mult))
                link(tt_(gather_f, gather_f, slot_t, ALU.add))
                link(dve.tensor_copy(gather_i, gather_f))
                dve.tensor_copy(gather_now, gather_i[:, 0:1]).then_inc(gather_set, 1)
                link(dve.tensor_copy(result_i, result_f))
                dve.tensor_copy(result_now, result_i[:, 0:1]).then_inc(result_set, 1)

            def experts():
                dve.wait_ge(jobs_ready, 1)
                n_jobs = dve.value_load(n_jobs_i[0:1, 0:1], min_val=MIN_JOBS, max_val=JOBS - 1)
                hid_flat = hid.rearrange("p k t -> p (k t)")
                with dve.Fori(0, n_jobs) as it:
                    dve.wait_ge(job_read, it * 16 + 16)
                    dve.tensor_copy(gather_now, gather_i[:, bass.ds(it + 1, 1)]).then_inc(gather_set, 1)
                    dve.wait_ge(e_done, it * 5 + 4)
                    dve.wait_ge(silu_out, it + 1)
                    tt_(hid_flat, ps[:, 1, :], silu_t, ALU.mult).then_inc(hid_ready, 1)
                    dve.wait_ge(y_stored, it * 16 + 16)
                    dve.tensor_copy(result_now, result_i[:, bass.ds(it + 1, 1)]).then_inc(result_set, 1)
                for t in range(ST):
                    dve.wait_ge(gathered[t], 32)
                    link(ts(both[:, t], got[:, 0, t], gate_c[:, 0, t:t + 1], None, ALU.mult))
                    stt(both[:, t], got[:, 1, t], gate_c[:, 1, t:t + 1], both[:, t], ALU.mult, ALU.add).then_inc(combined, 1)
                for k, p in enumerate(r["moe_out"]):
                    ready(dve, p)
                    xk = x[:, k, META:T2]
                    stt(xk, bank(p), mod2[:, 24 + k:25 + k], xk, ALU.mult, ALU.add).then_inc(bank_free[p.bank], 1)

            def ab_in():
                norm(par("final_g"), x[:, :, META:T2], x[:, :, META:T2], S, rstd[:, 0:S], x_normed, "ms_f")
                norm(par("norm_ab"), x, h2, T2, rstd[:, 0:T2], h_ready, "ms_ab")

            def lru():
                cw = par("conv_w").rearrange("p (i j) -> p i j", i=4)
                ready(dve, r["ab"][0])
                link(dve.memset(xr[:, :, 0:3], 0.0))
                for i in range(4):
                    read(dve, r["ab"][2 * i])
                    read(dve, r["ab"][2 * i + 1])
                    link(ts(xc[:, i], xr[:, i, 0:T2], cw[:, i, 0:1], par("conv_b")[:, i:i + 1], ALU.mult, ALU.add))
                    for j in (1, 2):
                        link(stt(xc[:, i], xr[:, i, j:j + T2], cw[:, i, j:j + 1], xc[:, i], ALU.mult, ALU.add))
                    stt(xc[:, i], xr[:, i, 3:3 + T2], cw[:, i, 3:4], xc[:, i], ALU.mult, ALU.add).then_inc(xc_ready, 1)
                link(ts(qk_gain[:, 0:1], par("q_norm"), DH ** -0.5, None, ALU.mult))
                link(dve.tensor_copy(qk_gain[:, 1:2], par("k_norm")))
                link(ts(neg_sink, par("sinks"), -1.0, None, ALU.mult))
                lam = par("lam")
                L = [lru_t[:, 4 * j:4 * j + 4] for j in range(9)]
                stt(L[0], lam, -1.0, lam, ALU.mult, ALU.max).then_inc(lru_y, 1)
                dve.wait_ge(lru_e, 1)
                link(ts(L[2], L[1], 2.0, None, ALU.add))
                link(dve.reciprocal(L[3], L[2]))
                link(tt_(L[2], L[1], L[3], ALU.mult))
                link(tt_(L[3], L[2], L[2], ALU.mult))
                link(ts(L[4], L[3], 1.0 / 17, None, ALU.mult))
                for n in (15, 13, 11, 9, 7, 5, 3):
                    link(stt(L[4], L[4], 1.0 / n, L[3], ALU.add, ALU.mult))
                link(stt(L[4], L[4], 1.0, L[2], ALU.add, ALU.mult))
                link(ts(L[5], lam, -1.0, 0.0, ALU.mult, ALU.max))
                link(stt(L[4], L[4], 2.0, L[5], ALU.mult, ALU.add))
                ts(lru_c, L[4], -8.0, None, ALU.mult).then_inc(lru_cr, 1)
                for i in range(5):
                    g = qk_gain[:, 0:1] if i < 4 else qk_gain[:, 1:2]
                    dve.wait_ge(rstd_ready, ROOTS["qk_ms"] - 10 + 2 * i + 2)
                    stt(qk[:, i], qk[:, i], g, qk_rs[:, i], ALU.mult, ALU.mult).then_inc(qk_n, 1)
                for i in range(4):
                    dve.wait_ge(lru_act, 4 + i + 1)
                    link(tt_(g_m[:, i], g_a[:, i], g_a[:, i], ALU.mult))
                    stt(g_m[:, i], g_m[:, i], 1.0, g_r[:, i], ALU.add, ALU.mult).then_inc(lru_m, 1)
                dve.wait_ge(swa_in, 32)
                for i in range(5):
                    dve.wait_ge(qk_n, i + 1)
                    for j, (at, n) in enumerate(HALVES2):
                        p = r["qk_sw"][2 * i + j]
                        ready(dve, p)
                        tt_(rope_t[:, i % 2, at:at + n], bank(p, n), rope_q[:, 1, at:at + n], ALU.mult).then_inc(bank_free[p.bank], 1)
                    read(dve, p)
                    link(tt_(qk[:, i], qk[:, i], rope_q[:, 0], ALU.mult))
                    tt_(qk[:, i], qk[:, i], rope_t[:, i % 2], ALU.add).then_inc(qk_rot, 1)

            def lru_out(i):
                dve.wait_ge(lru_s, i + 1)
                link(dve.memset(g_m[:, i, 0:1], 1.0))
                link(tt_(g_m[:, i], g_m[:, i], g_i[:, i], ALU.mult))
                link(tt_(g_m[:, i], g_m[:, i], xc[:, i], ALU.mult))
                link(dve.tensor_tensor_scan(g_r[:, i], g_a[:, i], g_m[:, i], 0.0, ALU.mult, ALU.add))
                tt_(mix[:, i], g_r[:, i], gate[:, i], ALU.mult).then_inc(mixed, 1)

            def swa():
                def maxima(i):
                    t, a = GROUPS[i]
                    nq, (col, _, n) = swa_queries(t)[1], swa_keys(t)[-1]
                    mc, mw = SWA_MASKS.get(t, (0, col + n))
                    p = r["swa_s", i]
                    ready(dve, p)
                    s = ps[0:nq, 0:4, 0:col + n]
                    link(tt_(s, s, bcast(swa_mask[0:nq, mc:mc + mw], 1, 4), ALU.add))
                    nm = neg_max[0:nq, i % 2]
                    link(dve.tensor_reduce(nm, s, AX_X, ALU.max, negate=True))
                    link(tt_(nm, nm, neg_sink[0:nq, 4 * a:4 * a + 4], ALU.min))
                    tt_(sink_d[0:nq, i % 2], nm, neg_sink[0:nq, 4 * a:4 * a + 4], ALU.subtract).then_inc(swa_max, 1)

                def take_o(i):
                    t, a = GROUPS[i]
                    q0, nq = swa_queries(t)
                    p = r["swa_o", i]
                    ready(dve, p)
                    dve.tensor_copy(mix[:, 4 + 2 * a:6 + 2 * a, q0:q0 + nq],
                                    ps[:, p.bank, 0:2 * P].rearrange("p (j q) -> p j q", j=2)[:, :, 0:nq]).then_inc(bank_free[p.bank], 1)

                maxima(0)
                for i, (t, a) in enumerate(GROUPS):
                    nq, (col, _, n) = swa_queries(t)[1], swa_keys(t)[-1]
                    read(dve, r["swa_s", i])
                    inv = row_inv[0:nq, i % 2]
                    link(tt_(inv, row_sum[0:nq, i % 2], sink_e[0:nq, i % 2], ALU.add))
                    link(dve.reciprocal(inv, inv))
                    pr = prob2[0:nq, i % 2, :, 0:col + n]
                    tt_(pr, pr, bcast(inv, 2, col + n), ALU.mult).then_inc(swa_prob, 1)
                    if i + 1 < len(GROUPS):
                        maxima(i + 1)
                    if i >= 1:
                        take_o(i - 1)
                    if i % 2 == 1 and i < 8:
                        lru_out(i // 2)
                take_o(len(GROUPS) - 1)

            def residual(products, pieces, t0, m, it=None):
                for p, (at, n) in zip(products, pieces):
                    ready(dve, p, it)
                    xm = x[:, m, t0 + at:t0 + at + n]
                    tt_(xm, bank(p, n), xm, ALU.add).then_inc(bank_free[p.bank], 1)

            def ab_out():
                for i in range(8):
                    residual(r["ab_out"][2 * i:2 * i + 2], HALVES2, 0, i)
                    if i > 0:
                        add_square(sq_a, i - 1, 5 * KT, T2)
                add_square(sq_a, KT - 1, 5 * KT, T2)

            def ffn(n):
                t0, pieces = (0, HALVES2) if n == 0 else (META, [(0, S)])
                np_ = len(pieces)
                width = T2 if n == 0 else S
                norm(par("norm_ffn")[:, 8 * n:8 * n + 8], x[:, :, t0:T2], h2, width, rstd[:, 0:width], h_ready,
                     ("ffn_ms", n))

                def products(g, u, tile, i, it=None):
                    for j, (at, w) in enumerate(pieces):
                        ready(dve, u[j], it)
                        read(dve, g[j], it)
                        tt_(act_w[:, tile, at:at + w], bank(u[j], w), silu_w[:, i, at:at + w], ALU.mult)\
                            .then_inc(bank_free[u[j].bank], 1)

                with dve.Fori(0, 3) as it:
                    for i in range(6):
                        a = np_ * 2 * i
                        body = r["ffn_loop", n]
                        products(body[a:a + np_], body[a + np_:a + 2 * np_], it * 6 + i, i, it)
                for i in range(4):
                    a = np_ * 2 * i
                    rest = r["ffn_rest", n]
                    products(rest[a:a + np_], rest[a + np_:a + 2 * np_], 18 + i, i)
                for k in range(KT):
                    m = k % 4
                    residual(r["ffn_down", n][np_ * m:np_ * (m + 1)], pieces, t0, k, k // 4)
                    if n == 0 and k > 0:
                        add_square(mix, k - 1, 6 * KT, T2)
                if n == 0:
                    add_square(mix, KT - 1, 6 * KT, T2)

            def retention():
                norm(par("norm_ret"), x, h2, T2, rstd[:, 0:T2], h_ready, "ms_ret")
                dve.wait_ge(ret_in, 32)
                cos, sin = rope_r[:, 0], rope_r[:, 1]
                with dve.Fori(0, RET_HEADS) as it:
                    me.loop(it, 12)
                    for name, to, pieces, off in (("q", ret_q, [(0, S)], META), ("k", ret_k, HALVES2, 0)):
                        np_ = len(pieces)
                        for j, (at, n) in enumerate(pieces):
                            p1, p2 = r["ret", name][j], r["ret", name][np_ + j]
                            c, s = cos[:, off + at:off + at + n], sin[:, off + at:off + at + n]
                            a, b = rot_t[:, 0, 0:n], rot_t[:, 1, 0:n]
                            lo, hi = to[:, 0, at:at + n], to[:, 1, at:at + n]
                            ready(dve, p2, it)
                            tt_(lo, bank(p1, n), c, ALU.mult)
                            link(tt_(a, bank(p2, n), s, ALU.mult))
                            link(tt_(lo, lo, a, ALU.subtract))
                            tt_(hi, bank(p2, n), c, ALU.mult).then_inc(bank_free[p2.bank], 1)
                            tt_(b, bank(p1, n), s, ALU.mult).then_inc(bank_free[p1.bank], 1)
                            read(dve, p1, it)
                            ins = tt_(hi, hi, b, ALU.add)
                            if name == "k" and j == np_ - 1:
                                ins.then_inc(ret_qk, 1)
                            else:
                                link(ins)
                    for t, p in enumerate(r["ret", "s"]):
                        n = P if t < 4 else META
                        at = max(P * t - META, 0)
                        first = META + at - P * t
                        ready(dve, p, it)
                        tt_(ret_s[0:n, t, at:S], ps[0:n, p.bank, at:S],
                            decay_r[0:n, it, first:first + S - at], ALU.mult).then_inc(bank_free[p.bank], 1)
                    dve.wait_ge(ret_rs, it + 1)
                    for i in range(4):
                        ins = tt_(ret_o[:, i], ret_o[:, i], rstd[:, 0:S], ALU.mult)
                        link(ins)
                    for i in range(4):
                        ins = tt_(ret_y[:, it * 4 + i], ret_o[:, i], ret_g[:, i], ALU.mult)
                    ins.then_inc(ret_yr, 1)
                    me.end(RET_HEADS)

            def ret_out():
                for i in range(8):
                    residual([r["ret_out"][i]], [(0, S)], META, i)
                    if i > 0:
                        add_square(mix, i - 1, 7 * KT, S)
                add_square(mix, KT - 1, 7 * KT, S)

            filters()
            modulation()
            hyena()
            projections()
            attentions()
            first_out()
            router()
            experts()
            ab_in()
            lru()
            swa()
            ab_out()
            ffn(0)
            retention()
            ret_out()
            ffn(1)



def shape_constants():
    import numpy as np
    f = np.float64
    out = {}
    ones = np.ones((P, P))
    head_ones = np.kron(np.eye(2), np.ones((DH, DH)))
    i = np.arange(P)
    swap_a = np.zeros((P, P)); swap_a[i ^ 16, i] = 1
    swap_q = np.zeros((P, P)); rot = i[i % DH < 16]; swap_q[rot ^ 8, rot] = 1
    qc, kc = i[:, None] % GRID, np.arange(GRID)[None, :]
    c0 = np.clip(qc - WIN_C // 2, 0, GRID - WIN_C)
    win = np.where((kc >= c0) & (kc < c0 + WIN_C), 0.0, NEG)
    falling = np.tile(EXPERTS - np.arange(EXPERTS), (P, 1))
    earlier = (i[:, None] < i[None, :]).astype(f)
    out["const"] = np.concatenate([np.eye(P), ones, head_ones, swap_a, swap_q, win, falling, earlier], 1)

    inv = 10000.0 ** (-np.arange(8, dtype=f) / 8)
    t = np.arange(S)
    ang = np.concatenate([(t // GRID)[:, None] * inv, (t % GRID)[:, None] * inv], 1).T
    r = i % 32
    a = ang[r % 16]
    out["rope_a"] = np.stack([np.cos(a), np.where(r < 16, -1, 1)[:, None] * np.sin(a)], 1)
    t = np.arange(T2)
    r = i % DH
    inv = 500000.0 ** (-np.arange(8, dtype=f) / 8)
    a = t[None, :] * inv[r % 8][:, None]
    on = (r < 16)[:, None]
    out["rope_q"] = np.stack([np.where(on, np.cos(a), 1.0), np.where(on, np.where(r < 8, -1, 1)[:, None] * np.sin(a), 0.0)], 1)
    inv = 10000.0 ** (-np.arange(P, dtype=f) / P)
    a = t[None, :] * inv[:, None]
    out["rope_r"] = np.stack([np.cos(a), np.sin(a)], 1)
    g = np.log1p(-np.exp2(-5.0 - np.arange(RET_HEADS, dtype=f)))
    d = np.arange(T2)[None, None, :] - i[:, None, None]
    out["decay_r"] = np.where(d >= 0, np.exp(np.maximum(d, 0) * g[None, :, None]), 0.0) / 16.0

    q = i[:, None]; k = i[None, :]
    prev, causal, seen = np.where(k > q, 0.0, NEG), np.where(k <= q, 0.0, NEG), np.zeros((P, META))
    out["swa_mask"] = np.concatenate([seen, prev, causal, seen, causal, causal[:, :META]], 1)

    n, k = np.arange(S, dtype=f)[:, None], np.arange(S, dtype=f)[None, :]
    w = 2 * np.pi * (k + 0.5) * n / (2 * S)
    tab = np.stack([np.cos(w), np.sin(w)]).reshape(2, ST, P, ST, P)
    out["dft"] = tab.transpose(3, 2, 0, 1, 4).reshape(ST, P, TILE)
    w = 2 * np.pi * (k + 0.5) * (n + 0.5) / (2 * S)
    out["dft_half"] = np.stack([np.cos(w), np.sin(w)]).reshape(2, ST, P, S).transpose(2, 0, 1, 3)
    tn = np.arange(S, dtype=np.float32) / np.float32(S - 1)
    bands = np.linspace(1e-4, 15, 16, dtype=np.float32)
    ang = (np.float32(2.0 * math.pi / S) * np.arange(S, dtype=np.float32)[:, None]) * bands[None, :]
    z = np.concatenate([tn[:, None], np.cos(ang), np.sin(ang)], 1).T
    out["z"] = np.concatenate([z, np.zeros((P - 33, S))], 0)
    deltas = np.abs(np.linspace(math.log(1e-2) / 1.5, math.log(1e-2) / 0.3, 256, dtype=np.float32))
    out["decay_h"] = np.exp(-tn[:, None] * deltas).reshape(ST, P, 256).transpose(1, 0, 2).reshape(P, 1024)
    t = np.arange(S)
    inv = []
    for w in (2, 4, 8, 16):
        inv.append(1.0 / (np.clip(t + w // 2, 0, S) - np.clip(t - w // 2, 0, S)))
    inv = np.repeat(np.stack(inv), DH, 0).reshape(2, P, S).transpose(1, 0, 2)
    out["pool_inv"] = inv
    return {k: np.ascontiguousarray(v, dtype=np.float32) for k, v in out.items()}


def lay_out(x, c, ctx, c_ctx, norm1_g, norm2_g, ada_w, ada_b, w_in, w_out, a_lambda, a_subln_g, b_rpb,
            pool_w, pool_scale, hy_short_w, hy_short_b, hy_f_w1, hy_f_b1, hy_f_w2, hy_f_b2, hy_f_w3,
            hy_f_b3, hy_skip, router_w, router_b, moe_w1, moe_w3, moe_w2, final_g, meta_tokens_2,
            mix_norm_ab_2, ab_w_in_2, lru_conv_w_2, lru_conv_b_2, lru_w_a_2, lru_b_a_2, lru_w_i_2,
            lru_b_i_2, lru_lambda_2, q_norm_2, k_norm_2, attn_sinks_2, ab_w_out_2, mix_norm_ret_2,
            ret_w_in_2, ret_w_out_2, ffn_norm_2, ffn_w_gu_2, ffn_w_down_2):
    import numpy as np
    k = shape_constants()

    def rows(v):
        return np.asarray(v).reshape(-1, P).T

    def every(v):
        v = np.asarray(v).reshape(1, -1)
        return np.repeat(v, P, 0)

    def padded(v):
        v = np.asarray(v)
        v = v.reshape(v.shape[0], -1)
        return np.concatenate([v, np.zeros((P - v.shape[0], v.shape[1]), v.dtype)], 0)

    def tiles(w):
        w = np.asarray(w)
        kk, m = w.shape
        return w.reshape(kk // P, P, m // P, P).transpose(2, 1, 0, 3).reshape(m // P, P, kk)

    def moving(w):
        w = np.asarray(w)
        n = w.shape[1]
        return w.reshape(4, 2, P, n // 512, 512).transpose(3, 0, 2, 1, 4).reshape(n // 512 * 4, P, TILE)

    def down(w):
        w = tiles(w)
        w = np.concatenate([w, np.zeros((KT, P, 24 * P - FF), w.dtype)], 2)
        return w.reshape(KT, P, 3, TILE).transpose(0, 2, 1, 3).reshape(24, P, TILE)

    def alternate(*ws):
        return np.stack(ws, 1).reshape(-1, P, ws[0].shape[-1])

    w_in0, w_out0, ada0 = (np.asarray(w)[0] for w in (w_in, w_out, ada_w))
    ada = ada0.reshape(KT, P, 6, TILE).transpose(2, 0, 1, 3).reshape(6 * KT, P, TILE)
    hy = tiles(w_in0[:, 1792:2560])
    mixers = np.concatenate([tiles(w_in0[:, a:a + 256]) for a in (0, 256, 768, 1024, 1536)])
    values = moving(np.concatenate([w_in0[:, 512:768], w_in0[:, 1280:1536]], 1))
    w1, w3, w2 = (np.asarray(w)[0] for w in (moe_w1, moe_w3, moe_w2))
    moe = []
    for e in range(EXPERTS):
        moe.append(np.concatenate([tiles(w1[e]), tiles(w3[e]), w2[e].reshape(4, P, TILE)]))
    ab = np.asarray(ab_w_in_2)[0]
    q_heads = np.array([4 * kv + j for j in range(4) for kv in range(2)])
    q_cols = (q_heads[:, None] * DH + np.arange(DH)).ravel()
    ab_tiles = np.concatenate([tiles(ab[:, 0:1024]), tiles(ab[:, 1024:1536][:, q_cols]), tiles(ab[:, 1536:1664])])
    ab_v = tiles(ab[:, 1664:1792])
    gates = []
    for i in range(4):
        for w in (lru_w_a_2, lru_w_i_2):
            w = np.asarray(w)[0]
            m = np.zeros((P, P), w.dtype)
            m[:DH, :DH], m[DH:, DH:] = w[2 * i], w[2 * i + 1]
            gates.append(m)
    gates = np.stack(gates, 1).reshape(1, P, TILE)
    ab_o = np.asarray(ab_w_out_2)[0]
    ab_o = tiles(np.concatenate([ab_o[:512], ab_o[512:][q_cols]], 0))
    ffn = []
    for n in range(2):
        gu, dn = np.asarray(ffn_w_gu_2)[n], np.asarray(ffn_w_down_2)[n]
        ffn.append(np.concatenate([alternate(tiles(gu[:, :FF]), tiles(gu[:, FF:])), down(dn)]))
    ret = np.asarray(ret_w_in_2)[0]
    heads = []
    for h in range(RET_HEADS):
        heads += [tiles(ret[:, h * 256:h * 256 + 256]), tiles(ret[:, 1024 + h * 256:1280 + h * 256]),
                  moving(ret[:, 2048 + h * 512:2560 + h * 512]), tiles(ret[:, 4096 + h * 512:4608 + h * 512])]
    ro = np.asarray(ret_w_out_2)[0]
    ro = tiles(ro).reshape(KT, P, 2, TILE).transpose(0, 2, 1, 3).reshape(16, P, TILE)

    parts = {"dft": k["dft"], "mod1": ada[:16], "hyena": hy[[4, 5, 0, 1, 2, 3]], "mixers": mixers, "values": values,
             "mod2": ada[16:], "w_out": tiles(w_out0), "ab": ab_tiles, "ab_values": ab_v,
             "lru_gates": gates, "ab_out": ab_o, "ffn0": ffn[0], "ret": np.concatenate(heads), "ret_out": ro,
             "ffn1": ffn[1]}
    for name, n in STREAM:
        assert parts[name].shape == (n, P, TILE), (name, parts[name].shape)
    weights = np.concatenate([parts[name] for name, _ in STREAM], 0)

    small = {
        "c": np.stack([rows(np.asarray(c)[0]), rows(c_ctx)], 2), "norm1_g": rows(norm1_g), "norm2_g": rows(norm2_g),
        "final_g": rows(final_g), "norm_ab": rows(mix_norm_ab_2), "norm_ret": rows(mix_norm_ret_2),
        "norm_ffn": rows(ffn_norm_2), "ada_b": rows(ada_b), "a_lambda": every(a_lambda),
        "subln_g": np.tile(np.asarray(a_subln_g).reshape(DH, 1), (2, 1)), "pool_scale": rows(pool_scale),
        "short_w": np.asarray(hy_short_w)[0].reshape(3, 6, P).transpose(2, 1, 0), "short_b": rows(hy_short_b),
        "f_b1": padded(np.asarray(hy_f_b1).T), "f_b2": padded(np.asarray(hy_f_b2).T),
        "skip": np.asarray(hy_skip)[0].reshape(2, 2, P).transpose(2, 0, 1),
        "router_w": np.asarray(router_w).reshape(KT, P, EXPERTS).transpose(1, 0, 2), "router_b": every(router_b),
        "conv_w": np.asarray(lru_conv_w_2)[0].reshape(4, 4, P).transpose(2, 1, 0), "conv_b": rows(lru_conv_b_2),
        "b_a": rows(np.asarray(lru_b_a_2).reshape(-1)), "b_i": rows(np.asarray(lru_b_i_2).reshape(-1)),
        "lam": rows(lru_lambda_2), "q_norm": np.tile(np.asarray(q_norm_2).reshape(DH, 1), (2, 1)),
        "k_norm": np.tile(np.asarray(k_norm_2).reshape(DH, 1), (2, 1)),
        "sinks": every(np.asarray(attn_sinks_2)[0][q_heads]),
    }
    small = np.concatenate([small[name].reshape(P, n) for name, n in SMALL], 1)
    w3 = np.concatenate([np.asarray(hy_f_w3)[0], np.asarray(hy_f_b3)], 0)
    filt = np.concatenate([padded(np.asarray(hy_f_w1)[0]), padded(np.asarray(hy_f_w2)[0]), k["z"], padded(w3), k["decay_h"]], 1)

    rpb = np.asarray(b_rpb)[0]
    wide = np.pad(rpb, ((0, 0), (1, 1), (GRID - WIN_C, GRID - WIN_C)))
    qc, kc = np.arange(GRID)[:, None], np.arange(GRID)[None, :]
    picked = wide[:, :, kc - qc + GRID - 1]
    picked = picked.transpose(2, 0, 1, 3)
    bias = np.concatenate([picked[:, :, 1:16], picked[:, :, 0:15]], 0)

    pw = np.asarray(pool_w)[0]
    pool = np.zeros((P, 2, P), pw.dtype)
    for g in range(4):
        o = DH * (g % 2)
        pool[o:o + DH, g // 2, o:o + DH] = pw[g]

    def feature_major(v):
        v = np.asarray(v)
        return v.reshape(-1, KT, P).transpose(2, 1, 0)

    arrays = {
        "weights": weights, "experts": np.stack(moe), "small": small, "const": k["const"], "filter": filt,
        "x": feature_major(np.asarray(x)[0]), "ctx": feature_major(np.asarray(ctx)[0]),
        "meta": feature_major(meta_tokens_2), "bias": bias, "pool_w": pool, "pool_inv": k["pool_inv"],
        "rope_a": k["rope_a"], "rope_q": k["rope_q"], "rope_r": k["rope_r"], "decay_r": k["decay_r"],
        "swa_mask": k["swa_mask"], "dft_half": k["dft_half"],
    }
    return {n: np.ascontiguousarray(a) for n, a in arrays.items()}


def kernel(**inputs):
    import concourse.bacc as _bacc
    from concourse import mybir as _mybir
    from concourse.bass_utils import run_bass_kernel_spmd as _run

    nc = _bacc.Bacc("TRN2", target_bir_lowering=False, num_devices=1)
    arrays = lay_out(**inputs)
    args = {n: nc.dram_tensor(f"in_{n}", a.shape, _mybir.dt.from_np(a.dtype), kind="ExternalInput").ap()
            for n, a in arrays.items()}
    args["out"] = nc.dram_tensor("out", (P, KT, S), F32, kind="ExternalOutput").ap()
    two_blocks(nc, args)
    r = _run(nc, [{f"in_{n}": a for n, a in arrays.items()}], core_ids=[0])
    got = r.results[0]["out"]
    return got.transpose(2, 1, 0).reshape(1, S, D)
```
